# Optimizing a Trainium2 kernel written in Bass

```python
import jax, jax.numpy as jnp
from jax import lax
import numpy as np

D_MODEL = 1024
BATCH = 1
SEQ = 2048
DEPTH = 1

HEAD_DIM = 64
W_A = D_MODEL // 4
W_B = D_MODEL // 2
W_C = D_MODEL // 4
NH_A = W_A // HEAD_DIM
NH_B = W_B // HEAD_DIM
NG_C = 4
G_C = W_C // NG_C
N_HEADS_TOTAL = NH_A + NH_B + W_C // HEAD_DIM
MIX_WIDTH = W_A + W_B + W_C
IN_COLS = 2 * W_A + 3 * W_B + W_C
CHUNK = 128
SB_BLOCK = 128
POOL_WINDOWS = (2, 4, 8, 16)
D_FF = ((8 * D_MODEL // 3) + 127) // 128 * 128
CONV_WIDTH = 3
EPS = 1e-6

kernel_name = "hybrid_sgu_stickbreak_pool_convffn"

def rmsnorm(x, g):
    xf = x.astype(jnp.float32)
    y = xf * lax.rsqrt(jnp.mean(xf * xf, axis=-1, keepdims=True) + EPS)
    return (y * g.astype(jnp.float32)).astype(x.dtype)

def chunked_sgu(a, sgu_norm_g, sgu_w, sgu_b):
    B, S, _ = a.shape
    u, v = jnp.split(jax.nn.gelu(a, approximate=False), 2, axis=-1)
    v = rmsnorm(v.reshape(B, S, NH_A, HEAD_DIM), sgu_norm_g.reshape(NH_A, HEAD_DIM))
    v = v.reshape(B, S // CHUNK, CHUNK, NH_A, HEAD_DIM)
    tril = jnp.tril(jnp.ones((CHUNK, CHUNK), dtype=bool))
    wm = jnp.where(tril[None], sgu_w, jnp.zeros_like(sgu_w)).astype(v.dtype)
    s = jnp.einsum('hts,bcshd->bcthd', wm, v)
    s = s + jnp.transpose(sgu_b)[None, None, :, :, None].astype(v.dtype)
    return u * s.reshape(B, S, W_A)

def _stick_breaking_block(qb, k, v, q_start):
    T = qb.shape[2]
    S = k.shape[2]
    z = jnp.einsum('bhtd,bhsd->bhts', qb, k).astype(jnp.float32) * (HEAD_DIM ** -0.5)
    t_idx = q_start + jnp.arange(T, dtype=jnp.int32)
    s_idx = jnp.arange(S, dtype=jnp.int32)
    mask = (s_idx[None, :] < t_idx[:, None])[None, None]
    log_1m = jnp.where(mask, jax.nn.log_sigmoid(-z), 0.0)
    tail = lax.cumsum(log_1m, axis=3, reverse=True) - log_1m
    log_a = jax.nn.log_sigmoid(z) + tail
    att = jnp.where(mask, jnp.exp(log_a), 0.0)
    out = jnp.einsum('bhts,bhsd->bhtd', att, v.astype(jnp.float32))
    return out.astype(qb.dtype)

def stick_breaking_attention(q, k, v):
    B, S, H, d = q.shape
    nb = S // SB_BLOCK
    qt = jnp.transpose(q, (0, 2, 1, 3)).reshape(B, H, nb, SB_BLOCK, d)
    qt = jnp.transpose(qt, (2, 0, 1, 3, 4))
    kt = jnp.transpose(k, (0, 2, 1, 3))
    vt = jnp.transpose(v, (0, 2, 1, 3))
    starts = jnp.arange(nb, dtype=jnp.int32) * SB_BLOCK
    out = lax.map(lambda args: _stick_breaking_block(args[0], kt, vt, args[1]), (qt, starts))
    out = jnp.transpose(out, (1, 0, 3, 2, 4))
    return out.reshape(B, S, H * d)

def causal_pool_mixer(p, pool_w, pool_scale):
    B, S, _ = p.shape
    pf = p.astype(jnp.float32)
    csum = jnp.cumsum(pf, axis=1)
    pos = jnp.arange(1, S + 1, dtype=jnp.float32)
    outs = []
    for g, w in enumerate(POOL_WINDOWS):
        c = csum[..., g * G_C:(g + 1) * G_C]
        shifted = jnp.pad(c, ((0, 0), (w, 0), (0, 0)))[:, :S]
        cnt = jnp.minimum(pos, float(w))[None, :, None]
        d = (c - shifted) / cnt - pf[..., g * G_C:(g + 1) * G_C]
        outs.append(jnp.einsum('bsc,cd->bsd', d, pool_w[g].astype(jnp.float32)))
    y = jnp.concatenate(outs, axis=-1) * pool_scale.astype(jnp.float32)
    return y.astype(p.dtype)

def conv_gated_ffn(h, w_up, conv_w, conv_b, w_down):
    S = h.shape[1]
    z = h @ w_up
    zp = jnp.pad(z, ((0, 0), (CONV_WIDTH - 1, 0), (0, 0)))
    zc = conv_b
    for k in range(CONV_WIDTH):
        zc = zc + zp[:, k:k + S] * conv_w[k]
    g, u = jnp.split(zc, 2, axis=-1)
    return (jax.nn.silu(g) * u) @ w_down

def setup_inputs(seed: int = 0) -> dict:
    key = jax.random.key(seed)
    ks = jax.random.split(key, 16)
    f32 = jnp.float32

    def nrm(k, shape, scale):
        return jax.random.normal(k, shape, f32) * scale

    return {
        "x": nrm(ks[0], (BATCH, SEQ, D_MODEL), 1.0),
        "norm1_g": 1.0 + nrm(ks[1], (DEPTH, D_MODEL), 0.05),
        "w_in": nrm(ks[2], (DEPTH, D_MODEL, IN_COLS), D_MODEL ** -0.5),
        "sgu_norm_g": 1.0 + nrm(ks[3], (DEPTH, W_A), 0.05),
        "sgu_w": nrm(ks[4], (DEPTH, NH_A, CHUNK, CHUNK), 0.05),
        "sgu_b": 1.0 + nrm(ks[5], (DEPTH, NH_A, CHUNK), 0.05),
        "pool_w": nrm(ks[6], (DEPTH, NG_C, G_C, G_C), G_C ** -0.5),
        "pool_scale": 1.0 + nrm(ks[7], (DEPTH, W_C), 0.05),
        "mix_norm_g": 1.0 + nrm(ks[8], (DEPTH, MIX_WIDTH), 0.05),
        "w_o": nrm(ks[9], (DEPTH, MIX_WIDTH, D_MODEL), MIX_WIDTH ** -0.5),
        "norm2_g": 1.0 + nrm(ks[10], (DEPTH, D_MODEL), 0.05),
        "w_up": nrm(ks[11], (DEPTH, D_MODEL, 2 * D_FF), D_MODEL ** -0.5),
        "conv_w": nrm(ks[12], (DEPTH, CONV_WIDTH, 2 * D_FF), CONV_WIDTH ** -0.5),
        "conv_b": nrm(ks[13], (DEPTH, 2 * D_FF), 0.01),
        "w_down": nrm(ks[14], (DEPTH, D_FF, D_MODEL), D_FF ** -0.5),
        "final_g": 1.0 + nrm(ks[15], (D_MODEL,), 0.05),
    }

def reference(x, norm1_g, w_in, sgu_norm_g, sgu_w, sgu_b, pool_w, pool_scale,
              mix_norm_g, w_o, norm2_g, w_up, conv_w, conv_b, w_down, final_g):
    B, S, D = x.shape
    for l in range(DEPTH):
        h = rmsnorm(x, norm1_g[l])
        proj = h @ w_in[l]
        a_in = proj[..., :2 * W_A]
        qkv = proj[..., 2 * W_A:2 * W_A + 3 * W_B]
        p_in = proj[..., 2 * W_A + 3 * W_B:]
        q, k, v = jnp.split(qkv.reshape(B, S, 3, NH_B, HEAD_DIM), 3, axis=2)
        y_a = chunked_sgu(a_in, sgu_norm_g[l], sgu_w[l], sgu_b[l])
        y_b = stick_breaking_attention(q[:, :, 0], k[:, :, 0], v[:, :, 0])
        y_c = causal_pool_mixer(p_in, pool_w[l], pool_scale[l])
        y = jnp.concatenate([y_a, y_b, y_c], axis=-1).reshape(B, S, N_HEADS_TOTAL, HEAD_DIM)
        y = rmsnorm(y, mix_norm_g[l].reshape(N_HEADS_TOTAL, HEAD_DIM)).reshape(B, S, MIX_WIDTH)
        x = x + y @ w_o[l]
        h = rmsnorm(x, norm2_g[l])
        x = x + conv_gated_ffn(h, w_up[l], conv_w[l], conv_b[l], w_down[l])
    return rmsnorm(x, final_g)


_drawn_inputs = setup_inputs


def setup_inputs(seed=0):
    import zlib

    import numpy as np

    out = dict(_drawn_inputs(seed))
    spreads = {}
    factors = {'sgu_norm_g': 8.0, 'sgu_b': 7.794, 'pool_scale': 3.039, 'conv_b': 8.0}
    for name, (base, spread) in spreads.items():
        noise = np.random.default_rng([zlib.crc32(name.encode()), seed]).standard_normal(out[name].shape)
        drawn = base * np.exp(spread * noise) if base else spread * noise
        out[name] = __import__('jax').numpy.asarray(drawn.astype(out[name].dtype))
    for name, factor in factors.items():
        out[name] = (out[name] * factor).astype(out[name].dtype)
    return out
```

```python
from contextlib import ExitStack

import concourse.bass as bass
from concourse import mybir

F32 = mybir.dt.float32
F32R = mybir.dt.float32r
ACT = mybir.ActivationFunctionType
ALU = mybir.AluOpType
AX_X = mybir.AxisListType.X

P = 128
S, D = 2048, 1024
KD = D // P
HD, NHB = 64, 8
NHT = 16
NB = S // P
TW = 512
NT = S // TW
BPT = TW // P
DFF = 2816
NF = DFF // P
EPS = 1e-6
BIG = 1e30
QSCALE = HD ** -0.5

CHUNK_ORDER = [4, 8, 5, 9, 0, 6, 10, 1, 7, 11, 2, 3, 12, 13]


def attention_slots():
    return [(T, c, i, (i + 1) * P if c == T else TW) for T in range(NT) for c in range(T, -1, -1) for i in range(BPT)]


def split_products(pe, out, parts, first=True, last=True):
    n = len(parts)
    for i, (sh, sl, mh, ml) in enumerate(parts):
        pe.matmul(out, sh, mh, start=first and i == 0, stop=False)
        pe.matmul(out, sh, ml, start=False, stop=False)
        mm = pe.matmul(out, sl, mh, start=False, stop=last and i == n - 1)
    return mm


def project_norm(nc, io, mem):
    hT_hi, hT_lo, ident = mem["hT_hi"], mem["hT_lo"], mem["ident"]
    q_chunk, k_chunk = 0, 1
    with ExitStack() as ctx:
        def sb(name, shape, dt=F32):
            return ctx.enter_context(nc.sbuf_tensor("pn_" + name, shape, dt))

        def sem(name):
            return ctx.enter_context(nc.semaphore("pn_" + name))

        x_in = sb("x_in", [P, 2, D])
        xn = sb("xn", [P, 2, D])
        gain = sb("gain", [P, D])
        sumsq = sb("sumsq", [P, NB])
        meansq = sb("meansq", [P, NB])
        minus_half = sb("minus_half", [P, NB])
        rstd = sb("rstd", [P, NB])
        wv_raw = sb("wv_raw", [P, 2, 512])
        wv_hi = sb("wv_hi", [P, KD, 512], F32R)
        wv_lo = sb("wv_lo", [P, KD, 512], F32R)
        wc_raw = sb("wc_raw", [P, KD, P])
        wc_hi = sb("wc_hi", [P, KD, P], F32R)
        wc_lo = sb("wc_lo", [P, KD, P], F32R)
        chunk_hi, chunk_lo = ([own[:], old[:, 0:2].rearrange("p a (b c) -> p (a b) c", c=P)]
                              for own, old in ((wc_hi, wv_hi), (wc_lo, wv_lo)))
        staged = sb("staged", [P, 2, 2 * TW])
        v_out = [staged[:, n].rearrange("s (h a e) -> s h a e", h=NHB, a=2) for n in range(2)]
        qk_out = [staged[:, n].rearrange("c (a t) -> c a t", a=2) for n in range(2)]
        turned = [ctx.enter_context(nc.psum_tensor(f"pn_turned{i}", [P, TW], F32)) for i in range(4)]
        prod = [ctx.enter_context(nc.psum_tensor(f"pn_prod{i}", [P, TW], F32)) for i in range(2)]

        x_loaded = [sem("x_loaded0"), sem("x_loaded1")]
        gain_loaded = sem("gain_loaded")
        wv_loaded = [sem("wv_loaded0"), sem("wv_loaded1")]
        wc_loaded = sem("wc_loaded")
        wv_high, wv_split, wc_high, wc_split = sem("wv_high"), sem("wv_split"), sem("wc_high"), sem("wc_split")
        ident_zero, ident_ready = sem("ident_zero"), sem("ident_ready")
        sumsq_done, meansq_done, rstd_done = sem("sumsq_done"), sem("meansq_done"), sem("rstd_done")
        xn_done = sem("xn_done")
        turned_done, turned_high, turned_split = sem("turned_done"), sem("turned_high"), sem("turned_split")
        prod_done, prod_high, prod_split = sem("prod_done"), sem("prod_high"), sem("prod_split")
        stored = [sem("stored0"), sem("stored1")]
        NQK = 2 * NT

        block = ctx.enter_context(nc.Block())

        @block.sync
        def _(sp):
            sp.dma_start(gain[:], io["norm1_g"].to_broadcast([P, D])).then_inc(gain_loaded, 16)
            for b in range(2):
                sp.dma_start(x_in[:, b], io["x"][b * P:(b + 1) * P, :]).then_inc(x_loaded[b], 16)
            def load_x(b):
                sp.wait_ge(xn_done, b - 1)
                sp.dma_start(x_in[:, b % 2], io["x"][b * P:(b + 1) * P, :]).then_inc(x_loaded[b % 2], 16)

            for k in range(KD):
                if k >= 2:
                    sp.wait_ge(wv_split, k - 1)
                sp.dma_start(wv_raw[:, k % 2], io["w_v"][k]).then_inc(wv_loaded[k % 2], 16)
                if k == 1:
                    load_x(2)
                if k == 3:
                    load_x(3)
            sp.dma_start(wc_raw[:], io["w_chunks"][q_chunk]).then_inc(wc_loaded, 16)
            for b in range(NB):
                if b + 4 < NB:
                    load_x(b + 4)
                sp.wait_ge(prod_split, b + 1)
                sp.dma_start(io["v_hbm"][:, b // BPT, :, b % BPT, :].rearrange("h s e -> s h e"),
                             staged[:, b % 2].rearrange("s (h a) -> s h a", h=NHB)).then_inc(stored[b % 2], 16)
                if b == 1:
                    sp.wait_ge(wc_split, 1)
                    sp.dma_start(wc_raw[:], io["w_chunks"][k_chunk]).then_inc(wc_loaded, 16)
            for n in range(NQK):
                dst = io["q_hbm"] if n < NT else io["k_hbm"]
                cols = slice(n % NT * TW, (n % NT + 1) * TW)
                sp.wait_ge(prod_split, NB + n + 1)
                sp.dma_start(dst[:, 0:P, cols].rearrange("a c t -> c a t"),
                             staged[:, n % 2].rearrange("c (a t) -> c a t", a=2)).then_inc(stored[n % 2], 16)
            for slot in range(2):
                sp.wait_ge(stored[slot], 16 * (NB + NQK) // 2)

        @block.gpsimd
        def _(pool):
            pool.memset(ident[:], 0.0).then_inc(ident_zero, 1)
            pool.wait_ge(ident_zero, 1)
            pool.affine_select(out=ident[:], in_=ident[:], compare_op=ALU.not_equal, fill=1.0, base=0,
                               pattern=[[-1, P]], channel_multiplier=1).then_inc(ident_ready, 1)
            pool.memset(minus_half[:], -0.5).then_inc(ident_ready, 1)
            pool.wait_ge(ident_ready, 2)

            def inverse_root(b):
                pool.wait_ge(meansq_done, b + 1)
                pool.tensor_tensor(rstd[:, b:b + 1], meansq[:, b:b + 1], minus_half[:, b:b + 1], ALU.pow).then_inc(rstd_done, 1)

            for k in range(KD):
                if k in (1, 3, 5):
                    inverse_root(k // 2)
                pool.wait_ge(wv_loaded[k % 2], 16 * (k // 2 + 1))
                pool.tensor_copy(wv_hi[:, k], wv_raw[:, k % 2]).then_inc(wv_high, 1)
                pool.wait_ge(wv_high, k + 1)
                pool.tensor_tensor(wv_lo[:, k], wv_raw[:, k % 2], wv_hi[:, k].bitcast(F32), ALU.subtract).then_inc(wv_split, 1)
            def split_chunk(n):
                pool.wait_ge(wc_loaded, 16 * (n + 1))
                pool.tensor_copy(chunk_hi[n], wc_raw[:]).then_inc(wc_high, 1)
                pool.wait_ge(wc_high, n + 1)
                pool.tensor_tensor(chunk_lo[n], wc_raw[:], chunk_hi[n].bitcast(F32), ALU.subtract).then_inc(wc_split, 1)

            for b in range(3, NB):
                inverse_root(b)
                if b == 5:
                    split_chunk(0)
            pool.wait_ge(prod_done, NB)
            split_chunk(1)

        @block.scalar
        def _(act):
            for b in range(NB + 2):
                if b < NB:
                    act.wait_ge(x_loaded[b % 2], 16 * (b // 2 + 1))
                    if b >= 2:
                        act.wait_ge(turned_done, 2 * (b - 1))
                    act.activation(xn[:, b % 2], x_in[:, b % 2], ACT.Square, accum_out=sumsq[:, b:b + 1]).then_inc(sumsq_done, 1)
                if 1 <= b <= NB:
                    for n in (2 * (b - 1), 2 * (b - 1) + 1):
                        act.wait_ge(turned_done, n + 1)
                        dst = hT_hi[:, 4 * (n % 2):4 * (n % 2) + 4, (b - 1) * P:b * P]
                        act.activation(dst, turned[n % 4][:].rearrange("p (k t) -> p k t", k=4), ACT.Copy).then_inc(turned_high, 1)
                if b >= 2:
                    n = b - 2
                    act.wait_ge(prod_done, n + 1)
                    if n >= 2:
                        act.wait_ge(stored[n % 2], 16 * (n // 2))
                    act.activation(v_out[n % 2][:, :, 0, :].bitcast(F32R), prod[n % 2][:].rearrange("p (h e) -> p h e", h=NHB),
                                   ACT.Copy).then_inc(prod_high, 1)
            for n in range(NQK):
                act.wait_ge(prod_done, NB + n + 1)
                act.wait_ge(stored[n % 2], 16 * ((NB + n) // 2))
                act.activation(qk_out[n % 2][:, 0].bitcast(F32R), prod[n % 2][:], ACT.Copy,
                               scale=QSCALE if n < NT else 1.0).then_inc(prod_high, 1)

        @block.vector
        def _(dve):
            dve.wait_ge(gain_loaded, 16)
            for b in range(NB + 2):
                if b < NB:
                    dve.wait_ge(sumsq_done, b + 1)
                    dve.tensor_scalar(meansq[:, b:b + 1], sumsq[:, b:b + 1], 1.0 / D, EPS, ALU.mult, ALU.add).then_inc(meansq_done, 1)
                    dve.wait_ge(rstd_done, b + 1)
                    dve.scalar_tensor_tensor(out=xn[:, b % 2], in0=x_in[:, b % 2], scalar=rstd[:, b:b + 1], in1=gain[:],
                                             op0=ALU.mult, op1=ALU.mult).then_inc(xn_done, 1)
                if 1 <= b <= NB:
                    for n in (2 * (b - 1), 2 * (b - 1) + 1):
                        dve.wait_ge(turned_high, n + 1)
                        ks = slice(4 * (n % 2), 4 * (n % 2) + 4)
                        dve.tensor_tensor(hT_lo[:, ks, (b - 1) * P:b * P], turned[n % 4][:].rearrange("p (k t) -> p k t", k=4),
                                          hT_hi[:, ks, (b - 1) * P:b * P].bitcast(F32), ALU.subtract).then_inc(turned_split, 1)
                if b >= 2:
                    n = b - 2
                    dve.wait_ge(prod_high, n + 1)
                    dve.tensor_tensor(v_out[n % 2][:, :, 1, :].bitcast(F32R), prod[n % 2][:].rearrange("p (h e) -> p h e", h=NHB),
                                      v_out[n % 2][:, :, 0, :], ALU.subtract).then_inc(prod_split, 1)
            for n in range(NQK):
                dve.wait_ge(prod_high, NB + n + 1)
                dve.scalar_tensor_tensor(out=qk_out[n % 2][:, 1].bitcast(F32R), in0=prod[n % 2][:], scalar=QSCALE if n < NT else 1.0,
                                         in1=qk_out[n % 2][:, 0], op0=ALU.mult, op1=ALU.subtract).then_inc(prod_split, 1)

        @block.tensor
        def _(pe):
            pe.wait_ge(ident_ready, 1)

            def turn(b):
                pe.wait_ge(xn_done, b + 1)
                for n in (2 * b, 2 * b + 1):
                    if n >= 4:
                        pe.wait_ge(turned_split, n - 3)
                    for j in range(4):
                        k = 4 * (n % 2) + j
                        mm = pe.transpose(turned[n % 4][:, j * P:(j + 1) * P], xn[:, b % 2, k * P:(k + 1) * P], ident[:])
                    mm.then_inc(turned_done, 1)

            turn(0)
            turn(1)
            for b in range(NB):
                if b == 0:
                    pe.wait_ge(wv_split, KD)
                pe.wait_ge(turned_split, 2 * b + 2)
                if b >= 2:
                    pe.wait_ge(prod_split, b - 1)
                ts = slice(b * P, (b + 1) * P)
                split_products(pe, prod[b % 2][:], [(hT_hi[:, k, ts], hT_lo[:, k, ts], wv_hi[:, k], wv_lo[:, k])
                                                    for k in range(KD)]).then_inc(prod_done, 1)
                if b + 2 < NB:
                    turn(b + 2)
            for n in range(NQK):
                T = n % NT
                pe.wait_ge(wc_split, n // NT + 1)
                pe.wait_ge(prod_split, NB + n - 1)
                ts = slice(T * TW, (T + 1) * TW)
                split_products(pe, prod[n % 2][:], [(chunk_hi[n // NT][:, k], chunk_lo[n // NT][:, k], hT_hi[:, k, ts],
                                                     hT_lo[:, k, ts]) for k in range(KD)]).then_inc(prod_done, 1)


def attend(nc, io, mem):
    hT_hi, hT_lo, ident = mem["hT_hi"], mem["hT_lo"], mem["ident"]
    HEAD = attention_slots()
    PER_HEAD, PER_PAIR = len(HEAD), 2 * len(HEAD)
    GROUPS = PER_HEAD // BPT
    TURN_LAG, AV_LAG, OUT_LAG = 5, 7, 8
    NFILL = 12
    FILL_START = [2 + f * (PER_PAIR - 2) // NFILL for f in range(NFILL)]
    FILL_STEPS = 6
    MM_PER_STEP = 3 * KD // FILL_STEPS
    SPLIT_HIGH, SPLIT_LOW, SPLIT_AFTER = [10, 37, 79], [12, 39, 79], [-4, 4, 12]
    CHUNK_SLOT = [0, 1, 0]
    LOAD_RAW = [1, 4, 11]

    def is_diag(s):
        T, c, _, _ = HEAD[s % PER_HEAD]
        return c == T

    def ends_tile(s):
        _, c, i, _ = HEAD[s % PER_HEAD]
        return c == 0 and i == BPT - 1

    def tile_number(s):
        return sum(ends_tile(r) for r in range(s))

    with ExitStack() as ctx:
        def sb(name, shape, dt=F32):
            return ctx.enter_context(nc.sbuf_tensor("at_" + name, shape, dt))

        def sem(name):
            return ctx.enter_context(nc.semaphore("at_" + name))

        def bank(name):
            return ctx.enter_context(nc.psum_tensor("at_" + name, [P, TW], F32))

        keep = sb("keep", [P, BPT, TW + 1])
        weight = sb("weight", [P, 2 * BPT, TW])
        product = sb("product", [P, 2, TW + 1])
        att_hi = sb("att_hi", [P, 2, TW], F32R)
        att_lo = sb("att_lo", [P, 2, TW], F32R)
        q_t = sb("q_t", [P, 2, 2, TW], F32R)
        k_t = sb("k_t", [P, 2, TW], F32R)
        v_t = sb("v_t", [P, 2, BPT, 2 * HD], F32R)
        y_out = sb("y_out", [P, TW])
        w_raw = sb("w_raw", [P, KD, P])
        w_hi = sb("w_hi", [P, 2, KD, P], F32R)
        w_lo = sb("w_lo", [P, 2, KD, P], F32R)
        staged = sb("staged", [P, 2, TW])
        ident_r = sb("ident_r", [P, P], F32R)
        mask_r = sb("mask_r", [P, P], F32R)
        z = [bank(f"z{i}") for i in range(BPT)]
        turned = [bank(f"turned{i}") for i in range(2)]
        y_acc, filled = bank("y_acc"), bank("filled")

        q_loaded, k_loaded, v_loaded = ([sem(f"{n}_loaded{i}") for i in range(2)] for n in "qkv")
        mask_zero, mask_set, mask_ready = sem("mask_zero"), sem("mask_set"), sem("mask_ready")
        scores_done, keep_done, gate_done = sem("scores_done"), sem("keep_done"), sem("gate_done")
        scan_done, weight_done, carry_done = sem("scan_done"), sem("weight_done"), sem("carry_done")
        turned_done, turned_high, turned_split = sem("turned_done"), sem("turned_high"), sem("turned_split")
        av_done, y_copied, y_stored = sem("av_done"), sem("y_copied"), sem("y_stored")
        w_loaded, w_high, w_split = sem("w_loaded"), sem("w_high"), sem("w_split")
        fill_done, fill_high, fill_split, fill_stored = sem("fill_done"), sem("fill_high"), sem("fill_split"), sem("fill_stored")

        def pairs(engine, body):
            body(0)
            with engine.Fori(1, 3) as p:
                body(p)
            body(3)

        def has(p, s):
            return s < PER_PAIR and not (isinstance(p, int) and p == 0 and s < 0)

        def last(p):
            return isinstance(p, int) and p == 3

        block = ctx.enter_context(nc.Block())

        @block.sync
        def _(sp):
            def load_q(p, e, T):
                slot = T % 2
                for a in (1, 0):
                    for half in range(2):
                        sp.dma_start(q_t[half * HD:(half + 1) * HD, slot, a].bitcast(F32),
                                     io["q_hbm"][a, bass.ds(p * P + e * HD, HD), T * TW:(T + 1) * TW]).then_inc(q_loaded[slot], 16)

            def load_k(p, g):
                T, c, _, _ = HEAD[BPT * g % PER_HEAD]
                e = g // GROUPS
                for half in (1, 0):
                    sp.dma_start(k_t[half * HD:(half + 1) * HD, g % 2].bitcast(F32),
                                 io["k_hbm"][half, bass.ds(p * P + e * HD, HD), c * TW:(c + 1) * TW]).then_inc(k_loaded[g % 2], 16)

            def load_v(p, g):
                T, c, _, _ = HEAD[BPT * g % PER_HEAD]
                sp.dma_start(v_t[:, g % 2].bitcast(F32).rearrange("s j e -> s (j e)"),
                             io["v_hbm"][bass.ds(2 * p + g // GROUPS, 1), c].rearrange("h s j e -> s (h j e)")).then_inc(v_loaded[g % 2], 16)

            def store_y(p, s):
                e, T = s % PER_PAIR // PER_HEAD, HEAD[s % PER_HEAD][0]
                head = 2 * p + e if s >= 0 else 2 * p - 1
                sp.wait_ge(y_copied, p * 8 + tile_number(s) + 1 if s >= 0 else p * 8)
                sp.dma_start(io["o_hbm"][bass.ds(head, 1), :, T * TW:(T + 1) * TW].rearrange("h e t -> (h e) t"), y_out[:]).then_inc(y_stored, 16)

            def store_fill(p, f):
                sp.wait_ge(fill_split, p * NFILL + f + 1)
                cols = slice(f % NT * TW, (f % NT + 1) * TW)
                if last(p) or f // NT == 2:
                    row = p + (f // NT if last(p) else 0)
                    sp.dma_start(io["ap_hbm"][bass.ds(row, 1), :, cols].rearrange("n c t -> (n c) t"), staged[:, 0]).then_inc(fill_stored, 16)
                else:
                    dst = io["q_hbm"] if f // NT == 0 else io["k_hbm"]
                    sp.dma_start(dst[:, bass.ds(p * P + P, P), cols].rearrange("a c t -> c a t"), staged[:]).then_inc(fill_stored, 16)

            def pair(p):
                for g in range(2 * GROUPS):
                    s = BPT * g
                    T = HEAD[s % PER_HEAD][0]
                    if is_diag(s) and not (last(p) and s // PER_HEAD == 1 and T == NT - 1):
                        e, T1 = (s // PER_HEAD, T + 1) if T < NT - 1 else (s // PER_HEAD + 1, 0)
                        if has(p, s - 1):
                            sp.wait_ge(scores_done, p * PER_PAIR + s)
                        if e == 2:
                            sp.wait_ge(fill_stored, p * (NFILL * 16) + 8 * 16)
                        load_q(p, e, T1)
                    if not (last(p) and g == 2 * GROUPS - 1):
                        if not (isinstance(p, int) and p == 0 and g == 0):
                            sp.wait_ge(scores_done, p * PER_PAIR + s)
                        load_k(p, g + 1)
                    if not (isinstance(p, int) and p == 0 and g < 2):
                        sp.wait_ge(av_done, p * PER_PAIR + s - BPT)
                    if not (isinstance(p, int) and p == 0 and g == 0):
                        load_v(p, g)
                    for w in range(3):
                        if g == LOAD_RAW[w] and not (last(p) and w == 2):
                            sp.wait_ge(w_split, p * 3 + w + 1)
                            sp.dma_start(w_raw[:], io["w_chunks"][bass.ds(p * 3 + w + 3, 1)].rearrange("n c k m -> c (n k) m")).then_inc(w_loaded, 16)
                    for f in range(NFILL):
                        if g == min(-(-(FILL_START[f] + 8) // BPT), 2 * GROUPS - 1):
                            store_fill(p, f)
                    for r in range(-BPT, PER_PAIR):
                        if ends_tile(r % PER_PAIR) and -(-(r + OUT_LAG + 1) // BPT) == g and has(p, r):
                            store_y(p, r)

            load_q(0, 0, 0)
            load_k(0, 0)
            load_v(0, 0)
            sp.dma_start(w_raw[:], io["w_chunks"][2]).then_inc(w_loaded, 16)
            pairs(sp, pair)
            store_y(3, PER_PAIR - 1)
            sp.wait_ge(y_stored, 16 * NHB * NT)
            sp.wait_ge(fill_stored, 16 * 4 * NFILL)

        @block.gpsimd
        def _(pool):
            pool.memset(y_out[:, 0:P], 0.0).then_inc(mask_zero, 1)
            pool.wait_ge(mask_zero, 1)
            pool.affine_select(out=y_out[:, 0:P], in_=y_out[:, 0:P], compare_op=ALU.is_gt, fill=-BIG, base=0,
                               pattern=[[-1, P]], channel_multiplier=1).then_inc(mask_set, 1)

            def pair(p):
                for s in range(PER_PAIR):
                    _, _, i, w = HEAD[s % PER_HEAD]
                    at = p * PER_PAIR + s
                    pool.wait_ge(scan_done, at + 1)
                    pool.wait_ge(gate_done, at + 1)
                    gate = weight[:, s % (2 * BPT), 0:w]
                    pool.tensor_tensor(gate, product[:, s % 2, 1:w + 1], gate, ALU.mult).then_inc(weight_done, 1)
                    pool.tensor_copy(keep[:, i, TW:TW + 1], product[:, s % 2, 0:1]).then_inc(carry_done, 1)

            pairs(pool, pair)

        @block.scalar
        def _(act):
            def pair(p):
                for s in range(PER_PAIR + (TURN_LAG if last(p) else 0)):
                    if s < PER_PAIR:
                        _, _, i, w = HEAD[s % PER_HEAD]
                        at = p * PER_PAIR + s
                        act.wait_ge(scores_done, at + 1)
                        if has(p, s - BPT):
                            act.wait_ge(scan_done, at - BPT + 1)
                        act.activation(keep[:, i, 0:w], z[i][:, 0:w], ACT.Sigmoid, scale=-1.0).then_inc(keep_done, 1)
                        if has(p, s - i - BPT * 2):
                            act.wait_ge(turned_done, at - i - BPT)
                        act.activation(weight[:, s % (2 * BPT), 0:w], z[i][:, 0:w], ACT.Sigmoid).then_inc(gate_done, 1)
                    for f in range(8):
                        if s == FILL_START[f] + FILL_STEPS and not last(p):
                            act.wait_ge(fill_done, p * NFILL + f + 1)
                            if has(p, f - 1):
                                act.wait_ge(fill_stored, (p * NFILL + f) * 16)
                            act.activation(staged[:, 0].bitcast(F32R), filled[:], ACT.Copy,
                                           scale=QSCALE if f < NT else 1.0).then_inc(fill_high, 1)
                    r = s - TURN_LAG
                    if has(p, r):
                        n0 = r % BPT * P if is_diag(r) else 0
                        at = p * PER_PAIR + r
                        act.wait_ge(turned_done, at + 1)
                        if has(p, r - 2):
                            act.wait_ge(av_done, at - 1)
                        act.activation(att_hi[:, r % 2, n0:TW], turned[r % 2][:, n0:TW], ACT.Copy).then_inc(turned_high, 1)

            pairs(act, pair)

        @block.vector
        def _(dve):
            def split_high(n, slot):
                dve.wait_ge(w_loaded, 16 * n)
                dve.tensor_copy(w_hi[:, slot], w_raw[:]).then_inc(w_high, 1)

            def split_low(n, slot):
                dve.wait_ge(w_high, n)
                dve.tensor_tensor(w_lo[:, slot], w_raw[:], w_hi[:, slot].bitcast(F32), ALU.subtract).then_inc(w_split, 1)

            def pair(p):
                for s in range(PER_PAIR + (OUT_LAG + 1 if last(p) else 0)):
                    if s < PER_PAIR:
                        _, _, i, w = HEAD[s % PER_HEAD]
                        at = p * PER_PAIR + s
                        dve.wait_ge(keep_done, at + 1)
                        if has(p, s - 2):
                            dve.wait_ge(carry_done, at - 1)
                        if is_diag(s):
                            dve.memset(product[:, s % 2, w:w + 1], 1.0)
                            n = w
                        else:
                            n = w + 1
                        back = keep[:, i, 0:n][:, ::-1]
                        dve.tensor_tensor_scan(product[:, s % 2, 0:n][:, ::-1], back, back, 1.0,
                                               ALU.mult, ALU.bypass).then_inc(scan_done, 1)
                    r = s - OUT_LAG
                    if has(p, r) and ends_tile(r % PER_PAIR):
                        dve.wait_ge(av_done, p * PER_PAIR + r + 1)
                        tiles = tile_number(r) if r >= 0 else -1
                        if not (isinstance(p, int) and p == 0 and tiles == 0):
                            dve.wait_ge(y_stored, (p * 8 + tiles) * 16)
                        dve.tensor_copy(y_out[:], y_acc[:]).then_inc(y_copied, 1)
                    for f in range(NFILL):
                        if s == FILL_START[f] + FILL_STEPS:
                            if f < 8 and not last(p):
                                dve.wait_ge(fill_high, p * 8 + f + 1)
                                dve.scalar_tensor_tensor(out=staged[:, 1].bitcast(F32R), in0=filled[:], scalar=QSCALE if f < NT else 1.0,
                                                         in1=staged[:, 0], op0=ALU.mult, op1=ALU.subtract).then_inc(fill_split, 1)
                            else:
                                dve.wait_ge(fill_done, p * NFILL + f + 1)
                                dve.wait_ge(fill_stored, (p * NFILL + f) * 16)
                                dve.tensor_copy(staged[:, 0], filled[:]).then_inc(fill_split, 1)
                    r = s - TURN_LAG
                    if has(p, r):
                        n0 = r % BPT * P if is_diag(r) else 0
                        dve.wait_ge(turned_high, p * PER_PAIR + r + 1)
                        dve.tensor_tensor(att_lo[:, r % 2, n0:TW], turned[r % 2][:, n0:TW], att_hi[:, r % 2, n0:TW].bitcast(F32),
                                          ALU.subtract).then_inc(turned_split, 1)
                    for w in range(3):
                        n = p * 3 + w + 2
                        if last(p) and w == 2:
                            continue
                        if s == SPLIT_HIGH[w]:
                            if has(p, SPLIT_AFTER[w]):
                                dve.wait_ge(fill_done, p * NFILL + SPLIT_AFTER[w])
                            split_high(n, CHUNK_SLOT[(w + 1) % 3])
                        if s == SPLIT_LOW[w]:
                            split_low(n, CHUNK_SLOT[(w + 1) % 3])

            dve.wait_ge(mask_set, 1)
            dve.tensor_copy(mask_r[:], y_out[:, 0:P])
            dve.tensor_copy(ident_r[:], ident[:]).then_inc(mask_ready, 1)
            split_high(1, CHUNK_SLOT[0])
            split_low(1, CHUNK_SLOT[0])
            pairs(dve, pair)

        @block.tensor
        def _(pe):
            def scores(p, s):
                T, _, i, w = HEAD[s % PER_HEAD]
                g = s // BPT
                if i == 0:
                    pe.wait_ge(k_loaded[g % 2], 32 * (p * GROUPS + g // 2 + 1))
                    if is_diag(s):
                        tiles = tile_number(s)
                        pe.wait_ge(q_loaded[T % 2], 64 * (p * 4 + tiles // 2 + 1))
                if has(p, s - BPT):
                    pe.wait_ge(gate_done, p * PER_PAIR + s - BPT + 1)
                keys = k_t[:, g % 2, 0:w]
                pe.matmul(z[i][:, 0:w], q_t[:, T % 2, 0, i * P:(i + 1) * P], keys, start=True, stop=False)
                mm = pe.matmul(z[i][:, 0:w], q_t[:, T % 2, 1, i * P:(i + 1) * P], keys, start=False, stop=not is_diag(s))
                if is_diag(s):
                    mm = pe.matmul(z[i][:, w - P:w], ident_r[:], mask_r[:], start=False, stop=True)
                mm.then_inc(scores_done, 1)

            def turn(p, r):
                j = r % BPT
                if j == 0:
                    pe.wait_ge(weight_done, p * PER_PAIR + r + BPT)
                if has(p, r - 2):
                    pe.wait_ge(turned_split, p * PER_PAIR + r - 1)
                for i in range(j if is_diag(r) else 0, BPT):
                    mm = pe.transpose(turned[r % 2][:, i * P:(i + 1) * P],
                                      weight[:, (r // BPT % 2) * BPT + i, j * P:(j + 1) * P], ident[:])
                mm.then_inc(turned_done, 1)

            def multiply_v(p, r):
                j, g = r % BPT, r // BPT
                n0 = j * P if is_diag(r) else 0
                pe.wait_ge(turned_split, p * PER_PAIR + r + 1)
                if j == 0:
                    pe.wait_ge(v_loaded[g % 2], 16 * (p * GROUPS + g // 2 + 1))
                starts = is_diag(r) and j == 0
                if starts:
                    tiles = tile_number(r)
                    if not (isinstance(p, int) and p == 0 and tiles == 0):
                        pe.wait_ge(y_copied, p * 8 + tiles)
                v = v_t[:, g % 2, j]
                pe.matmul(y_acc[:, n0:TW], v, att_hi[:, r % 2, n0:TW], start=starts, stop=False)
                pe.matmul(y_acc[:, n0:TW], v, att_lo[:, r % 2, n0:TW], start=False,
                          stop=ends_tile(r % PER_PAIR)).then_inc(av_done, 1)

            def project(p, s):
                for f in range(NFILL):
                    part = s - FILL_START[f]
                    if not 0 <= part < FILL_STEPS:
                        continue
                    w, T = f // NT, f % NT
                    if part == 0:
                        if T == 0:
                            pe.wait_ge(w_split, p * 3 + w + 1)
                        if has(p, f - 1):
                            pe.wait_ge(fill_split, p * NFILL + f)
                    slot = CHUNK_SLOT[w]
                    for m in range(part * MM_PER_STEP, (part + 1) * MM_PER_STEP):
                        k, kind = m // 3, m % 3
                        wt = (w_hi, w_hi, w_lo)[kind][:, slot, k]
                        ht = (hT_hi, hT_lo, hT_hi)[kind][:, k, T * TW:(T + 1) * TW]
                        mm = pe.matmul(filled[:], wt, ht, start=m == 0, stop=m == 3 * KD - 1)
                    if part == FILL_STEPS - 1:
                        mm.then_inc(fill_done, 1)

            def pair(p):
                for s in range(PER_PAIR + (AV_LAG if last(p) else 0)):
                    if s < PER_PAIR:
                        scores(p, s)
                    if has(p, s - TURN_LAG):
                        turn(p, s - TURN_LAG)
                    if has(p, s - AV_LAG):
                        multiply_v(p, s - AV_LAG)
                    if s < PER_PAIR:
                        project(p, s)

            pe.wait_ge(mask_ready, 1)
            pairs(pe, pair)


HALO = 16
POOL_WINDOWS = (2, 4, 8, 16)


def mix(nc, io, mem):
    ident = mem["ident"]
    with ExitStack() as ctx:
        def sb(name, shape, dt=F32):
            return ctx.enter_context(nc.sbuf_tensor("mx_" + name, shape, dt))

        def sem(name):
            return ctx.enter_context(nc.semaphore("mx_" + name))

        def sem2(name):
            return [sem(name + "0"), sem(name + "1")]

        wo_raw = sb("wo_raw", [P, 2, D])
        wo_hi, wo_lo = sb("wo_hi", [P, KD, D], F32R), sb("wo_lo", [P, KD, D], F32R)
        a_t = sb("a_t", [P, 2, 4, P])
        p_t = sb("p_t", [P, 2, 2, HALO + P])
        o_t = sb("o_t", [P, 2, NHB, P])
        x_t = sb("x_t", [P, 2, D])
        y_t = sb("y_t", [P, 2, D])
        squares = sb("squares", [P, D])
        yT_hi, yT_lo = sb("yT_hi", [P, KD, P], F32R), sb("yT_lo", [P, KD, P], F32R)
        xn = sb("xn", [P, D])
        h_out = sb("h_out", [P, 2, 2, KD, P])
        sum2, sum4, sum8 = (sb(n, [P, 2, HALO + P]) for n in ("sum2", "sum4", "sum8"))
        window = sb("window", [P, 2, P])
        mean = sb("mean", [P, 2, P])
        pooled = sb("pooled", [P, 2, P])
        v_sq, v_n, v_g, s_b = (sb(n, [P, 256]) for n in ("v_sq", "v_n", "v_g", "s_b"))
        v_stat, y_stat, x_stat = sb("v_stat", [P, 3, 4]), sb("y_stat", [P, 3, NHT]), sb("x_stat", [P, 3, 1])
        minus_half = sb("minus_half", [P, NHT])
        sgu_w, sgu_g, sgu_b = sb("sgu_w", [P, 4, P]), sb("sgu_g", [P, 256]), sb("sgu_b", [P, 4])
        pool_w, pool_scale = sb("pool_w", [P, 2, P]), sb("pool_scale", [P, 256])
        inv_first, inv_rest = sb("inv_first", [P, 2, P]), sb("inv_rest", [P, 2, P])
        mix_g, norm2_g = sb("mix_g", [P, D]), sb("norm2_g", [P, D])
        two_ident = sb("two_ident", [P, HD])

        proj = ctx.enter_context(nc.psum_tensor("mx_proj", [P, 2, TW], F32))
        gelu_turned, y_b, small = (ctx.enter_context(nc.psum_tensor("mx_" + n, [P, TW], F32)) for n in ("gelu_turned", "y_b", "small"))
        turned = ctx.enter_context(nc.psum_tensor("mx_turned", [P, 2, TW], F32))

        const_loaded, pool_w_zero, const_ready = sem("const_loaded"), sem("pool_w_zero"), sem("const_ready")
        N_CONST = 12
        wo_loaded, wo_high, wo_split = sem2("wo_loaded"), sem("wo_high"), sem("wo_split")
        a_loaded, p_loaded, o_loaded, x_loaded = (sem2(n + "_loaded") for n in "apox")
        halo_zero = sem("halo_zero")
        gelu_done, window_step, mean_done, pooled_done = (sem(n) for n in ("gelu_done", "window_step", "mean_done", "pooled_done"))
        gelu_turned_done, yb_done, yb_copied = sem("gelu_turned_done"), sem("yb_done"), sem("yb_copied")
        vsq_done, vsum_done, vmean_done, vstd_done, vn_done, vg_done = (sem(n) for n in ("vsq_done", "vsum_done", "vmean_done", "vstd_done", "vn_done", "vg_done"))
        small_done, sb_done, y_done = sem("small_done"), sem("sb_done"), sem("y_done")
        ysq_done, ysum_done, ymean_done, ystd_done, yn_done, yg_done = (sem(n) for n in ("ysq_done", "ysum_done", "ymean_done", "ystd_done", "yn_done", "yg_done"))
        yT_turned, yT_high, yT_split = sem("yT_turned"), sem("yT_high"), sem("yT_split")
        proj_done, x2_done, x2_stored = sem("proj_done"), sem("x2_done"), sem2("x2_stored")
        xsq_done, xmean_done, xstd_done, xn_done = sem("xsq_done"), sem("xmean_done"), sem("xstd_done"), sem("xn_done")
        hT_turned, hT_high, hT_split, h_stored = sem("hT_turned"), sem("hT_high"), sem("hT_split"), sem2("h_stored")

        def pipeline(engine, slot, start, end):
            for b in range(start, 4):
                slot(b // 2, b % 2)
            with engine.Fori(2, 6) as i:
                slot(i, 0)
                slot(i, 1)
            for b in range(12, end + 1):
                slot(b // 2, b % 2)

        def stage(i, parity, ahead):
            if isinstance(i, int) and not 0 <= 2 * i + parity + ahead < NB:
                return None
            n = parity + ahead
            return i * 2 + n, i + n // 2, n % 2

        def early(k, n=1):
            return isinstance(k, int) and k < n

        block = ctx.enter_context(nc.Block())

        @block.sync
        def _(sp):
            def tokens(k):
                return bass.ds(k * P, P)

            def load_a_o(k, q):
                sp.dma_start(a_t[:, q], io["ap_hbm"][0:4, :, tokens(k)].rearrange("n c t -> c n t")).then_inc(a_loaded[q], 16)
                sp.dma_start(o_t[:, q], io["o_hbm"][:, :, tokens(k)].rearrange("h e t -> e h t")).then_inc(o_loaded[q], 16)

            def load_p(k, q):
                if early(k):
                    src, dst = io["ap_hbm"][4:6, :, 0:P], p_t[:, q, :, HALO:HALO + P]
                else:
                    src, dst = io["ap_hbm"][4:6, :, bass.ds(k * P - HALO, HALO + P)], p_t[:, q]
                sp.dma_start(dst, src.rearrange("n c t -> c n t")).then_inc(p_loaded[q], 16)

            def load_x(k, q):
                sp.dma_start(x_t[:, q], io["x"][tokens(k), :]).then_inc(x_loaded[q], 16)

            def slot(i, parity):
                at = stage(i, parity, -1)
                if at:
                    k, h, q = at
                    sp.wait_ge(x2_done, k + 1)
                    sp.dma_start(io["x2_hbm"][tokens(k), :], x_t[:, q]).then_inc(x2_stored[q], 16)
                    if stage(i, parity, 1):
                        sp.wait_ge(xn_done, k + 1)
                        sp.wait_ge(x2_stored[q], h * 16 + 16)
                        load_x(k + 2, q)
                    sp.wait_ge(hT_split, k * 2 + 2)
                    for a in (1, 0):
                        sp.dma_start(io["h2_hbm"][a, :, :, tokens(k)].rearrange("k c t -> c k t"), h_out[:, q, a]).then_inc(h_stored[q], 16)
                at = stage(i, parity, 4)
                if at and not early(at[0], 2):
                    k, h, q = at
                    sp.wait_ge(gelu_turned_done, k - 1)
                    sp.wait_ge(yb_done, k - 1)
                    load_a_o(k, q)
                    sp.wait_ge(pooled_done, k - 1)
                    load_p(k, q)

            for k in range(2):
                load_a_o(k, k)
                load_p(k, k)
            for n, c in (("sgu_w", sgu_w), ("sgu_b", sgu_b), ("inv_first", inv_first), ("inv_rest", inv_rest)):
                sp.dma_start(c[:], io[n]).then_inc(const_loaded, 16)
            for n, c, w in (("sgu_g", sgu_g, 256), ("pool_scale", pool_scale, 256), ("mix_g", mix_g, D), ("norm2_g", norm2_g, D)):
                sp.dma_start(c[:], io[n].to_broadcast([P, w])).then_inc(const_loaded, 16)
            sp.wait_ge(pool_w_zero, 1)
            for g in range(4):
                rows = slice(g % 2 * HD, g % 2 * HD + HD)
                sp.dma_start(pool_w[rows, g // 2, rows], io["pool_w"][g]).then_inc(const_loaded, 16)
            for k in range(KD):
                if k >= 2:
                    sp.wait_ge(wo_split, k - 1)
                sp.dma_start(wo_raw[:, k % 2], io["w_o"][k]).then_inc(wo_loaded[k % 2], 16)
            for k in range(2):
                load_x(k, k)
            pipeline(sp, slot, -3, NB)
            for q in range(2):
                sp.wait_ge(x2_stored[q], 16 * NB // 2)
                sp.wait_ge(h_stored[q], 32 * NB // 2)

        @block.gpsimd
        def _(pool):
            pool.memset(pool_w[:], 0.0).then_inc(pool_w_zero, 1)
            pool.memset(p_t[:, 0, :, 0:HALO], 0.0).then_inc(halo_zero, 1)
            pool.memset(minus_half[:], -0.5).then_inc(halo_zero, 1)
            pool.wait_ge(const_loaded, 16 * N_CONST)
            pool.affine_select(out=sgu_w[:], in_=sgu_w[:], compare_op=ALU.is_ge, fill=0.0, base=0,
                               pattern=[[0, 4], [1, P]], channel_multiplier=-1).then_inc(const_ready, 1)

            def add_windows(k, h, q):
                tok, p = p_t[:, q], HALO + P
                lo, hi = slice(0, HD), slice(HD, P)
                steps = [
                    (sum2[:, :, 1:p], tok[:, :, 1:p], tok[:, :, 0:p - 1]),
                    (window[lo, 0], tok[lo, 0, HALO:p], tok[lo, 0, HALO - 1:p - 1]),
                    (window[hi, 0], sum2[hi, 0, HALO:p], sum2[hi, 0, HALO - 2:p - 2]),
                    (sum4[:, 1, 3:p], sum2[:, 1, 3:p], sum2[:, 1, 1:p - 2]),
                    (window[lo, 1], sum4[lo, 1, HALO:p], sum4[lo, 1, HALO - 4:p - 4]),
                    (sum8[hi, 1, 7:p], sum4[hi, 1, 7:p], sum4[hi, 1, 3:p - 4]),
                    (window[hi, 1], sum8[hi, 1, HALO:p], sum8[hi, 1, HALO - 8:p - 8]),
                ]
                pool.wait_ge(p_loaded[q], h * 16 + 16)
                if not early(k):
                    pool.wait_ge(mean_done, k)
                for n, (out, x, y) in enumerate(steps):
                    if n:
                        pool.wait_ge(window_step, k * 7 + n)
                    pool.tensor_tensor(out, x, y, ALU.add).then_inc(window_step, 1)
                pool.wait_ge(window_step, k * 7 + 7)

            def inverse_root(stat, ready, done, k):
                w = stat.shape[-1]
                pool.wait_ge(ready, k + 1)
                pool.tensor_tensor(stat[:, 2], stat[:, 1], minus_half[:, 0:w], ALU.pow).then_inc(done, 1)

            def slot(i, parity):
                at = stage(i, parity, -1)
                if at:
                    inverse_root(x_stat, xmean_done, xstd_done, at[0])
                at = stage(i, parity, 1)
                if at:
                    inverse_root(y_stat, ymean_done, ystd_done, at[0])
                    pool.wait_ge(yn_done, at[0] + 1)
                    pool.tensor_tensor(y_t[:, at[2]], y_t[:, at[2]], mix_g[:], ALU.mult).then_inc(yg_done, 1)
                at = stage(i, parity, 2)
                if at:
                    inverse_root(v_stat, vmean_done, vstd_done, at[0])
                at = stage(i, parity, 3)
                if at:
                    add_windows(*at)

            pool.wait_ge(halo_zero, 2)
            pipeline(pool, slot, -3, NB)

        @block.scalar
        def _(act):
            for k in range(KD):
                act.wait_ge(wo_loaded[k % 2], 16 * (k // 2 + 1))
                act.activation(wo_hi[:, k], wo_raw[:, k % 2], ACT.Copy).then_inc(wo_high, 1)

            def slot(i, parity):
                at = stage(i, parity, -1)
                if at:
                    k, h, q = at
                    act.wait_ge(x2_done, k + 1)
                    act.activation(squares[:], x_t[:, q], ACT.Square, accum_out=x_stat[:, 0]).then_inc(xsq_done, 1)
                at = stage(i, parity, 1)
                if at:
                    k, h, q = at
                    act.wait_ge(y_done, k + 1)
                    if not early(k, 2):
                        act.wait_ge(xsq_done, k - 1)
                    act.activation(squares[:], y_t[:, q], ACT.Square).then_inc(ysq_done, 1)
                at = stage(i, parity, 2)
                if at:
                    k, h, q = at
                    act.wait_ge(gelu_turned_done, k + 1)
                    act.activation(v_sq[:], gelu_turned[:, 256:512], ACT.Square).then_inc(vsq_done, 1)
                    act.wait_ge(yb_done, k + 1)
                    if not early(k, 2):
                        act.wait_ge(yT_turned, k * 2 - 2)
                    act.activation(y_t[:, q, 256:768], y_b[:], ACT.Copy).then_inc(yb_copied, 1)
                at = stage(i, parity, 3)
                if at:
                    k, h, q = at
                    act.wait_ge(a_loaded[q], h * 16 + 16)
                    act.activation(a_t[:, q], a_t[:, q], ACT.Gelu).then_inc(gelu_done, 1)
                at = stage(i, parity, -1)
                if at:
                    k, h, q = at
                    for n in range(2):
                        act.wait_ge(hT_turned, k * 2 + n + 1)
                        if n == 0 and not early(k, 2):
                            act.wait_ge(h_stored[q], h * 32)
                        act.activation(h_out[:, q, 0, 4 * n:4 * n + 4].bitcast(F32R),
                                       turned[:, n].rearrange("p (k t) -> p k t", k=4), ACT.Copy).then_inc(hT_high, 1)
                at = stage(i, parity, 1)
                if at:
                    k, h, q = at
                    for n in range(2):
                        act.wait_ge(yT_turned, k * 2 + n + 1)
                        if n == 0 and not early(k):
                            act.wait_ge(proj_done, k * 2)
                        act.activation(yT_hi[:, 4 * n:4 * n + 4], turned[:, n].rearrange("p (k t) -> p k t", k=4),
                                       ACT.Copy).then_inc(yT_high, 1)

            pipeline(act, slot, -3, NB)

        @block.vector
        def _(dve):
            for k in range(KD):
                dve.wait_ge(wo_high, k + 1)
                dve.tensor_tensor(wo_lo[:, k], wo_raw[:, k % 2], wo_hi[:, k].bitcast(F32), ALU.subtract).then_inc(wo_split, 1)
            dve.tensor_copy(two_ident[0:HD], ident[0:HD, 0:HD]).then_inc(const_ready, 1)
            dve.tensor_copy(two_ident[HD:P], ident[HD:P, HD:P]).then_inc(const_ready, 1)
            dve.wait_ge(const_loaded, 16 * N_CONST)

            def mean_plus_eps(stat, n, done):
                dve.tensor_scalar(stat[:, 1], stat[:, 0], 1.0 / n, EPS, ALU.mult, ALU.add).then_inc(done, 1)

            def per_head(ap, n):
                return ap.rearrange("t (h e) -> t h e", h=n)

            def spread(ap, n):
                return ap.unsqueeze(2).to_broadcast([P, n, HD])

            def slot(i, parity):
                at = stage(i, parity, -1)
                if at:
                    k, h, q = at
                    dve.wait_ge(proj_done, k * 2 + 2)
                    dve.wait_ge(x_loaded[q], h * 16 + 16)
                    dve.tensor_tensor(x_t[:, q], proj[:].rearrange("t a n -> t (a n)"), x_t[:, q], ALU.add).then_inc(x2_done, 1)
                    dve.wait_ge(xsq_done, k + 1)
                    mean_plus_eps(x_stat, D, xmean_done)
                    dve.wait_ge(xstd_done, k + 1)
                    if not early(k):
                        dve.wait_ge(hT_turned, k * 2)
                    dve.scalar_tensor_tensor(out=xn[:], in0=x_t[:, q], scalar=x_stat[:, 2], in1=norm2_g[:],
                                             op0=ALU.mult, op1=ALU.mult).then_inc(xn_done, 1)
                at = stage(i, parity, 1)
                if at:
                    k, h, q = at
                    dve.wait_ge(small_done, k + 1)
                    dve.tensor_tensor(per_head(s_b[:], 4), per_head(small[:, 0:256], 4), spread(sgu_b[:], 4), ALU.add).then_inc(sb_done, 1)
                    dve.tensor_tensor(y_t[:, q, 768:1024], small[:, 256:512], pool_scale[:], ALU.mult)
                    dve.wait_ge(sb_done, k + 1)
                    dve.wait_ge(yb_copied, k + 1)
                    dve.tensor_tensor(y_t[:, q, 0:256], s_b[:], gelu_turned[:, 0:256], ALU.mult).then_inc(y_done, 1)
                    dve.wait_ge(ysq_done, k + 1)
                    dve.tensor_reduce(y_stat[:, 0], per_head(squares[:], NHT), AX_X, ALU.add).then_inc(ysum_done, 1)
                    dve.wait_ge(ysum_done, k + 1)
                    mean_plus_eps(y_stat, HD, ymean_done)
                    dve.wait_ge(ystd_done, k + 1)
                    dve.tensor_tensor(per_head(y_t[:, q], NHT), per_head(y_t[:, q], NHT), spread(y_stat[:, 2], NHT), ALU.mult).then_inc(yn_done, 1)
                at = stage(i, parity, 2)
                if at:
                    k, h, q = at
                    dve.wait_ge(vsq_done, k + 1)
                    dve.tensor_reduce(v_stat[:, 0], per_head(v_sq[:], 4), AX_X, ALU.add).then_inc(vsum_done, 1)
                    dve.wait_ge(vsum_done, k + 1)
                    mean_plus_eps(v_stat, HD, vmean_done)
                    dve.wait_ge(window_step, k * 7 + 7)
                    dve.tensor_tensor(mean[:], window[:], (inv_first if early(k) else inv_rest)[:], ALU.mult).then_inc(mean_done, 1)
                    dve.wait_ge(mean_done, k + 1)
                    if not early(k):
                        dve.wait_ge(small_done, k)
                    dve.tensor_tensor(pooled[:], mean[:], p_t[:, q, :, HALO:HALO + P], ALU.subtract).then_inc(pooled_done, 1)
                    dve.wait_ge(vstd_done, k + 1)
                    dve.tensor_tensor(per_head(v_n[:], 4), per_head(gelu_turned[:, 256:512], 4), spread(v_stat[:, 2], 4), ALU.mult).then_inc(vn_done, 1)
                    dve.wait_ge(vn_done, k + 1)
                    dve.tensor_tensor(v_g[:], v_n[:], sgu_g[:], ALU.mult).then_inc(vg_done, 1)
                at = stage(i, parity, -1)
                if at:
                    k, h, q = at
                    for n in range(2):
                        dve.wait_ge(hT_high, k * 2 + n + 1)
                        dve.tensor_tensor(h_out[:, q, 1, 4 * n:4 * n + 4].bitcast(F32R), turned[:, n].rearrange("p (k t) -> p k t", k=4),
                                          h_out[:, q, 0, 4 * n:4 * n + 4], ALU.subtract).then_inc(hT_split, 1)
                at = stage(i, parity, 1)
                if at:
                    k, h, q = at
                    for n in range(2):
                        dve.wait_ge(yT_high, k * 2 + n + 1)
                        dve.tensor_tensor(yT_lo[:, 4 * n:4 * n + 4], turned[:, n].rearrange("p (k t) -> p k t", k=4),
                                          yT_hi[:, 4 * n:4 * n + 4].bitcast(F32), ALU.subtract).then_inc(yT_split, 1)

            pipeline(dve, slot, -3, NB)

        @block.tensor
        def _(pe):
            def project(k, n):
                if n == 0:
                    pe.wait_ge(yT_split, k * 2 + 2)
                    if not early(k):
                        pe.wait_ge(x2_done, k)
                cols = slice(n * TW, (n + 1) * TW)
                split_products(pe, proj[:, n], [(yT_hi[:, c], yT_lo[:, c], wo_hi[:, c, cols], wo_lo[:, c, cols])
                                                for c in range(KD)]).then_inc(proj_done, 1)

            def turn(src, done):
                for n in range(2):
                    for j in range(4):
                        c = 4 * n + j
                        mm = pe.transpose(turned[:, n, j * P:(j + 1) * P], src[:, c * P:(c + 1) * P], ident[:])
                    mm.then_inc(done, 1)

            def slot(i, parity):
                at = stage(i, parity, 0)
                if at:
                    project(at[0], 0)
                at = stage(i, parity, 2)
                if at:
                    k, h, q = at
                    pe.wait_ge(gelu_done, k + 1)
                    if not early(k):
                        pe.wait_ge(y_done, k)
                    for j in range(4):
                        mm = pe.transpose(gelu_turned[:, j * P:(j + 1) * P], a_t[:, q, j], ident[:])
                    mm.then_inc(gelu_turned_done, 1)
                    pe.wait_ge(o_loaded[q], h * 16 + 16)
                    if not early(k):
                        pe.wait_ge(yb_copied, k)
                    for j in range(NHB):
                        mm = pe.matmul(y_b[:, j * HD:(j + 1) * HD], o_t[:, q, j], two_ident[:], start=True, stop=True)
                    mm.then_inc(yb_done, 1)
                at = stage(i, parity, -1)
                if at:
                    k = at[0]
                    pe.wait_ge(xn_done, k + 1)
                    if not early(k):
                        pe.wait_ge(yT_split, k * 2 + 2)
                    turn(xn[:], hT_turned)
                at = stage(i, parity, 0)
                if at:
                    project(at[0], 1)
                at = stage(i, parity, 1)
                if at:
                    k, h, q = at
                    pe.wait_ge(yg_done, k + 1)
                    if not early(k, 2):
                        pe.wait_ge(hT_split, k * 2 - 2)
                    turn(y_t[:, q], yT_turned)
                at = stage(i, parity, 2)
                if at:
                    k, h, q = at
                    pe.wait_ge(vg_done, k + 1)
                    pe.wait_ge(pooled_done, k + 1)
                    if not early(k):
                        pe.wait_ge(y_done, k)
                    for j in range(4):
                        pe.matmul(small[:, j * HD:(j + 1) * HD], sgu_w[:, j], v_g[:, j * HD:(j + 1) * HD], start=True, stop=True)
                    for j in range(2):
                        mm = pe.matmul(small[:, 256 + j * P:256 + (j + 1) * P], pooled[:, j], pool_w[:, j], start=True, stop=True)
                    mm.then_inc(small_done, 1)

            pe.wait_ge(const_ready, 3)
            pe.wait_ge(wo_split, KD)
            pipeline(pe, slot, -3, NB)


def ffn_up(nc, io):
    with ExitStack() as ctx:
        def sb(name, shape, dt=F32):
            return ctx.enter_context(nc.sbuf_tensor("up_" + name, shape, dt))

        def sem(name):
            return ctx.enter_context(nc.semaphore("up_" + name))

        h_hi, h_lo = sb("h_hi", [P, KD, S], F32R), sb("h_lo", [P, KD, S], F32R)
        w_raw = sb("w_raw", [P, 2, KD, P])
        w_hi, w_lo = sb("w_hi", [P, 2, KD, P], F32R), sb("w_lo", [P, 2, KD, P], F32R)
        conv = sb("conv", [P, NF, 2, 4])
        z_c = sb("z_c", [P, 2, S])
        gated = sb("gated", [P, S])
        z = [ctx.enter_context(nc.psum_tensor(f"up_z{i}", [P, S], F32)) for i in range(2)]

        h_loaded = [sem(f"h_loaded{T}") for T in range(NT)]
        conv_loaded = sem("conv_loaded")
        w_loaded = [sem("w_loaded0"), sem("w_loaded1")]
        w_high, w_split = sem("w_high"), sem("w_split")
        z_done, tap2_done, tap1_done, conv_done = sem("z_done"), sem("tap2_done"), sem("tap1_done"), sem("conv_done")
        silu_done, gated_done, gated_stored = sem("silu_done"), sem("gated_done"), sem("gated_stored")

        block = ctx.enter_context(nc.Block())

        @block.sync
        def _(sp):
            def load_w(c):
                for half in range(2):
                    sp.dma_start(w_raw[:, half], io["w_up"][bass.ds(c, 1), half].rearrange("n c k m -> c (n k) m")).then_inc(w_loaded[half], 16)

            load_w(0)
            for T in range(NT):
                for a, h in enumerate((h_hi, h_lo)):
                    cols = slice(T * TW, (T + 1) * TW)
                    sp.dma_start(h[:, :, cols].bitcast(F32), io["h2_hbm"][a, :, :, cols].rearrange("k c t -> c k t")).then_inc(h_loaded[T], 16)
                if T == 0:
                    sp.dma_start(conv[:], io["conv"]).then_inc(conv_loaded, 16)
            with sp.Fori(0, NF - 1) as c:
                sp.wait_ge(w_split, c * 2 + 2)
                load_w(c + 1)
                sp.wait_ge(gated_done, c + 1)
                sp.dma_start(io["gated_hbm"][bass.ds(c, 1)].rearrange("n f t -> f (n t)"), gated[:]).then_inc(gated_stored, 16)
            sp.wait_ge(gated_done, NF)
            sp.dma_start(io["gated_hbm"][NF - 1], gated[:]).then_inc(gated_stored, 16)
            sp.wait_ge(gated_stored, 16 * NF)

        @block.gpsimd
        def _(pool):
            def split(c, half):
                pool.wait_ge(w_high, c * 2 + half + 1)
                pool.tensor_tensor(w_lo[:, half], w_raw[:, half], w_hi[:, half].bitcast(F32), ALU.subtract).then_inc(w_split, 1)

            def gate(c):
                pool.wait_ge(silu_done, c + 1)
                pool.wait_ge(conv_done, c * 2 + 2)
                if not isinstance(c, int) or c > 0:
                    pool.wait_ge(gated_stored, c * 16)
                pool.tensor_tensor(gated[:], z_c[:, 0], z_c[:, 1], ALU.mult).then_inc(gated_done, 1)

            split(0, 0)
            split(0, 1)
            def chunk(c):
                split(c + 1, 0)
                split(c + 1, 1)
                gate(c)

            chunk(0)
            with pool.Fori(1, NF - 1) as c:
                chunk(c)
            gate(NF - 1)

        @block.scalar
        def _(act):
            def high(c, half):
                act.wait_ge(w_loaded[half], c * 16 + 16)
                act.activation(w_hi[:, half], w_raw[:, half], ACT.Copy).then_inc(w_high, 1)

            def last_tap(c, half):
                def per_channel(n):
                    return conv[:, bass.ds(c, 1), half, n:n + 1].rearrange("p a b -> p (a b)")
                act.wait_ge(z_done, c * 8 + half * 4 + 4)
                if not isinstance(c, int) or c > 0:
                    act.wait_ge(gated_done, c)
                act.activation(z_c[:, half], z[half][:], ACT.Identity, bias=per_channel(3), scale=per_channel(2)).then_inc(tap2_done, 1)

            def silu(c):
                act.wait_ge(conv_done, c * 2 + 1)
                act.activation(z_c[:, 0], z_c[:, 0], ACT.Silu).then_inc(silu_done, 1)

            high(0, 0)
            high(0, 1)
            act.wait_ge(conv_loaded, 16)

            def chunk(c):
                last_tap(c, 0)
                high(c + 1, 0)
                silu(c)
                last_tap(c, 1)
                high(c + 1, 1)

            chunk(0)
            with act.Fori(1, NF - 1) as c:
                chunk(c)
            last_tap(NF - 1, 0)
            silu(NF - 1)
            last_tap(NF - 1, 1)

        @block.vector
        def _(dve):
            dve.wait_ge(conv_loaded, 16)
            with dve.Fori(0, NF) as c:
                for half in range(2):
                    n = c * 2 + half
                    for tap, done, ready in ((1, tap1_done, tap2_done), (0, conv_done, tap1_done)):
                        back = 2 - tap
                        dve.wait_ge(ready, n + 1)
                        dve.scalar_tensor_tensor(out=z_c[:, half, back:S], in0=z[half][:, 0:S - back],
                                                 scalar=conv[:, bass.ds(c, 1), half, tap:tap + 1].rearrange("p a b -> p (a b)"),
                                                 in1=z_c[:, half, back:S], op0=ALU.mult, op1=ALU.add).then_inc(done, 1)

        @block.tensor
        def _(pe):
            def chunk(c):
                for half in range(2):
                    pe.wait_ge(w_split, c * 2 + half + 1)
                    if not isinstance(c, int):
                        pe.wait_ge(conv_done, c * 2 + half - 1)
                    for T in range(NT):
                        if isinstance(c, int):
                            pe.wait_ge(h_loaded[T], 32)
                        cols = slice(T * TW, (T + 1) * TW)
                        split_products(pe, z[half][:, cols], [(w_hi[:, half, k], w_lo[:, half, k], h_hi[:, k, cols], h_lo[:, k, cols])
                                                              for k in range(KD)]).then_inc(z_done, 1)

            chunk(0)
            with pe.Fori(1, NF) as c:
                chunk(c)


def ffn_down(nc, io):
    with ExitStack() as ctx:
        def sb(name, shape, dt=F32):
            return ctx.enter_context(nc.sbuf_tensor("dn_" + name, shape, dt))

        def sem(name):
            return ctx.enter_context(nc.semaphore("dn_" + name))

        def sem2(name):
            return [sem(name + "0"), sem(name + "1")]

        w_raw = sb("w_raw", [P, 2, D])
        w_hi, w_lo = sb("w_hi", [P, 2, D], F32R), sb("w_lo", [P, 2, D], F32R)
        g_raw = sb("g_raw", [P, 2, TW])
        g_hi, g_lo = sb("g_hi", [P, 2, TW], F32R), sb("g_lo", [P, 2, TW], F32R)
        x_t = sb("x_t", [P, 2, BPT, D])
        squares = sb("squares", [P, BPT, D])
        stat = sb("stat", [P, 3, BPT])
        minus_half = sb("minus_half", [P, BPT])
        final_g = sb("final_g", [P, D])
        acc = [ctx.enter_context(nc.psum_tensor(f"dn_acc{j}", [P, D], F32)) for j in range(BPT)]

        w_loaded, g_loaded, x_loaded, out_stored = sem2("w_loaded"), sem2("g_loaded"), sem2("x_loaded"), sem("out_stored")
        gain_loaded, half_set = sem("gain_loaded"), sem("half_set")
        high_done, split_done, used = sem("high_done"), sem("split_done"), sem("used")
        acc_done, x3_done, sq_done, mean_done, std_done, out_done = (sem(n) for n in ("acc_done", "x3_done", "sq_done", "mean_done", "std_done", "out_done"))

        block = ctx.enter_context(nc.Block())

        def steps(engine, step, before_tile=None, after_first=None):
            def tile(T):
                if before_tile:
                    before_tile(T)
                for f in range(2):
                    step(T, f, f)
                if after_first:
                    after_first(T)
                with engine.Fori(1, NF // 2) as j:
                    step(T, j * 2, 0)
                    step(T, j * 2 + 1, 1)

            tile(0)
            with engine.Fori(1, NT) as T:
                tile(T)

        def is_start(T, f):
            return isinstance(T, int) and isinstance(f, int)

        @block.sync
        def _(sp):
            def step(T, f, q):
                if not is_start(T, f):
                    sp.wait_ge(split_done, T * (2 * NF) + f * 2 - 2)
                sp.dma_start(w_raw[:, q], io["w_down"][bass.ds(f, 1)].rearrange("n f d -> f (n d)")).then_inc(w_loaded[q], 16)
                sp.dma_start(g_raw[:, q], io["gated_hbm"][bass.ds(f, 1), :, bass.ds(T * TW, TW)].rearrange("n f t -> f (n t)")).then_inc(g_loaded[q], 16)

            def x_rows(name, T):
                return io[name][bass.ds(T * TW, TW), :].rearrange("(j t) d -> t j d", t=P)

            def store(T):
                sp.wait_ge(out_done, T * BPT + BPT)
                sp.dma_start(x_rows("out", T), x_t[:, 0]).then_inc(out_stored, 16)

            def tile_start(T):
                if isinstance(T, int):
                    sp.dma_start(x_t[:, 0], x_rows("x2_hbm", 0)).then_inc(x_loaded[0], 16)

            def after_first(T):
                if not isinstance(T, int):
                    store(T - 1)
                    sp.wait_ge(out_stored, T * 16)
                    sp.dma_start(x_t[:, 0], x_rows("x2_hbm", T)).then_inc(x_loaded[0], 16)

            sp.dma_start(final_g[:], io["final_g"].to_broadcast([P, D])).then_inc(gain_loaded, 16)
            steps(sp, step, tile_start, after_first)
            store(NT - 1)
            sp.wait_ge(out_stored, 16 * NT)

        @block.gpsimd
        def _(pool):
            pool.memset(minus_half[:], -0.5).then_inc(half_set, 1)
            pool.wait_ge(half_set, 1)

            def root(T):
                for j in range(BPT):
                    pool.wait_ge(mean_done, T * BPT + j + 1)
                    pool.tensor_tensor(stat[:, 2, j:j + 1], stat[:, 1, j:j + 1], minus_half[:, j:j + 1], ALU.pow).then_inc(std_done, 1)

            with pool.Fori(0, NT) as T:
                root(T)

        @block.scalar
        def _(act):
            def step(T, f, q):
                loads = T * (NF // 2 * 16) + f * 8 + (16 - 8 * q)
                act.wait_ge(w_loaded[q], loads)
                act.wait_ge(g_loaded[q], loads)
                if isinstance(f, int) and not isinstance(T, int):
                    if f == 1:
                        act.wait_ge(acc_done, T * BPT)
                    else:
                        act.wait_ge(used, T * (NF - 1))
                elif not isinstance(f, int):
                    act.wait_ge(used, T * (NF - 1) + f - 1)
                act.activation(w_hi[:, q], w_raw[:, q], ACT.Copy).then_inc(high_done, 1)
                act.activation(g_hi[:, q], g_raw[:, q], ACT.Copy).then_inc(high_done, 1)

            def finish(T):
                for j in range(BPT):
                    act.wait_ge(x3_done, T * BPT + j + 1)
                    act.activation(squares[:, j], x_t[:, 0, j], ACT.Square, accum_out=stat[:, 0, j:j + 1]).then_inc(sq_done, 1)

            def after_first(T):
                if not isinstance(T, int):
                    finish(T - 1)

            steps(act, step, None, after_first)
            finish(NT - 1)

        @block.vector
        def _(dve):
            dve.wait_ge(gain_loaded, 16)

            def step(T, f, q):
                n = T * (2 * NF) + f * 2
                dve.wait_ge(high_done, n + 1)
                dve.tensor_tensor(w_lo[:, q], w_raw[:, q], w_hi[:, q].bitcast(F32), ALU.subtract).then_inc(split_done, 1)
                dve.wait_ge(high_done, n + 2)
                dve.tensor_tensor(g_lo[:, q], g_raw[:, q], g_hi[:, q].bitcast(F32), ALU.subtract).then_inc(split_done, 1)

            def finish(T):
                dve.wait_ge(x_loaded[0], T * 16 + 16)
                for j in range(BPT):
                    dve.wait_ge(acc_done, T * BPT + j + 1)
                    dve.tensor_tensor(x_t[:, 0, j], acc[j][:], x_t[:, 0, j], ALU.add).then_inc(x3_done, 1)
                for j in range(BPT):
                    dve.wait_ge(sq_done, T * BPT + j + 1)
                    dve.tensor_scalar(stat[:, 1, j:j + 1], stat[:, 0, j:j + 1], 1.0 / D, EPS, ALU.mult, ALU.add).then_inc(mean_done, 1)
                for j in range(BPT):
                    dve.wait_ge(std_done, T * BPT + j + 1)
                    dve.scalar_tensor_tensor(out=x_t[:, 0, j], in0=x_t[:, 0, j], scalar=stat[:, 2, j:j + 1], in1=final_g[:],
                                             op0=ALU.mult, op1=ALU.mult).then_inc(out_done, 1)

            def after_first(T):
                if not isinstance(T, int):
                    finish(T - 1)

            steps(dve, step, None, after_first)
            finish(NT - 1)

        @block.tensor
        def _(pe):
            def step(T, n, q, start, stop):
                pe.wait_ge(split_done, n * 2 + 2)
                for j in range(BPT):
                    if start and not isinstance(T, int):
                        pe.wait_ge(x3_done, T * BPT - BPT + j + 1)
                    t = slice(j * P, (j + 1) * P)
                    for half in range(2):
                        cols = slice(half * TW, (half + 1) * TW)
                        mm = split_products(pe, acc[j][:, cols], [(g_hi[:, q, t], g_lo[:, q, t], w_hi[:, q, cols], w_lo[:, q, cols])],
                                            first=start, last=stop)
                    if stop:
                        mm.then_inc(acc_done, 1)
                if not stop:
                    mm.then_inc(used, 1)

            def tile(T):
                step(T, T * NF, 0, True, False)
                step(T, T * NF + 1, 1, False, False)
                with pe.Fori(1, NF // 2 - 1) as i:
                    step(T, T * NF + i * 2, 0, False, False)
                    step(T, T * NF + i * 2 + 1, 1, False, False)
                step(T, T * NF + NF - 2, 0, False, False)
                step(T, T * NF + NF - 1, 1, False, True)

            tile(0)
            with pe.Fori(1, NT) as T:
                tile(T)


def build(nc, io, upto=5):
    def hbm(name, shape):
        io[name] = nc.dram_tensor(name, shape, F32, kind="Internal").ap()

    hbm("q_hbm", (2, NHB * HD, S))
    hbm("k_hbm", (2, NHB * HD, S))
    hbm("v_hbm", (NHB, NT, P, BPT, 2 * HD))
    hbm("ap_hbm", (6, P, S))
    hbm("o_hbm", (NHB, P, S))
    hbm("x2_hbm", (S, D))
    hbm("h2_hbm", (2, KD, P, S))
    hbm("gated_hbm", (NF, P, S))
    with ExitStack() as ctx:
        mem = {"ident": ctx.enter_context(nc.sbuf_tensor("ident", [P, P], F32))}
        with ExitStack() as front:
            for n in ("hT_hi", "hT_lo"):
                mem[n] = front.enter_context(nc.sbuf_tensor(n, [P, KD, S], F32R))
            project_norm(nc, io, mem)
            if upto >= 2:
                attend(nc, io, mem)
        if upto >= 3:
            mix(nc, io, mem)
        if upto >= 4:
            ffn_up(nc, io)
        if upto >= 5:
            ffn_down(nc, io)


def laid_out(inputs):
    import numpy as np

    a = {n: np.asarray(v) for n, v in inputs.items()}
    w_in = a["w_in"][0]
    wa, wq, wk, wv, wp = np.split(w_in, [512, 1024, 1536, 2048], axis=1)
    w_cm = np.concatenate([wa, wq, wk, wp], axis=1).reshape(KD, P, 14, P)
    conv = np.concatenate([a["conv_w"][0], a["conv_b"]], axis=0)
    width = np.repeat(np.array(POOL_WINDOWS, np.float32), HD).reshape(2, P).T[:, :, None]
    inv_first = (1.0 / np.minimum(np.arange(1, P + 1, dtype=np.float32), width)).astype(np.float32)
    inv_rest = np.broadcast_to(1.0 / width, (P, 2, P)).astype(np.float32)
    return {
        "x": a["x"][0],
        "norm1_g": a["norm1_g"],
        "w_chunks": w_cm.transpose(2, 1, 0, 3)[CHUNK_ORDER],
        "w_v": wv.reshape(KD, P, 512),
        "sgu_g": a["sgu_norm_g"],
        "sgu_w": a["sgu_w"][0].transpose(2, 0, 1),
        "sgu_b": a["sgu_b"][0].transpose(1, 0),
        "pool_w": a["pool_w"][0],
        "pool_scale": a["pool_scale"],
        "inv_first": inv_first,
        "inv_rest": inv_rest,
        "mix_g": a["mix_norm_g"],
        "w_o": a["w_o"][0].reshape(KD, P, D),
        "norm2_g": a["norm2_g"],
        "w_up": a["w_up"][0].reshape(KD, P, 2, NF, P).transpose(3, 2, 1, 0, 4),
        "conv": conv.reshape(4, 2, NF, P).transpose(3, 2, 1, 0),
        "w_down": a["w_down"][0].reshape(NF, P, D),
        "final_g": a["final_g"][None, :],
    }


def kernel(**inputs):
    import numpy as np
    import concourse.bacc as bacc
    from concourse.bass_utils import run_bass_kernel_spmd

    nc = bacc.Bacc("TRN2", target_bir_lowering=False, num_devices=1)
    arrays = {n: np.ascontiguousarray(v) for n, v in laid_out(inputs).items()}
    io = {n: nc.dram_tensor(f"in_{n}", v.shape, F32, kind="ExternalInput").ap() for n, v in arrays.items()}
    io["out"] = nc.dram_tensor("out", (S, D), F32, kind="ExternalOutput").ap()
    build(nc, io)
    r = run_bass_kernel_spmd(nc, [{f"in_{n}": v for n, v in arrays.items()}], core_ids=[0])
    return r.results[0]["out"].reshape(1, S, D)
```

```python
from contextlib import ExitStack

import concourse.bass as bass
from concourse import mybir

F32 = mybir.dt.float32
F32R = mybir.dt.float32r
ACT = mybir.ActivationFunctionType
ALU = mybir.AluOpType
AX_X = mybir.AxisListType.X

P = 128
S, D = 2048, 1024
KD = D // P
HD, NHB = 64, 8
NHT = 16
NB = S // P
TW = 512
NT = S // TW
BPT = TW // P
DFF = 2816
NF = DFF // P
EPS = 1e-6
FIRST_PIECES = 2
BIG = 1e30
QSCALE = HD ** -0.5

CHUNK_ORDER = [4, 8, 5, 9, 0, 6, 10, 1, 7, 11, 2, 3, 12, 13]


def attention_slots():
    return [(T, c, i, (i + 1) * P if c == T else TW) for T in range(NT) for c in range(T, -1, -1) for i in range(BPT)]


def split_products(pe, out, parts, first=True, last=True):
    n = len(parts)
    for i, (sh, sl, mh, ml) in enumerate(parts):
        pe.matmul(out, sh, mh, start=first and i == 0, stop=False)
        pe.matmul(out, sh, ml, start=False, stop=False)
        mm = pe.matmul(out, sl, mh, start=False, stop=last and i == n - 1)
    return mm


def project_norm(nc, io, mem):
    hT_hi, hT_lo, ident = mem["hT_hi"], mem["hT_lo"], mem["ident"]
    q_chunk, k_chunk = 0, 1
    with ExitStack() as ctx:
        def sb(name, shape, dt=F32):
            return ctx.enter_context(nc.sbuf_tensor("pn_" + name, shape, dt))

        def sem(name):
            return ctx.enter_context(nc.semaphore("pn_" + name))

        x_in = sb("x_in", [P, 2, D])
        xn = sb("xn", [P, 2, D])
        gain = sb("gain", [P, D])
        sumsq = sb("sumsq", [P, NB])
        meansq = sb("meansq", [P, NB])
        minus_half = sb("minus_half", [P, NB])
        rstd = sb("rstd", [P, NB])
        wv_raw = sb("wv_raw", [P, 2, 512])
        wv_hi = sb("wv_hi", [P, KD, 512], F32R)
        wv_lo = sb("wv_lo", [P, KD, 512], F32R)
        wc_raw = sb("wc_raw", [P, KD, P])
        wc_hi = sb("wc_hi", [P, KD, P], F32R)
        wc_lo = sb("wc_lo", [P, KD, P], F32R)
        chunk_hi, chunk_lo = ([own[:], old[:, 0:2].rearrange("p a (b c) -> p (a b) c", c=P)]
                              for own, old in ((wc_hi, wv_hi), (wc_lo, wv_lo)))
        staged = sb("staged", [P, 2, 2 * TW])
        v_out = [staged[:, n].rearrange("s (h a e) -> s h a e", h=NHB, a=2) for n in range(2)]
        qk_out = [staged[:, n].rearrange("c (a t) -> c a t", a=2) for n in range(2)]
        turned = [ctx.enter_context(nc.psum_tensor(f"pn_turned{i}", [P, TW], F32)) for i in range(4)]
        prod = [ctx.enter_context(nc.psum_tensor(f"pn_prod{i}", [P, TW], F32)) for i in range(2)]

        x_loaded = [sem("x_loaded0"), sem("x_loaded1")]
        gain_loaded = sem("gain_loaded")
        wv_loaded = [sem("wv_loaded0"), sem("wv_loaded1")]
        wc_loaded = sem("wc_loaded")
        wv_high, wv_split, wc_high, wc_split = sem("wv_high"), sem("wv_split"), sem("wc_high"), sem("wc_split")
        ident_zero, ident_ready = sem("ident_zero"), sem("ident_ready")
        sumsq_done, meansq_done, rstd_done = sem("sumsq_done"), sem("meansq_done"), sem("rstd_done")
        xn_done = sem("xn_done")
        turned_done, turned_high, turned_split = sem("turned_done"), sem("turned_high"), sem("turned_split")
        prod_done, prod_high, prod_split = sem("prod_done"), sem("prod_high"), sem("prod_split")
        stored = [sem("stored0"), sem("stored1")]
        NQK = 2 * NT

        block = ctx.enter_context(nc.Block())

        @block.sync
        def _(sp):
            sp.dma_start(gain[:], io["norm1_g"].to_broadcast([P, D])).then_inc(gain_loaded, 16)
            for b in range(2):
                sp.dma_start(x_in[:, b], io["x"][b * P:(b + 1) * P, :]).then_inc(x_loaded[b], 16)
            def load_x(b):
                sp.wait_ge(xn_done, b - 1)
                sp.dma_start(x_in[:, b % 2], io["x"][b * P:(b + 1) * P, :]).then_inc(x_loaded[b % 2], 16)

            for k in range(KD):
                if k >= 2:
                    sp.wait_ge(wv_split, k - 1)
                sp.dma_start(wv_raw[:, k % 2], io["w_v"][k]).then_inc(wv_loaded[k % 2], 16)
                if k == 1:
                    load_x(2)
                if k == 3:
                    load_x(3)
            sp.dma_start(wc_raw[:], io["w_chunks"][q_chunk]).then_inc(wc_loaded, 16)
            for b in range(NB):
                if b + 4 < NB:
                    load_x(b + 4)
                sp.wait_ge(prod_split, b + 1)
                sp.dma_start(io["v_hbm"][:, b // BPT, :, b % BPT, :].rearrange("h s e -> s h e"),
                             staged[:, b % 2].rearrange("s (h a) -> s h a", h=NHB)).then_inc(stored[b % 2], 16)
                if b == 1:
                    sp.wait_ge(wc_split, 1)
                    sp.dma_start(wc_raw[:], io["w_chunks"][k_chunk]).then_inc(wc_loaded, 16)
            for n in range(NQK):
                dst = io["q_hbm"] if n < NT else io["k_hbm"]
                cols = slice(n % NT * TW, (n % NT + 1) * TW)
                sp.wait_ge(prod_split, NB + n + 1)
                sp.dma_start(dst[:, 0:P, cols].rearrange("a c t -> c a t"),
                             staged[:, n % 2].rearrange("c (a t) -> c a t", a=2)).then_inc(stored[n % 2], 16)
            for slot in range(2):
                sp.wait_ge(stored[slot], 16 * (NB + NQK) // 2)

        @block.gpsimd
        def _(pool):
            pool.memset(ident[:], 0.0).then_inc(ident_zero, 1)
            pool.wait_ge(ident_zero, 1)
            pool.affine_select(out=ident[:], in_=ident[:], compare_op=ALU.not_equal, fill=1.0, base=0,
                               pattern=[[-1, P]], channel_multiplier=1).then_inc(ident_ready, 1)
            pool.memset(minus_half[:], -0.5).then_inc(ident_ready, 1)
            pool.wait_ge(ident_ready, 2)

            def inverse_root(b):
                pool.wait_ge(meansq_done, b + 1)
                pool.tensor_tensor(rstd[:, b:b + 1], meansq[:, b:b + 1], minus_half[:, b:b + 1], ALU.pow).then_inc(rstd_done, 1)

            for k in range(KD):
                if k in (1, 3, 5):
                    inverse_root(k // 2)
                pool.wait_ge(wv_loaded[k % 2], 16 * (k // 2 + 1))
                pool.tensor_copy(wv_hi[:, k], wv_raw[:, k % 2]).then_inc(wv_high, 1)
                pool.wait_ge(wv_high, k + 1)
                pool.tensor_tensor(wv_lo[:, k], wv_raw[:, k % 2], wv_hi[:, k].bitcast(F32), ALU.subtract).then_inc(wv_split, 1)
            def split_chunk(n):
                pool.wait_ge(wc_loaded, 16 * (n + 1))
                pool.tensor_copy(chunk_hi[n], wc_raw[:]).then_inc(wc_high, 1)
                pool.wait_ge(wc_high, n + 1)
                pool.tensor_tensor(chunk_lo[n], wc_raw[:], chunk_hi[n].bitcast(F32), ALU.subtract).then_inc(wc_split, 1)

            for b in range(3, NB):
                inverse_root(b)
                if b == 5:
                    split_chunk(0)
            pool.wait_ge(prod_done, NB)
            split_chunk(1)

        @block.scalar
        def _(act):
            for b in range(NB + 2):
                if b < NB:
                    act.wait_ge(x_loaded[b % 2], 16 * (b // 2 + 1))
                    if b >= 2:
                        act.wait_ge(turned_done, 2 * (b - 1))
                    act.activation(xn[:, b % 2], x_in[:, b % 2], ACT.Square, accum_out=sumsq[:, b:b + 1]).then_inc(sumsq_done, 1)
                if 1 <= b <= NB:
                    for n in (2 * (b - 1), 2 * (b - 1) + 1):
                        act.wait_ge(turned_done, n + 1)
                        dst = hT_hi[:, 4 * (n % 2):4 * (n % 2) + 4, (b - 1) * P:b * P]
                        act.activation(dst, turned[n % 4][:].rearrange("p (k t) -> p k t", k=4), ACT.Copy).then_inc(turned_high, 1)
                if b >= 2:
                    n = b - 2
                    act.wait_ge(prod_done, n + 1)
                    if n >= 2:
                        act.wait_ge(stored[n % 2], 16 * (n // 2))
                    act.activation(v_out[n % 2][:, :, 0, :].bitcast(F32R), prod[n % 2][:].rearrange("p (h e) -> p h e", h=NHB),
                                   ACT.Copy).then_inc(prod_high, 1)
            for n in range(NQK):
                act.wait_ge(prod_done, NB + n + 1)
                act.wait_ge(stored[n % 2], 16 * ((NB + n) // 2))
                act.activation(qk_out[n % 2][:, 0].bitcast(F32R), prod[n % 2][:], ACT.Copy,
                               scale=QSCALE if n < NT else 1.0).then_inc(prod_high, 1)

        @block.vector
        def _(dve):
            dve.wait_ge(gain_loaded, 16)
            for b in range(NB + 2):
                if b < NB:
                    dve.wait_ge(sumsq_done, b + 1)
                    dve.tensor_scalar(meansq[:, b:b + 1], sumsq[:, b:b + 1], 1.0 / D, EPS, ALU.mult, ALU.add).then_inc(meansq_done, 1)
                    dve.wait_ge(rstd_done, b + 1)
                    dve.scalar_tensor_tensor(out=xn[:, b % 2], in0=x_in[:, b % 2], scalar=rstd[:, b:b + 1], in1=gain[:],
                                             op0=ALU.mult, op1=ALU.mult).then_inc(xn_done, 1)
                if 1 <= b <= NB:
                    for n in (2 * (b - 1), 2 * (b - 1) + 1):
                        dve.wait_ge(turned_high, n + 1)
                        ks = slice(4 * (n % 2), 4 * (n % 2) + 4)
                        dve.tensor_tensor(hT_lo[:, ks, (b - 1) * P:b * P], turned[n % 4][:].rearrange("p (k t) -> p k t", k=4),
                                          hT_hi[:, ks, (b - 1) * P:b * P].bitcast(F32), ALU.subtract).then_inc(turned_split, 1)
                if b >= 2:
                    n = b - 2
                    dve.wait_ge(prod_high, n + 1)
                    dve.tensor_tensor(v_out[n % 2][:, :, 1, :].bitcast(F32R), prod[n % 2][:].rearrange("p (h e) -> p h e", h=NHB),
                                      v_out[n % 2][:, :, 0, :], ALU.subtract).then_inc(prod_split, 1)
            for n in range(NQK):
                dve.wait_ge(prod_high, NB + n + 1)
                dve.scalar_tensor_tensor(out=qk_out[n % 2][:, 1].bitcast(F32R), in0=prod[n % 2][:], scalar=QSCALE if n < NT else 1.0,
                                         in1=qk_out[n % 2][:, 0], op0=ALU.mult, op1=ALU.subtract).then_inc(prod_split, 1)

        @block.tensor
        def _(pe):
            pe.wait_ge(ident_ready, 1)

            def turn(b):
                pe.wait_ge(xn_done, b + 1)
                for n in (2 * b, 2 * b + 1):
                    if n >= 4:
                        pe.wait_ge(turned_split, n - 3)
                    for j in range(4):
                        k = 4 * (n % 2) + j
                        mm = pe.transpose(turned[n % 4][:, j * P:(j + 1) * P], xn[:, b % 2, k * P:(k + 1) * P], ident[:])
                    mm.then_inc(turned_done, 1)

            turn(0)
            turn(1)
            for b in range(NB):
                if b == 0:
                    pe.wait_ge(wv_split, KD)
                pe.wait_ge(turned_split, 2 * b + 2)
                if b >= 2:
                    pe.wait_ge(prod_split, b - 1)
                ts = slice(b * P, (b + 1) * P)
                split_products(pe, prod[b % 2][:], [(hT_hi[:, k, ts], hT_lo[:, k, ts], wv_hi[:, k], wv_lo[:, k])
                                                    for k in range(KD)]).then_inc(prod_done, 1)
                if b + 2 < NB:
                    turn(b + 2)
            for n in range(NQK):
                T = n % NT
                pe.wait_ge(wc_split, n // NT + 1)
                pe.wait_ge(prod_split, NB + n - 1)
                ts = slice(T * TW, (T + 1) * TW)
                split_products(pe, prod[n % 2][:], [(chunk_hi[n // NT][:, k], chunk_lo[n // NT][:, k], hT_hi[:, k, ts],
                                                     hT_lo[:, k, ts]) for k in range(KD)]).then_inc(prod_done, 1)


def attend(nc, io, mem):
    hT_hi, hT_lo, ident = mem["hT_hi"], mem["hT_lo"], mem["ident"]
    HEAD = attention_slots()
    PER_HEAD, PER_PAIR = len(HEAD), 2 * len(HEAD)
    GROUPS = PER_HEAD // BPT
    TURN_LAG, AV_LAG, OUT_LAG = 5, 7, 8
    NFILL = 12
    FILL_START = [2 + f * (PER_PAIR - 2) // NFILL for f in range(NFILL)]
    FILL_STEPS = 6
    MM_PER_STEP = 3 * KD // FILL_STEPS
    SPLIT_HIGH, SPLIT_LOW, SPLIT_AFTER = [10, 37, 79], [12, 39, 79], [-4, 4, 12]
    CHUNK_SLOT = [0, 1, 0]
    LOAD_RAW = [1, 4, 11]

    def is_diag(s):
        T, c, _, _ = HEAD[s % PER_HEAD]
        return c == T

    def ends_tile(s):
        _, c, i, _ = HEAD[s % PER_HEAD]
        return c == 0 and i == BPT - 1

    def tile_number(s):
        return sum(ends_tile(r) for r in range(s))

    with ExitStack() as ctx:
        def sb(name, shape, dt=F32):
            return ctx.enter_context(nc.sbuf_tensor("at_" + name, shape, dt))

        def sem(name):
            return ctx.enter_context(nc.semaphore("at_" + name))

        def bank(name):
            return ctx.enter_context(nc.psum_tensor("at_" + name, [P, TW], F32))

        keep = sb("keep", [P, BPT, TW + 1])
        weight = sb("weight", [P, 2 * BPT, TW])
        product = sb("product", [P, 2, TW + 1])
        att_hi = sb("att_hi", [P, 2, TW], F32R)
        att_lo = sb("att_lo", [P, 2, TW], F32R)
        q_t = sb("q_t", [P, 2, 2, TW], F32R)
        k_t = sb("k_t", [P, 2, TW], F32R)
        v_t = sb("v_t", [P, 2, BPT, 2 * HD], F32R)
        y_out = sb("y_out", [P, TW])
        w_raw = sb("w_raw", [P, KD, P])
        w_hi = sb("w_hi", [P, 2, KD, P], F32R)
        w_lo = sb("w_lo", [P, 2, KD, P], F32R)
        staged = sb("staged", [P, 2, TW])
        ident_r = sb("ident_r", [P, P], F32R)
        mask_r = sb("mask_r", [P, P], F32R)
        z = [bank(f"z{i}") for i in range(BPT)]
        turned = [bank(f"turned{i}") for i in range(2)]
        y_acc, filled = bank("y_acc"), bank("filled")

        q_loaded, k_loaded, v_loaded = ([sem(f"{n}_loaded{i}") for i in range(2)] for n in "qkv")
        mask_zero, mask_set, mask_ready = sem("mask_zero"), sem("mask_set"), sem("mask_ready")
        scores_done, keep_done, gate_done = sem("scores_done"), sem("keep_done"), sem("gate_done")
        scan_done, weight_done, carry_done = sem("scan_done"), sem("weight_done"), sem("carry_done")
        turned_done, turned_high, turned_split = sem("turned_done"), sem("turned_high"), sem("turned_split")
        av_done, y_copied, y_stored = sem("av_done"), sem("y_copied"), sem("y_stored")
        w_loaded, w_high, w_split = sem("w_loaded"), sem("w_high"), sem("w_split")
        fill_done, fill_high, fill_split, fill_stored = sem("fill_done"), sem("fill_high"), sem("fill_split"), sem("fill_stored")

        def pairs(engine, body):
            body(0)
            with engine.Fori(1, 3) as p:
                body(p)
            body(3)

        def has(p, s):
            return s < PER_PAIR and not (isinstance(p, int) and p == 0 and s < 0)

        def last(p):
            return isinstance(p, int) and p == 3

        block = ctx.enter_context(nc.Block())

        @block.sync
        def _(sp):
            def load_q(p, e, T):
                slot = T % 2
                for a in (1, 0):
                    for half in range(2):
                        sp.dma_start(q_t[half * HD:(half + 1) * HD, slot, a].bitcast(F32),
                                     io["q_hbm"][a, bass.ds(p * P + e * HD, HD), T * TW:(T + 1) * TW]).then_inc(q_loaded[slot], 16)

            def load_k(p, g):
                T, c, _, _ = HEAD[BPT * g % PER_HEAD]
                e = g // GROUPS
                for half in (1, 0):
                    sp.dma_start(k_t[half * HD:(half + 1) * HD, g % 2].bitcast(F32),
                                 io["k_hbm"][half, bass.ds(p * P + e * HD, HD), c * TW:(c + 1) * TW]).then_inc(k_loaded[g % 2], 16)

            def load_v(p, g):
                T, c, _, _ = HEAD[BPT * g % PER_HEAD]
                sp.dma_start(v_t[:, g % 2].bitcast(F32).rearrange("s j e -> s (j e)"),
                             io["v_hbm"][bass.ds(2 * p + g // GROUPS, 1), c].rearrange("h s j e -> s (h j e)")).then_inc(v_loaded[g % 2], 16)

            def store_y(p, s):
                e, T = s % PER_PAIR // PER_HEAD, HEAD[s % PER_HEAD][0]
                head = 2 * p + e if s >= 0 else 2 * p - 1
                sp.wait_ge(y_copied, p * 8 + tile_number(s) + 1 if s >= 0 else p * 8)
                sp.dma_start(io["o_hbm"][bass.ds(head, 1), :, T * TW:(T + 1) * TW].rearrange("h e t -> (h e) t"), y_out[:]).then_inc(y_stored, 16)

            def store_fill(p, f):
                sp.wait_ge(fill_split, p * NFILL + f + 1)
                cols = slice(f % NT * TW, (f % NT + 1) * TW)
                if last(p) or f // NT == 2:
                    row = p + (f // NT if last(p) else 0)
                    sp.dma_start(io["ap_hbm"][bass.ds(row, 1), :, cols].rearrange("n c t -> (n c) t"), staged[:, 0]).then_inc(fill_stored, 16)
                else:
                    dst = io["q_hbm"] if f // NT == 0 else io["k_hbm"]
                    sp.dma_start(dst[:, bass.ds(p * P + P, P), cols].rearrange("a c t -> c a t"), staged[:]).then_inc(fill_stored, 16)

            def pair(p):
                for g in range(2 * GROUPS):
                    s = BPT * g
                    T = HEAD[s % PER_HEAD][0]
                    if is_diag(s) and not (last(p) and s // PER_HEAD == 1 and T == NT - 1):
                        e, T1 = (s // PER_HEAD, T + 1) if T < NT - 1 else (s // PER_HEAD + 1, 0)
                        if has(p, s - 1):
                            sp.wait_ge(scores_done, p * PER_PAIR + s)
                        if e == 2:
                            sp.wait_ge(fill_stored, p * (NFILL * 16) + 8 * 16)
                        load_q(p, e, T1)
                    if not (last(p) and g == 2 * GROUPS - 1):
                        if not (isinstance(p, int) and p == 0 and g == 0):
                            sp.wait_ge(scores_done, p * PER_PAIR + s)
                        load_k(p, g + 1)
                    if not (isinstance(p, int) and p == 0 and g < 2):
                        sp.wait_ge(av_done, p * PER_PAIR + s - BPT)
                    if not (isinstance(p, int) and p == 0 and g == 0):
                        load_v(p, g)
                    for w in range(3):
                        if g == LOAD_RAW[w] and not (last(p) and w == 2):
                            sp.wait_ge(w_split, p * 3 + w + 1)
                            sp.dma_start(w_raw[:], io["w_chunks"][bass.ds(p * 3 + w + 3, 1)].rearrange("n c k m -> c (n k) m")).then_inc(w_loaded, 16)
                    for f in range(NFILL):
                        if g == min(-(-(FILL_START[f] + 8) // BPT), 2 * GROUPS - 1):
                            store_fill(p, f)
                    for r in range(-BPT, PER_PAIR):
                        if ends_tile(r % PER_PAIR) and -(-(r + OUT_LAG + 1) // BPT) == g and has(p, r):
                            store_y(p, r)

            load_q(0, 0, 0)
            load_k(0, 0)
            load_v(0, 0)
            sp.dma_start(w_raw[:], io["w_chunks"][2]).then_inc(w_loaded, 16)
            pairs(sp, pair)
            store_y(3, PER_PAIR - 1)
            sp.wait_ge(y_stored, 16 * NHB * NT)
            sp.wait_ge(fill_stored, 16 * 4 * NFILL)

        @block.gpsimd
        def _(pool):
            pool.memset(y_out[:, 0:P], 0.0).then_inc(mask_zero, 1)
            pool.wait_ge(mask_zero, 1)
            pool.affine_select(out=y_out[:, 0:P], in_=y_out[:, 0:P], compare_op=ALU.is_gt, fill=-BIG, base=0,
                               pattern=[[-1, P]], channel_multiplier=1).then_inc(mask_set, 1)

            def pair(p):
                for s in range(PER_PAIR):
                    _, _, i, w = HEAD[s % PER_HEAD]
                    at = p * PER_PAIR + s
                    pool.wait_ge(scan_done, at + 1)
                    pool.wait_ge(gate_done, at + 1)
                    gate = weight[:, s % (2 * BPT), 0:w]
                    pool.tensor_tensor(gate, product[:, s % 2, 1:w + 1], gate, ALU.mult).then_inc(weight_done, 1)
                    pool.tensor_copy(keep[:, i, TW:TW + 1], product[:, s % 2, 0:1]).then_inc(carry_done, 1)

            pairs(pool, pair)

        @block.scalar
        def _(act):
            def pair(p):
                for s in range(PER_PAIR + (TURN_LAG if last(p) else 0)):
                    if s < PER_PAIR:
                        _, _, i, w = HEAD[s % PER_HEAD]
                        at = p * PER_PAIR + s
                        act.wait_ge(scores_done, at + 1)
                        if has(p, s - BPT):
                            act.wait_ge(scan_done, at - BPT + 1)
                        act.activation(keep[:, i, 0:w], z[i][:, 0:w], ACT.Sigmoid, scale=-1.0).then_inc(keep_done, 1)
                        if has(p, s - i - BPT * 2):
                            act.wait_ge(turned_done, at - i - BPT)
                        act.activation(weight[:, s % (2 * BPT), 0:w], z[i][:, 0:w], ACT.Sigmoid).then_inc(gate_done, 1)
                    for f in range(8):
                        if s == FILL_START[f] + FILL_STEPS and not last(p):
                            act.wait_ge(fill_done, p * NFILL + f + 1)
                            if has(p, f - 1):
                                act.wait_ge(fill_stored, (p * NFILL + f) * 16)
                            act.activation(staged[:, 0].bitcast(F32R), filled[:], ACT.Copy,
                                           scale=QSCALE if f < NT else 1.0).then_inc(fill_high, 1)
                    r = s - TURN_LAG
                    if has(p, r):
                        n0 = r % BPT * P if is_diag(r) else 0
                        at = p * PER_PAIR + r
                        act.wait_ge(turned_done, at + 1)
                        if has(p, r - 2):
                            act.wait_ge(av_done, at - 1)
                        act.activation(att_hi[:, r % 2, n0:TW], turned[r % 2][:, n0:TW], ACT.Copy).then_inc(turned_high, 1)

            pairs(act, pair)

        @block.vector
        def _(dve):
            def split_high(n, slot):
                dve.wait_ge(w_loaded, 16 * n)
                dve.tensor_copy(w_hi[:, slot], w_raw[:]).then_inc(w_high, 1)

            def split_low(n, slot):
                dve.wait_ge(w_high, n)
                dve.tensor_tensor(w_lo[:, slot], w_raw[:], w_hi[:, slot].bitcast(F32), ALU.subtract).then_inc(w_split, 1)

            def pair(p):
                for s in range(PER_PAIR + (OUT_LAG + 1 if last(p) else 0)):
                    if s < PER_PAIR:
                        _, _, i, w = HEAD[s % PER_HEAD]
                        at = p * PER_PAIR + s
                        dve.wait_ge(keep_done, at + 1)
                        if has(p, s - 2):
                            dve.wait_ge(carry_done, at - 1)
                        if is_diag(s):
                            dve.memset(product[:, s % 2, w:w + 1], 1.0)
                            n = w
                        else:
                            n = w + 1
                        back = keep[:, i, 0:n][:, ::-1]
                        dve.tensor_tensor_scan(product[:, s % 2, 0:n][:, ::-1], back, back, 1.0,
                                               ALU.mult, ALU.bypass).then_inc(scan_done, 1)
                    r = s - OUT_LAG
                    if has(p, r) and ends_tile(r % PER_PAIR):
                        dve.wait_ge(av_done, p * PER_PAIR + r + 1)
                        tiles = tile_number(r) if r >= 0 else -1
                        if not (isinstance(p, int) and p == 0 and tiles == 0):
                            dve.wait_ge(y_stored, (p * 8 + tiles) * 16)
                        dve.tensor_copy(y_out[:], y_acc[:]).then_inc(y_copied, 1)
                    for f in range(NFILL):
                        if s == FILL_START[f] + FILL_STEPS:
                            if f < 8 and not last(p):
                                dve.wait_ge(fill_high, p * 8 + f + 1)
                                dve.scalar_tensor_tensor(out=staged[:, 1].bitcast(F32R), in0=filled[:], scalar=QSCALE if f < NT else 1.0,
                                                         in1=staged[:, 0], op0=ALU.mult, op1=ALU.subtract).then_inc(fill_split, 1)
                            else:
                                dve.wait_ge(fill_done, p * NFILL + f + 1)
                                dve.wait_ge(fill_stored, (p * NFILL + f) * 16)
                                dve.tensor_copy(staged[:, 0], filled[:]).then_inc(fill_split, 1)
                    r = s - TURN_LAG
                    if has(p, r):
                        n0 = r % BPT * P if is_diag(r) else 0
                        dve.wait_ge(turned_high, p * PER_PAIR + r + 1)
                        dve.tensor_tensor(att_lo[:, r % 2, n0:TW], turned[r % 2][:, n0:TW], att_hi[:, r % 2, n0:TW].bitcast(F32),
                                          ALU.subtract).then_inc(turned_split, 1)
                    for w in range(3):
                        n = p * 3 + w + 2
                        if last(p) and w == 2:
                            continue
                        if s == SPLIT_HIGH[w]:
                            if has(p, SPLIT_AFTER[w]):
                                dve.wait_ge(fill_done, p * NFILL + SPLIT_AFTER[w])
                            split_high(n, CHUNK_SLOT[(w + 1) % 3])
                        if s == SPLIT_LOW[w]:
                            split_low(n, CHUNK_SLOT[(w + 1) % 3])

            dve.wait_ge(mask_set, 1)
            dve.tensor_copy(mask_r[:], y_out[:, 0:P])
            dve.tensor_copy(ident_r[:], ident[:]).then_inc(mask_ready, 1)
            split_high(1, CHUNK_SLOT[0])
            split_low(1, CHUNK_SLOT[0])
            pairs(dve, pair)

        @block.tensor
        def _(pe):
            def scores(p, s):
                T, _, i, w = HEAD[s % PER_HEAD]
                g = s // BPT
                if i == 0:
                    pe.wait_ge(k_loaded[g % 2], 32 * (p * GROUPS + g // 2 + 1))
                    if is_diag(s):
                        tiles = tile_number(s)
                        pe.wait_ge(q_loaded[T % 2], 64 * (p * 4 + tiles // 2 + 1))
                if has(p, s - BPT):
                    pe.wait_ge(gate_done, p * PER_PAIR + s - BPT + 1)
                keys = k_t[:, g % 2, 0:w]
                pe.matmul(z[i][:, 0:w], q_t[:, T % 2, 0, i * P:(i + 1) * P], keys, start=True, stop=False)
                mm = pe.matmul(z[i][:, 0:w], q_t[:, T % 2, 1, i * P:(i + 1) * P], keys, start=False, stop=not is_diag(s))
                if is_diag(s):
                    mm = pe.matmul(z[i][:, w - P:w], ident_r[:], mask_r[:], start=False, stop=True)
                mm.then_inc(scores_done, 1)

            def turn(p, r):
                j = r % BPT
                if j == 0:
                    pe.wait_ge(weight_done, p * PER_PAIR + r + BPT)
                if has(p, r - 2):
                    pe.wait_ge(turned_split, p * PER_PAIR + r - 1)
                for i in range(j if is_diag(r) else 0, BPT):
                    mm = pe.transpose(turned[r % 2][:, i * P:(i + 1) * P],
                                      weight[:, (r // BPT % 2) * BPT + i, j * P:(j + 1) * P], ident[:])
                mm.then_inc(turned_done, 1)

            def multiply_v(p, r):
                j, g = r % BPT, r // BPT
                n0 = j * P if is_diag(r) else 0
                pe.wait_ge(turned_split, p * PER_PAIR + r + 1)
                if j == 0:
                    pe.wait_ge(v_loaded[g % 2], 16 * (p * GROUPS + g // 2 + 1))
                starts = is_diag(r) and j == 0
                if starts:
                    tiles = tile_number(r)
                    if not (isinstance(p, int) and p == 0 and tiles == 0):
                        pe.wait_ge(y_copied, p * 8 + tiles)
                v = v_t[:, g % 2, j]
                pe.matmul(y_acc[:, n0:TW], v, att_hi[:, r % 2, n0:TW], start=starts, stop=False)
                pe.matmul(y_acc[:, n0:TW], v, att_lo[:, r % 2, n0:TW], start=False,
                          stop=ends_tile(r % PER_PAIR)).then_inc(av_done, 1)

            def project(p, s):
                for f in range(NFILL):
                    part = s - FILL_START[f]
                    if not 0 <= part < FILL_STEPS:
                        continue
                    w, T = f // NT, f % NT
                    if part == 0:
                        if T == 0:
                            pe.wait_ge(w_split, p * 3 + w + 1)
                        if has(p, f - 1):
                            pe.wait_ge(fill_split, p * NFILL + f)
                    slot = CHUNK_SLOT[w]
                    for m in range(part * MM_PER_STEP, (part + 1) * MM_PER_STEP):
                        k, kind = m // 3, m % 3
                        wt = (w_hi, w_hi, w_lo)[kind][:, slot, k]
                        ht = (hT_hi, hT_lo, hT_hi)[kind][:, k, T * TW:(T + 1) * TW]
                        mm = pe.matmul(filled[:], wt, ht, start=m == 0, stop=m == 3 * KD - 1)
                    if part == FILL_STEPS - 1:
                        mm.then_inc(fill_done, 1)

            def pair(p):
                for s in range(PER_PAIR + (AV_LAG if last(p) else 0)):
                    if s < PER_PAIR:
                        scores(p, s)
                    if has(p, s - TURN_LAG):
                        turn(p, s - TURN_LAG)
                    if has(p, s - AV_LAG):
                        multiply_v(p, s - AV_LAG)
                    if s < PER_PAIR:
                        project(p, s)

            pe.wait_ge(mask_ready, 1)
            pairs(pe, pair)


HALO = 16
POOL_WINDOWS = (2, 4, 8, 16)


def mix(nc, io, mem):
    ident = mem["ident"]
    with ExitStack() as ctx:
        def sb(name, shape, dt=F32):
            return ctx.enter_context(nc.sbuf_tensor("mx_" + name, shape, dt))

        def sem(name):
            return ctx.enter_context(nc.semaphore("mx_" + name))

        def sem2(name):
            return [sem(name + "0"), sem(name + "1")]

        wo_raw = mem["wo_raw"]
        wo_hi, wo_lo = sb("wo_hi", [P, KD, D], F32R), sb("wo_lo", [P, KD, D], F32R)
        a_t = sb("a_t", [P, 2, 4, P])
        p_t = sb("p_t", [P, 2, 2, HALO + P])
        o_t = sb("o_t", [P, 2, NHB, P])
        x_t = sb("x_t", [P, 2, D])
        y_t, y_sq = mem["gated"][:].rearrange("p (a d) -> p a d", a=2), mem["g_raw"][:].rearrange("p a t -> p (a t)")
        yT_hi, yT_lo = sb("yT_hi", [P, 2, KD, P], F32R), sb("yT_lo", [P, 2, KD, P], F32R)
        xn = sb("xn", [P, D])
        h_out = sb("h_out", [P, 2, 2, KD, P])
        sum2, sum4, sum8 = (sb(n, [P, 2, HALO + P]) for n in ("sum2", "sum4", "sum8"))
        window = sb("window", [P, 2, P])
        mean = sb("mean", [P, 2, P])
        pooled = sb("pooled", [P, 2, P])
        v_sq, v_n, v_g, s_b = (sb(n, [P, 256]) for n in ("v_sq", "v_n", "v_g", "s_b"))
        v_stat, y_stat, x_stat = sb("v_stat", [P, 3, 4]), sb("y_stat", [P, 3, NHT]), sb("x_stat", [P, 3, 1])
        minus_half = sb("minus_half", [P, NHT])
        sgu_w, sgu_g, sgu_b = sb("sgu_w", [P, 4, P]), sb("sgu_g", [P, 256]), sb("sgu_b", [P, 4])
        pool_w, pool_scale = sb("pool_w", [P, 2, P]), sb("pool_scale", [P, 256])
        inv_first, inv_rest = sb("inv_first", [P, 2, P]), sb("inv_rest", [P, 2, P])
        mix_g, norm2_g = sb("mix_g", [P, D]), sb("norm2_g", [P, D])
        two_ident = sb("two_ident", [P, HD])

        proj = ctx.enter_context(nc.psum_tensor("mx_proj", [P, 2, TW], F32))
        gelu_turned, y_b, small = (ctx.enter_context(nc.psum_tensor("mx_" + n, [P, TW], F32)) for n in ("gelu_turned", "y_b", "small"))
        turned = ctx.enter_context(nc.psum_tensor("mx_turned", [P, 2, TW], F32))

        const_loaded, pool_w_zero, const_ready = sem("const_loaded"), sem("pool_w_zero"), sem("const_ready")
        N_CONST = 12
        wo_loaded, wo_high, wo_split = sem2("wo_loaded"), sem("wo_high"), sem("wo_split")
        a_loaded, p_loaded, o_loaded, x_loaded = (sem2(n + "_loaded") for n in "apox")
        halo_zero = sem("halo_zero")
        gelu_done, window_step, mean_done, pooled_done = (sem(n) for n in ("gelu_done", "window_step", "mean_done", "pooled_done"))
        gelu_turned_done, yb_done, yb_copied = sem("gelu_turned_done"), sem("yb_done"), sem("yb_copied")
        vsq_done, vsum_done, vmean_done, vstd_done, vn_done, vg_done = (sem(n) for n in ("vsq_done", "vsum_done", "vmean_done", "vstd_done", "vn_done", "vg_done"))
        small_done, sb_done, y_done = sem("small_done"), sem("sb_done"), sem("y_done")
        ysq_done, ysum_done, ymean_done, ystd_done, yn_done, yg_done = (sem(n) for n in ("ysq_done", "ysum_done", "ymean_done", "ystd_done", "yn_done", "yg_done"))
        yT_turned, yT_high, yT_split = sem("yT_turned"), sem("yT_high"), sem("yT_split")
        proj_done, x2_done, x2_stored = sem("proj_done"), sem("x2_done"), sem2("x2_stored")
        xsq_done, xmean_done, xstd_done, xn_done = sem("xsq_done"), sem("xmean_done"), sem("xstd_done"), sem("xn_done")
        hT_turned, hT_high, hT_split, h_stored = sem("hT_turned"), sem("hT_high"), sem("hT_split"), sem2("h_stored")

        def pipeline(engine, slot, start, end):
            for b in range(start, 4):
                slot(b // 2, b % 2)
            with engine.Fori(2, 6) as i:
                slot(i, 0)
                slot(i, 1)
            for b in range(12, end + 1):
                slot(b // 2, b % 2)

        def stage(i, parity, ahead):
            if isinstance(i, int) and not 0 <= 2 * i + parity + ahead < NB:
                return None
            n = parity + ahead
            return i * 2 + n, i + n // 2, n % 2

        def early(k, n=1):
            return isinstance(k, int) and k < n

        WO_SHARE = {(-2, 1): range(0, 3), (-1, 0): range(3, 6), (-1, 1): range(6, KD)}

        block = ctx.enter_context(nc.Block())

        @block.sync
        def _(sp):
            def tokens(k):
                return bass.ds(k * P, P)

            def load_a_o(k, q):
                sp.dma_start(a_t[:, q], io["ap_hbm"][0:4, :, tokens(k)].rearrange("n c t -> c n t")).then_inc(a_loaded[q], 16)
                sp.dma_start(o_t[:, q], io["o_hbm"][:, :, tokens(k)].rearrange("h e t -> e h t")).then_inc(o_loaded[q], 16)

            def load_p(k, q):
                if early(k):
                    src, dst = io["ap_hbm"][4:6, :, 0:P], p_t[:, q, :, HALO:HALO + P]
                else:
                    src, dst = io["ap_hbm"][4:6, :, bass.ds(k * P - HALO, HALO + P)], p_t[:, q]
                sp.dma_start(dst, src.rearrange("n c t -> c n t")).then_inc(p_loaded[q], 16)

            def load_x(k, q):
                sp.dma_start(x_t[:, q], io["x"][tokens(k), :]).then_inc(x_loaded[q], 16)

            def load_for_ffn_up():
                for half in range(2):
                    sp.dma_start(mem["w_raw"][:, half], io["w_up"][0, half].rearrange("c k m -> c (k m)")).then_inc(mem["w_loaded"][half], 16)
                for q in range(2):
                    sp.wait_ge(h_stored[q], 32 * BPT // 2)
                for piece in range(FIRST_PIECES):
                    ks = slice(piece * KD // FIRST_PIECES, (piece + 1) * KD // FIRST_PIECES)
                    for a in range(2):
                        sp.dma_start(mem["first_tile"][:, a, ks].bitcast(F32), io["h2_hbm"][a, ks, :, 0:TW].rearrange("k c t -> c k t")).then_inc(mem["first_loaded"][piece], 16)

            def slot(i, parity):
                if isinstance(i, int) and (i, parity) == (6, 0):
                    load_for_ffn_up()
                ahead = stage(i, parity, 4)
                if ahead and not early(ahead[0], 2):
                    k, h, q = ahead
                    sp.wait_ge(gelu_turned_done, k - 1)
                    sp.wait_ge(yb_done, k - 1)
                    load_a_o(k, q)
                at = stage(i, parity, -1)
                if at:
                    sp.wait_ge(x2_done, at[0] * 2 + 2)
                    sp.dma_start(io["x2_hbm"][tokens(at[0]), :], x_t[:, at[2]]).then_inc(x2_stored[at[2]], 16)
                at = stage(i, parity, -2)
                if at:
                    k, h, q = at
                    sp.wait_ge(hT_split, k * 2 + 2)
                    for a in (1, 0):
                        sp.dma_start(io["h2_hbm"][a, :, :, tokens(k)].rearrange("k c t -> c k t"), h_out[:, q, a]).then_inc(h_stored[q], 16)
                if ahead and not early(ahead[0], 2):
                    k, h, q = ahead
                    sp.wait_ge(pooled_done, k - 1)
                    load_p(k, q)
                at = stage(i, parity, -1)
                if at and stage(i, parity, 1):
                    k, h, q = at
                    sp.wait_ge(xn_done, k + 1)
                    sp.wait_ge(x2_stored[q], h * 16 + 16)
                    load_x(k + 2, q)

            for k in range(2):
                load_a_o(k, k)
                load_p(k, k)
            for n, c in (("sgu_w", sgu_w), ("sgu_b", sgu_b), ("inv_first", inv_first), ("inv_rest", inv_rest)):
                sp.dma_start(c[:], io[n]).then_inc(const_loaded, 16)
            for n, c, w in (("sgu_g", sgu_g, 256), ("pool_scale", pool_scale, 256), ("mix_g", mix_g, D), ("norm2_g", norm2_g, D)):
                sp.dma_start(c[:], io[n].to_broadcast([P, w])).then_inc(const_loaded, 16)
            sp.wait_ge(pool_w_zero, 1)
            for g in range(4):
                rows = slice(g % 2 * HD, g % 2 * HD + HD)
                sp.dma_start(pool_w[rows, g // 2, rows], io["pool_w"][g]).then_inc(const_loaded, 16)
            for n in range(2):
                sp.dma_start(wo_raw[:, 4 * n:4 * n + 4], io["w_o"][4 * n:4 * n + 4].rearrange("k c d -> c k d")).then_inc(wo_loaded[n], 16)
            for k in range(2):
                load_x(k, k)
            pipeline(sp, slot, -3, NB + 1)
            for q in range(2):
                sp.wait_ge(x2_stored[q], 16 * NB // 2)
                sp.wait_ge(h_stored[q], 32 * NB // 2)

        @block.gpsimd
        def _(pool):
            pool.memset(pool_w[:], 0.0).then_inc(pool_w_zero, 1)
            pool.memset(p_t[:, 0, :, 0:HALO], 0.0).then_inc(halo_zero, 1)
            pool.memset(minus_half[:], -0.5).then_inc(halo_zero, 1)
            pool.wait_ge(const_loaded, 16 * N_CONST)
            pool.affine_select(out=sgu_w[:], in_=sgu_w[:], compare_op=ALU.is_ge, fill=0.0, base=0,
                               pattern=[[0, 4], [1, P]], channel_multiplier=-1).then_inc(const_ready, 1)

            def add_windows(k, h, q):
                tok, p = p_t[:, q], HALO + P
                lo, hi = slice(0, HD), slice(HD, P)
                steps = [
                    (sum2[:, :, 1:p], tok[:, :, 1:p], tok[:, :, 0:p - 1]),
                    (window[lo, 0], tok[lo, 0, HALO:p], tok[lo, 0, HALO - 1:p - 1]),
                    (window[hi, 0], sum2[hi, 0, HALO:p], sum2[hi, 0, HALO - 2:p - 2]),
                    (sum4[:, 1, 3:p], sum2[:, 1, 3:p], sum2[:, 1, 1:p - 2]),
                    (window[lo, 1], sum4[lo, 1, HALO:p], sum4[lo, 1, HALO - 4:p - 4]),
                    (sum8[hi, 1, 7:p], sum4[hi, 1, 7:p], sum4[hi, 1, 3:p - 4]),
                    (window[hi, 1], sum8[hi, 1, HALO:p], sum8[hi, 1, HALO - 8:p - 8]),
                ]
                pool.wait_ge(p_loaded[q], h * 16 + 16)
                if not early(k):
                    pool.wait_ge(mean_done, k)
                for n, (out, x, y) in enumerate(steps):
                    if n:
                        pool.wait_ge(window_step, k * 7 + n)
                    pool.tensor_tensor(out, x, y, ALU.add).then_inc(window_step, 1)
                pool.wait_ge(window_step, k * 7 + 7)

            def inverse_root(stat, ready, done, k):
                w = stat.shape[-1]
                pool.wait_ge(ready, k + 1)
                pool.tensor_tensor(stat[:, 2], stat[:, 1], minus_half[:, 0:w], ALU.pow).then_inc(done, 1)

            def slot(i, parity):
                at = stage(i, parity, 2)
                if at:
                    inverse_root(v_stat, vmean_done, vstd_done, at[0])
                at = stage(i, parity, -1)
                if at:
                    inverse_root(x_stat, xmean_done, xstd_done, at[0])
                at = stage(i, parity, 3)
                if at:
                    add_windows(*at)
                at = stage(i, parity, 2)
                if at:
                    inverse_root(y_stat, ymean_done, ystd_done, at[0])
                    pool.wait_ge(yn_done, at[0] + 1)
                    pool.tensor_tensor(y_t[:, at[2]], y_t[:, at[2]], mix_g[:], ALU.mult).then_inc(yg_done, 1)

            pool.wait_ge(halo_zero, 2)
            pipeline(pool, slot, -3, NB + 1)

        @block.scalar
        def _(act):
            def slot(i, parity):
                at = stage(i, parity, 2)
                if at:
                    act.wait_ge(gelu_turned_done, at[0] + 1)
                    act.activation(v_sq[:], gelu_turned[:, 256:512], ACT.Square).then_inc(vsq_done, 1)
                at = stage(i, parity, -2)
                if at:
                    k, h, q = at
                    for n in range(2):
                        act.wait_ge(hT_turned, k * 2 + n + 1)
                        if n == 0 and not early(k, 2):
                            act.wait_ge(h_stored[q], h * 32)
                        act.activation(h_out[:, q, 0, 4 * n:4 * n + 4].bitcast(F32R),
                                       turned[:, n].rearrange("p (k t) -> p k t", k=4), ACT.Copy).then_inc(hT_high, 1)
                at = stage(i, parity, 2)
                if at:
                    k, h, q = at
                    act.wait_ge(yb_done, k + 1)
                    if not early(k, 2):
                        act.wait_ge(yT_turned, k * 2 - 2)
                    act.activation(y_t[:, q, 256:768], y_b[:], ACT.Copy).then_inc(yb_copied, 1)
                at = stage(i, parity, -1)
                if at:
                    k, h, q = at
                    act.wait_ge(x2_done, k * 2 + 2)
                    if not early(k):
                        act.wait_ge(hT_turned, k * 2)
                    act.activation(xn[:], x_t[:, q], ACT.Square, accum_out=x_stat[:, 0]).then_inc(xsq_done, 1)
                at = stage(i, parity, 3)
                if at:
                    k, h, q = at
                    act.wait_ge(a_loaded[q], h * 16 + 16)
                    act.activation(a_t[:, q], a_t[:, q], ACT.Gelu).then_inc(gelu_done, 1)
                at = stage(i, parity, 1)
                if at:
                    k, h, q = at
                    for n in range(2):
                        act.wait_ge(yT_turned, k * 2 + n + 1)
                        if n == 0 and not early(k, 2):
                            act.wait_ge(proj_done, k * 2 - 2)
                        act.activation(yT_hi[:, q, 4 * n:4 * n + 4], turned[:, n].rearrange("p (k t) -> p k t", k=4),
                                       ACT.Copy).then_inc(yT_high, 1)
                at = stage(i, parity, 2)
                if at:
                    act.wait_ge(y_done, at[0] + 1)
                    act.activation(y_sq, y_t[:, at[2]], ACT.Square).then_inc(ysq_done, 1)
                if isinstance(i, int) and (i, parity) in WO_SHARE:
                    for k in WO_SHARE[i, parity]:
                        act.wait_ge(wo_loaded[k // 4], 16)
                        act.activation(wo_hi[:, k], wo_raw[:, k], ACT.Copy).then_inc(wo_high, 1)

            pipeline(act, slot, -3, NB + 1)

        @block.vector
        def _(dve):
            dve.tensor_copy(two_ident[0:HD], ident[0:HD, 0:HD]).then_inc(const_ready, 1)
            dve.tensor_copy(two_ident[HD:P], ident[HD:P, HD:P]).then_inc(const_ready, 1)
            dve.wait_ge(const_loaded, 16 * N_CONST)

            def mean_plus_eps(stat, n, done):
                dve.tensor_scalar(stat[:, 1], stat[:, 0], 1.0 / n, EPS, ALU.mult, ALU.add).then_inc(done, 1)

            def per_head(ap, n):
                return ap.rearrange("t (h e) -> t h e", h=n)

            def spread(ap, n):
                return ap.unsqueeze(2).to_broadcast([P, n, HD])

            def add_residual(k, h, q, n):
                cols = slice(n * TW, (n + 1) * TW)
                dve.wait_ge(proj_done, k * 2 + n + 1)
                if n == 0:
                    dve.wait_ge(x_loaded[q], h * 16 + 16)
                dve.tensor_tensor(x_t[:, q, cols], proj[:, n], x_t[:, q, cols], ALU.add).then_inc(x2_done, 1)

            def slot(i, parity):
                second_norm, heads = stage(i, parity, -1), stage(i, parity, 2)
                if second_norm:
                    add_residual(*second_norm, 1)
                at = stage(i, parity, -2)
                if at:
                    k, h, q = at
                    for n in range(2):
                        dve.wait_ge(hT_high, k * 2 + n + 1)
                        dve.tensor_tensor(h_out[:, q, 1, 4 * n:4 * n + 4].bitcast(F32R), turned[:, n].rearrange("p (k t) -> p k t", k=4),
                                          h_out[:, q, 0, 4 * n:4 * n + 4], ALU.subtract).then_inc(hT_split, 1)
                if heads:
                    k, h, q = heads
                    dve.wait_ge(vsq_done, k + 1)
                    dve.tensor_reduce(v_stat[:, 0], per_head(v_sq[:], 4), AX_X, ALU.add).then_inc(vsum_done, 1)
                    dve.wait_ge(vsum_done, k + 1)
                    mean_plus_eps(v_stat, HD, vmean_done)
                    dve.wait_ge(window_step, k * 7 + 7)
                    dve.tensor_tensor(mean[:], window[:], (inv_first if early(k) else inv_rest)[:], ALU.mult).then_inc(mean_done, 1)
                    dve.wait_ge(mean_done, k + 1)
                    if not early(k):
                        dve.wait_ge(small_done, k)
                    dve.tensor_tensor(pooled[:], mean[:], p_t[:, q, :, HALO:HALO + P], ALU.subtract).then_inc(pooled_done, 1)
                    dve.wait_ge(vstd_done, k + 1)
                    dve.tensor_tensor(per_head(v_n[:], 4), per_head(gelu_turned[:, 256:512], 4), spread(v_stat[:, 2], 4), ALU.mult).then_inc(vn_done, 1)
                if second_norm:
                    dve.wait_ge(xsq_done, second_norm[0] + 1)
                    mean_plus_eps(x_stat, D, xmean_done)
                if heads:
                    dve.wait_ge(vn_done, k + 1)
                    dve.tensor_tensor(v_g[:], v_n[:], sgu_g[:], ALU.mult).then_inc(vg_done, 1)
                if second_norm:
                    k, h, q = second_norm
                    dve.wait_ge(xstd_done, k + 1)
                    dve.scalar_tensor_tensor(out=xn[:], in0=x_t[:, q], scalar=x_stat[:, 2], in1=norm2_g[:],
                                             op0=ALU.mult, op1=ALU.mult).then_inc(xn_done, 1)
                at = stage(i, parity, 0)
                if at:
                    add_residual(*at, 0)
                at = stage(i, parity, 1)
                if at:
                    k, h, q = at
                    for n in range(2):
                        dve.wait_ge(yT_high, k * 2 + n + 1)
                        dve.tensor_tensor(yT_lo[:, q, 4 * n:4 * n + 4], turned[:, n].rearrange("p (k t) -> p k t", k=4),
                                          yT_hi[:, q, 4 * n:4 * n + 4].bitcast(F32), ALU.subtract).then_inc(yT_split, 1)
                if heads:
                    k, h, q = heads
                    dve.wait_ge(small_done, k + 1)
                    dve.tensor_tensor(per_head(s_b[:], 4), per_head(small[:, 0:256], 4), spread(sgu_b[:], 4), ALU.add).then_inc(sb_done, 1)
                    dve.tensor_tensor(y_t[:, q, 768:1024], small[:, 256:512], pool_scale[:], ALU.mult)
                    dve.wait_ge(sb_done, k + 1)
                    dve.wait_ge(yb_copied, k + 1)
                    dve.tensor_tensor(y_t[:, q, 0:256], s_b[:], gelu_turned[:, 0:256], ALU.mult).then_inc(y_done, 1)
                    dve.wait_ge(ysq_done, k + 1)
                    dve.tensor_reduce(y_stat[:, 0], per_head(y_sq, NHT), AX_X, ALU.add).then_inc(ysum_done, 1)
                    dve.wait_ge(ysum_done, k + 1)
                    mean_plus_eps(y_stat, HD, ymean_done)
                    dve.wait_ge(ystd_done, k + 1)
                    dve.tensor_tensor(per_head(y_t[:, q], NHT), per_head(y_t[:, q], NHT), spread(y_stat[:, 2], NHT), ALU.mult).then_inc(yn_done, 1)
                if isinstance(i, int) and (i, parity) in WO_SHARE:
                    for k in WO_SHARE[i, parity]:
                        dve.wait_ge(wo_high, k + 1)
                        dve.tensor_tensor(wo_lo[:, k], wo_raw[:, k], wo_hi[:, k].bitcast(F32), ALU.subtract).then_inc(wo_split, 1)

            pipeline(dve, slot, -3, NB + 1)

        @block.tensor
        def _(pe):
            def project(k, q, n):
                if n == 0:
                    if early(k):
                        pe.wait_ge(wo_split, KD)
                    pe.wait_ge(yT_split, k * 2 + 2)
                if not early(k):
                    pe.wait_ge(x2_done, k * 2 + (n - 1))
                cols = slice(n * TW, (n + 1) * TW)
                split_products(pe, proj[:, n], [(yT_hi[:, q, c], yT_lo[:, q, c], wo_hi[:, c, cols], wo_lo[:, c, cols])
                                                for c in range(KD)]).then_inc(proj_done, 1)

            def turn(src, done):
                for n in range(2):
                    for j in range(4):
                        c = 4 * n + j
                        mm = pe.transpose(turned[:, n, j * P:(j + 1) * P], src[:, c * P:(c + 1) * P], ident[:])
                    mm.then_inc(done, 1)

            def slot(i, parity):
                at = stage(i, parity, 0)
                if at:
                    project(at[0], at[2], 0)
                at = stage(i, parity, 1)
                if at:
                    k, h, q = at
                    pe.wait_ge(yg_done, k + 1)
                    if not early(k, 3):
                        pe.wait_ge(hT_split, k * 2 - 4)
                    turn(y_t[:, q], yT_turned)
                at = stage(i, parity, 2)
                if at:
                    k, h, q = at
                    pe.wait_ge(vg_done, k + 1)
                    pe.wait_ge(pooled_done, k + 1)
                    if not early(k):
                        pe.wait_ge(y_done, k)
                    for j in range(4):
                        pe.matmul(small[:, j * HD:(j + 1) * HD], sgu_w[:, j], v_g[:, j * HD:(j + 1) * HD], start=True, stop=True)
                    for j in range(2):
                        mm = pe.matmul(small[:, 256 + j * P:256 + (j + 1) * P], pooled[:, j], pool_w[:, j], start=True, stop=True)
                    mm.then_inc(small_done, 1)
                at = stage(i, parity, 0)
                if at:
                    project(at[0], at[2], 1)
                at = stage(i, parity, 3)
                if at:
                    k, h, q = at
                    pe.wait_ge(gelu_done, k + 1)
                    if not early(k):
                        pe.wait_ge(y_done, k)
                    for j in range(4):
                        mm = pe.transpose(gelu_turned[:, j * P:(j + 1) * P], a_t[:, q, j], ident[:])
                    mm.then_inc(gelu_turned_done, 1)
                    pe.wait_ge(o_loaded[q], h * 16 + 16)
                    if not early(k):
                        pe.wait_ge(yb_copied, k)
                    for j in range(NHB):
                        mm = pe.matmul(y_b[:, j * HD:(j + 1) * HD], o_t[:, q, j], two_ident[:], start=True, stop=True)
                    mm.then_inc(yb_done, 1)
                at = stage(i, parity, -1)
                if at:
                    k = at[0]
                    pe.wait_ge(xn_done, k + 1)
                    if stage(i, parity, 1):
                        pe.wait_ge(yT_split, k * 2 + 6)
                    else:
                        pe.wait_ge(hT_split, k * 2)
                    turn(xn[:], hT_turned)

            pe.wait_ge(const_ready, 3)
            pipeline(pe, slot, -3, NB + 1)


def ffn_up(nc, io, mem):
    with ExitStack() as ctx:
        def sb(name, shape, dt=F32):
            return ctx.enter_context(nc.sbuf_tensor("up_" + name, shape, dt))

        def sem(name):
            return ctx.enter_context(nc.semaphore("up_" + name))

        first_tile = mem["first_tile"]
        h_hi, h_lo = sb("h_hi", [P, KD, S - TW], F32R), sb("h_lo", [P, KD, S - TW], F32R)
        w_raw = mem["w_raw"][:].rearrange("c n (k m) -> c n k m", k=KD)
        w_hi, w_lo = sb("w_hi", [P, 2, KD, P], F32R), sb("w_lo", [P, 2, KD, P], F32R)
        conv = sb("conv", [P, NF, 2, 4])
        z_c = sb("z_c", [P, 2, S])
        gated = mem["gated"]
        z = [ctx.enter_context(nc.psum_tensor(f"up_z{i}", [P, S], F32)) for i in range(2)]

        h_loaded = [sem(f"h_loaded{T}") for T in range(NT)]
        conv_loaded = sem("conv_loaded")
        w_loaded, first_loaded, gated_stored = mem["w_loaded"], mem["first_loaded"], mem["gated_stored"]
        w_high, w_split = sem("w_high"), sem("w_split")
        z_done = [sem("z_done0"), sem("z_done1")]
        tap2_done, tap1_done, conv_done = sem("tap2_done"), sem("tap1_done"), sem("conv_done")
        silu_done, gated_done = sem("silu_done"), sem("gated_done")

        LAST = NF - 1

        def tile_cols(T, back=0):
            return slice(max(back, T * TW), (T + 1) * TW)

        block = ctx.enter_context(nc.Block())

        @block.sync
        def _(sp):
            def load_w(c):
                for half in range(2):
                    sp.dma_start(w_raw[:, half], io["w_up"][bass.ds(c, 1), half].rearrange("n c k m -> c (n k) m")).then_inc(w_loaded[half], 16)

            sp.dma_start(conv[:], io["conv"]).then_inc(conv_loaded, 16)
            for T in range(1, NT):
                for a, h in enumerate((h_hi, h_lo)):
                    own, src = slice((T - 1) * TW, T * TW), slice(T * TW, (T + 1) * TW)
                    sp.dma_start(h[:, :, own].bitcast(F32), io["h2_hbm"][a, :, :, src].rearrange("k c t -> c k t")).then_inc(h_loaded[T], 16)
            with sp.Fori(0, LAST) as c:
                sp.wait_ge(w_split, c * 2 + 2)
                load_w(c + 1)
                sp.wait_ge(gated_done, c + 1)
                sp.dma_start(io["gated_hbm"][bass.ds(c, 1)].rearrange("n f t -> f (n t)"), gated[:]).then_inc(gated_stored, 16)
            sp.wait_ge(w_split, NF * 2)
            sp.wait_ge(gated_stored, 16 * 2)
            for f in range(2):
                sp.dma_start(mem["g_raw"][:, f], io["gated_hbm"][f, :, 0:TW]).then_inc(mem["g_loaded"][f], 16)
                sp.dma_start(mem["w_raw"][:, f], io["w_down"][f]).then_inc(mem["down_loaded"][f], 16)
            sp.wait_ge(gated_stored, 16 * LAST)
            for T in range(NT):
                sp.wait_ge(gated_done, LAST + T + 1)
                sp.dma_start(io["gated_hbm"][LAST, :, tile_cols(T)], gated[:, tile_cols(T)]).then_inc(gated_stored, 16)

        @block.gpsimd
        def _(pool):
            def split(c, half):
                pool.wait_ge(w_high, c * 2 + half + 1)
                pool.tensor_tensor(w_lo[:, half], w_raw[:, half], w_hi[:, half].bitcast(F32), ALU.subtract).then_inc(w_split, 1)

            def gate(c):
                pool.wait_ge(silu_done, c + 1)
                pool.wait_ge(conv_done, c * 2 + 2)
                if not isinstance(c, int) or c > 0:
                    pool.wait_ge(gated_stored, c * 16)
                pool.tensor_tensor(gated[:], z_c[:, 0], z_c[:, 1], ALU.mult).then_inc(gated_done, 1)

            split(0, 0)
            split(0, 1)
            def chunk(c):
                split(c + 1, 0)
                split(c + 1, 1)
                gate(c)

            chunk(0)
            with pool.Fori(1, LAST) as c:
                chunk(c)
            pool.wait_ge(gated_stored, LAST * 16)
            for T in range(NT):
                pool.wait_ge(silu_done, LAST + T + 1)
                pool.wait_ge(conv_done, LAST * 2 + NT + T + 1)
                pool.tensor_tensor(gated[:, tile_cols(T)], z_c[:, 0, tile_cols(T)], z_c[:, 1, tile_cols(T)], ALU.mult).then_inc(gated_done, 1)

        @block.scalar
        def _(act):
            def high(c, half):
                act.wait_ge(w_loaded[half], c * 16 + 16)
                act.activation(w_hi[:, half], w_raw[:, half], ACT.Copy).then_inc(w_high, 1)

            def per_channel(c, half, n):
                return conv[:, bass.ds(c, 1), half, n:n + 1].rearrange("p a b -> p (a b)")

            def last_tap(c, half):
                act.wait_ge(z_done[half], c * NT + NT)
                if not isinstance(c, int) or c > 0:
                    act.wait_ge(gated_done, c)
                act.activation(z_c[:, half], z[half][:], ACT.Identity, bias=per_channel(c, half, 3),
                               scale=per_channel(c, half, 2)).then_inc(tap2_done, 1)

            def silu(c):
                act.wait_ge(conv_done, c * 2 + 1)
                act.activation(z_c[:, 0], z_c[:, 0], ACT.Silu).then_inc(silu_done, 1)

            high(0, 0)
            high(0, 1)
            act.wait_ge(conv_loaded, 16)

            def chunk(c):
                last_tap(c, 0)
                high(c + 1, 0)
                silu(c)
                last_tap(c, 1)
                high(c + 1, 1)

            chunk(0)
            with act.Fori(1, LAST) as c:
                chunk(c)
            act.wait_ge(gated_done, LAST)
            for half in range(2):
                for T in range(NT):
                    act.wait_ge(z_done[half], LAST * NT + T + 1)
                    act.activation(z_c[:, half, tile_cols(T)], z[half][:, tile_cols(T)], ACT.Identity, bias=per_channel(LAST, half, 3),
                                   scale=per_channel(LAST, half, 2)).then_inc(tap2_done, 1)
                    if half == 0:
                        act.wait_ge(conv_done, LAST * 2 + T + 1)
                        act.activation(z_c[:, 0, tile_cols(T)], z_c[:, 0, tile_cols(T)], ACT.Silu).then_inc(silu_done, 1)

        @block.vector
        def _(dve):
            def taps(c, half, n, cols):
                for tap, done, ready in ((1, tap1_done, tap2_done), (0, conv_done, tap1_done)):
                    back = 2 - tap
                    out = cols(back)
                    dve.wait_ge(ready, n + 1)
                    dve.scalar_tensor_tensor(out=z_c[:, half, out], in0=z[half][:, out.start - back:out.stop - back],
                                             scalar=conv[:, bass.ds(c, 1), half, tap:tap + 1].rearrange("p a b -> p (a b)"),
                                             in1=z_c[:, half, out], op0=ALU.mult, op1=ALU.add).then_inc(done, 1)

            dve.wait_ge(conv_loaded, 16)
            with dve.Fori(0, LAST) as c:
                for half in range(2):
                    taps(c, half, c * 2 + half, lambda back: slice(back, S))
            for half in range(2):
                for T in range(NT):
                    taps(LAST, half, LAST * 2 + half * NT + T, lambda back: tile_cols(T, back))

        @block.tensor
        def _(pe):
            def product(half, T):
                cols = slice(T * TW, (T + 1) * TW)
                if T == 0:
                    moving = [(first_tile[:, 0, k], first_tile[:, 1, k]) for k in range(KD)]
                else:
                    own = slice((T - 1) * TW, T * TW)
                    moving = [(h_hi[:, k, own], h_lo[:, k, own]) for k in range(KD)]
                split_products(pe, z[half][:, cols], [(w_hi[:, half, k], w_lo[:, half, k], *moving[k])
                                                      for k in range(KD)]).then_inc(z_done[half], 1)

            for part in first_loaded:
                pe.wait_ge(part, 32)
            for T in range(NT):
                for half in range(2):
                    if T == 0:
                        pe.wait_ge(w_split, half + 1)
                    elif half == 0:
                        pe.wait_ge(h_loaded[T], 32)
                    product(half, T)
            with pe.Fori(1, NF) as c:
                for half in range(2):
                    pe.wait_ge(w_split, c * 2 + half + 1)
                    pe.wait_ge(conv_done, c * 2 + half - 1)
                    for T in range(NT):
                        product(half, T)


def ffn_down(nc, io, mem):
    with ExitStack() as ctx:
        def sb(name, shape, dt=F32):
            return ctx.enter_context(nc.sbuf_tensor("dn_" + name, shape, dt))

        def sem(name):
            return ctx.enter_context(nc.semaphore("dn_" + name))

        def sem2(name):
            return [sem(name + "0"), sem(name + "1")]

        w_first, w_rest = mem["w_raw"], sb("w_rest", [P, NF - 2, D])
        w_hi, w_lo = sb("w_hi", [P, 2, D], F32R), sb("w_lo", [P, 2, D], F32R)
        g_raw = mem["g_raw"]
        g_hi, g_lo = sb("g_hi", [P, 2, TW], F32R), sb("g_lo", [P, 2, TW], F32R)
        x_t = sb("x_t", [P, BPT, D])
        squares = sb("squares", [P, BPT, D])
        stat = sb("stat", [P, 3, BPT])
        minus_half = sb("minus_half", [P, BPT])
        final_g = sb("final_g", [P, D])
        acc = [ctx.enter_context(nc.psum_tensor(f"dn_acc{j}", [P, D], F32)) for j in range(BPT)]

        w_loaded, g_loaded, gated_stored = mem["down_loaded"], mem["g_loaded"], mem["gated_stored"]
        x_loaded, out_stored = sem("x_loaded"), sem("out_stored")
        gain_loaded, half_set = sem("gain_loaded"), sem("half_set")
        high_done, split_done, used = sem("high_done"), sem("split_done"), sem("used")
        acc_done, x3_done, sq_done, mean_done, std_done, out_done = (sem(n) for n in ("acc_done", "x3_done", "sq_done", "mean_done", "std_done", "out_done"))

        block = ctx.enter_context(nc.Block())

        HEAD = 4

        def w_chunk(f):
            if isinstance(f, int) and f < 2:
                return w_first[:, f]
            return w_rest[:, bass.ds(f - 2, 1)].rearrange("f n d -> f (n d)")

        def steps(engine, step, between=None):
            def tile(T):
                for f in range(HEAD):
                    step(T, f, f % 2)
                    if between:
                        between(T, f)
                with engine.Fori(HEAD // 2, NF // 2) as j:
                    step(T, j * 2, 0)
                    step(T, j * 2 + 1, 1)

            tile(0)
            with engine.Fori(1, NT) as T:
                tile(T)

        @block.sync
        def _(sp):
            def load_w(f, q):
                sp.dma_start(w_chunk(f), io["w_down"][bass.ds(f, 1)].rearrange("n f d -> f (n d)")).then_inc(w_loaded[q], 16)

            def load_g(T, f, q):
                sp.dma_start(g_raw[:, q], io["gated_hbm"][bass.ds(f, 1), :, bass.ds(T * TW, TW)].rearrange("n f t -> f (n t)")).then_inc(g_loaded[q], 16)

            sp.dma_start(final_g[:], io["final_g"].to_broadcast([P, D])).then_inc(gain_loaded, 16)
            for q in range(2):
                sp.wait_ge(w_loaded[q], 16)
                load_w(2 + q, q)
            with sp.Fori(1, NF // 2 - 1) as j:
                for q in range(2):
                    sp.wait_ge(split_done, j * 4 + (2 * q - 2))
                    load_g(0, j * 2 + q, q)
                    sp.wait_ge(w_loaded[q], j * 16 + 16)
                    load_w(j * 2 + (q + 2), q)
            for q in range(2):
                sp.wait_ge(split_done, NF * 2 + 2 * q - 6)
                if q == 1:
                    sp.wait_ge(gated_stored, 16 * (NF - 1 + NT))
                load_g(0, NF - 2 + q, q)
            with sp.Fori(1, NT) as T:
                with sp.Fori(0, NF // 2) as j:
                    for q in range(2):
                        sp.wait_ge(split_done, T * (2 * NF) + j * 4 + (2 * q - 2))
                        load_g(T, j * 2 + q, q)

        @block.gpsimd
        def _(pool):
            def x_rows(name, T):
                return io[name][bass.ds(T * TW, TW), :].rearrange("(j t) d -> t j d", t=P)

            pool.memset(minus_half[:], -0.5).then_inc(half_set, 1)
            pool.wait_ge(half_set, 1)
            pool.dma_start(x_t[:], x_rows("x2_hbm", 0)).then_inc(x_loaded, 16)

            def finish(T):
                for j in range(BPT):
                    pool.wait_ge(mean_done, T * BPT + j + 1)
                    pool.tensor_tensor(stat[:, 2, j:j + 1], stat[:, 1, j:j + 1], minus_half[:, j:j + 1], ALU.pow).then_inc(std_done, 1)
                pool.wait_ge(out_done, T * BPT + BPT)
                pool.dma_start(x_rows("out", T), x_t[:]).then_inc(out_stored, 16)

            with pool.Fori(0, NT - 1) as T:
                finish(T)
                pool.wait_ge(out_stored, T * 16 + 16)
                pool.dma_start(x_t[:], x_rows("x2_hbm", T + 1)).then_inc(x_loaded, 16)
            finish(NT - 1)
            pool.wait_ge(out_stored, 16 * NT)

        @block.scalar
        def _(act):
            def step(T, f, q):
                if isinstance(T, int):
                    act.wait_ge(w_loaded[q], f * 8 + (16 - 8 * q))
                act.wait_ge(g_loaded[q], T * (NF // 2 * 16) + f * 8 + (16 - 8 * q))
                if not isinstance(f, int):
                    act.wait_ge(used, T * (NF - 1) + f - 1)
                elif f >= 2:
                    act.wait_ge(used, T * (NF - 1) + (f - 1))
                elif not isinstance(T, int):
                    if f == 1:
                        act.wait_ge(acc_done, T * BPT)
                    else:
                        act.wait_ge(used, T * (NF - 1))
                act.activation(g_hi[:, q], g_raw[:, q], ACT.Copy).then_inc(high_done, 1)
                act.activation(w_hi[:, q], w_chunk(f), ACT.Copy).then_inc(high_done, 1)

            def squared(T):
                for j in range(BPT):
                    act.wait_ge(x3_done, T * BPT + j + 1)
                    act.activation(squares[:, j], x_t[:, j], ACT.Square, accum_out=stat[:, 0, j:j + 1]).then_inc(sq_done, 1)

            def between(T, f):
                if not isinstance(T, int) and f == 1:
                    squared(T - 1)

            steps(act, step, between)
            squared(NT - 1)

        @block.vector
        def _(dve):
            dve.wait_ge(gain_loaded, 16)

            def step(T, f, q):
                n = T * (2 * NF) + f * 2
                dve.wait_ge(high_done, n + 1)
                dve.tensor_tensor(g_lo[:, q], g_raw[:, q], g_hi[:, q].bitcast(F32), ALU.subtract).then_inc(split_done, 1)
                dve.wait_ge(high_done, n + 2)
                dve.tensor_tensor(w_lo[:, q], w_chunk(f), w_hi[:, q].bitcast(F32),
                                  ALU.subtract).then_inc(split_done, 1)

            def add_residual(T):
                dve.wait_ge(x_loaded, T * 16 + 16)
                for j in range(BPT):
                    dve.wait_ge(acc_done, T * BPT + j + 1)
                    dve.tensor_tensor(x_t[:, j], acc[j][:], x_t[:, j], ALU.add).then_inc(x3_done, 1)

            def normalise(T):
                for j in range(BPT):
                    dve.wait_ge(sq_done, T * BPT + j + 1)
                    dve.tensor_scalar(stat[:, 1, j:j + 1], stat[:, 0, j:j + 1], 1.0 / D, EPS, ALU.mult, ALU.add).then_inc(mean_done, 1)
                for j in range(BPT):
                    dve.wait_ge(std_done, T * BPT + j + 1)
                    dve.scalar_tensor_tensor(out=x_t[:, j], in0=x_t[:, j], scalar=stat[:, 2, j:j + 1], in1=final_g[:],
                                             op0=ALU.mult, op1=ALU.mult).then_inc(out_done, 1)

            def between(T, f):
                if not isinstance(T, int):
                    if f == 0:
                        add_residual(T - 1)
                    if f == 2:
                        normalise(T - 1)

            steps(dve, step, between)
            add_residual(NT - 1)
            normalise(NT - 1)

        @block.tensor
        def _(pe):
            def step(T, n, q, start, stop):
                pe.wait_ge(split_done, n * 2 + 2)
                for j in range(BPT):
                    if start and not isinstance(T, int):
                        pe.wait_ge(x3_done, T * BPT - BPT + j + 1)
                    t = slice(j * P, (j + 1) * P)
                    for half in range(2):
                        cols = slice(half * TW, (half + 1) * TW)
                        mm = split_products(pe, acc[j][:, cols], [(g_hi[:, q, t], g_lo[:, q, t], w_hi[:, q, cols], w_lo[:, q, cols])],
                                            first=start, last=stop)
                    if stop:
                        mm.then_inc(acc_done, 1)
                if not stop:
                    mm.then_inc(used, 1)

            def tile(T):
                step(T, T * NF, 0, True, False)
                step(T, T * NF + 1, 1, False, False)
                with pe.Fori(1, NF // 2 - 1) as i:
                    step(T, T * NF + i * 2, 0, False, False)
                    step(T, T * NF + i * 2 + 1, 1, False, False)
                step(T, T * NF + NF - 2, 0, False, False)
                step(T, T * NF + NF - 1, 1, False, True)

            tile(0)
            with pe.Fori(1, NT) as T:
                tile(T)


def build(nc, io, upto=5):
    def hbm(name, shape):
        io[name] = nc.dram_tensor(name, shape, F32, kind="Internal").ap()

    hbm("q_hbm", (2, NHB * HD, S))
    hbm("k_hbm", (2, NHB * HD, S))
    hbm("v_hbm", (NHB, NT, P, BPT, 2 * HD))
    hbm("ap_hbm", (6, P, S))
    hbm("o_hbm", (NHB, P, S))
    hbm("x2_hbm", (S, D))
    hbm("h2_hbm", (2, KD, P, S))
    hbm("gated_hbm", (NF, P, S))
    with ExitStack() as ctx:
        mem = {"ident": ctx.enter_context(nc.sbuf_tensor("ident", [P, P], F32))}
        with ExitStack() as front:
            for n in ("hT_hi", "hT_lo"):
                mem[n] = front.enter_context(nc.sbuf_tensor(n, [P, KD, S], F32R))
            project_norm(nc, io, mem)
            if upto >= 2:
                attend(nc, io, mem)
        def sem(name):
            return ctx.enter_context(nc.semaphore(name))

        with nc.sbuf_tensor("wo_raw", [P, KD, D], F32) as mem["wo_raw"]:
            pass
        for n, shape, dt in (("first_tile", [P, 2, KD, TW], F32R), ("w_raw", [P, 2, D], F32), ("g_raw", [P, 2, TW], F32), ("gated", [P, S], F32)):
            mem[n] = ctx.enter_context(nc.sbuf_tensor(n, shape, dt))
        mem["w_loaded"] = [sem("w_up_loaded0"), sem("w_up_loaded1")]
        mem["first_loaded"] = [sem(f"first_loaded{n}") for n in range(FIRST_PIECES)]
        mem["gated_stored"] = sem("gated_stored")
        mem["down_loaded"], mem["g_loaded"] = ([sem(n + "0"), sem(n + "1")] for n in ("down_loaded", "g_loaded"))
        if upto >= 3:
            mix(nc, io, mem)
        if upto >= 4:
            ffn_up(nc, io, mem)
        if upto >= 5:
            ffn_down(nc, io, mem)


def laid_out(inputs):
    import numpy as np

    a = {n: np.asarray(v) for n, v in inputs.items()}
    w_in = a["w_in"][0]
    wa, wq, wk, wv, wp = np.split(w_in, [512, 1024, 1536, 2048], axis=1)
    w_cm = np.concatenate([wa, wq, wk, wp], axis=1).reshape(KD, P, 14, P)
    conv = np.concatenate([a["conv_w"][0], a["conv_b"]], axis=0)
    width = np.repeat(np.array(POOL_WINDOWS, np.float32), HD).reshape(2, P).T[:, :, None]
    inv_first = (1.0 / np.minimum(np.arange(1, P + 1, dtype=np.float32), width)).astype(np.float32)
    inv_rest = np.broadcast_to(1.0 / width, (P, 2, P)).astype(np.float32)
    return {
        "x": a["x"][0],
        "norm1_g": a["norm1_g"],
        "w_chunks": w_cm.transpose(2, 1, 0, 3)[CHUNK_ORDER],
        "w_v": wv.reshape(KD, P, 512),
        "sgu_g": a["sgu_norm_g"],
        "sgu_w": a["sgu_w"][0].transpose(2, 0, 1),
        "sgu_b": a["sgu_b"][0].transpose(1, 0),
        "pool_w": a["pool_w"][0],
        "pool_scale": a["pool_scale"],
        "inv_first": inv_first,
        "inv_rest": inv_rest,
        "mix_g": a["mix_norm_g"],
        "w_o": a["w_o"][0].reshape(KD, P, D),
        "norm2_g": a["norm2_g"],
        "w_up": a["w_up"][0].reshape(KD, P, 2, NF, P).transpose(3, 2, 1, 0, 4),
        "conv": conv.reshape(4, 2, NF, P).transpose(3, 2, 1, 0),
        "w_down": a["w_down"][0].reshape(NF, P, D),
        "final_g": a["final_g"][None, :],
    }


def kernel(**inputs):
    import numpy as np
    import concourse.bacc as bacc
    from concourse.bass_utils import run_bass_kernel_spmd

    nc = bacc.Bacc("TRN2", target_bir_lowering=False, num_devices=1)
    arrays = {n: np.ascontiguousarray(v) for n, v in laid_out(inputs).items()}
    io = {n: nc.dram_tensor(f"in_{n}", v.shape, F32, kind="ExternalInput").ap() for n, v in arrays.items()}
    io["out"] = nc.dram_tensor("out", (S, D), F32, kind="ExternalOutput").ap()
    build(nc, io)
    r = run_bass_kernel_spmd(nc, [{f"in_{n}": v for n, v in arrays.items()}], core_ids=[0])
    return r.results[0]["out"].reshape(1, S, D)
```

```python
from contextlib import ExitStack

import concourse.bass as bass
from concourse import mybir

F32 = mybir.dt.float32
F32R = mybir.dt.float32r
BF16 = mybir.dt.bfloat16
ACT = mybir.ActivationFunctionType
ALU = mybir.AluOpType
AX_X = mybir.AxisListType.X

P = 128
S, D = 2048, 1024
KD = D // P
HD, NHB = 64, 8
NHT = 16
NB = S // P
TW = 512
NT = S // TW
BPT = TW // P
DFF = 2816
NF = DFF // P
EPS = 1e-6
FIRST_PIECES = 2
BIG = 1e30
QSCALE = HD ** -0.5

CHUNK_ORDER = [4, 8, 5, 9, 0, 6, 10, 1, 7, 11, 2, 3, 12, 13]


def attention_slots():
    return [(T, c, i, (i + 1) * P if c == T else TW) for T in range(NT) for c in range(T, -1, -1) for i in range(BPT)]


def split_products(pe, out, parts, first=True, last=True):
    n = len(parts)
    for i, (sh, sl, mh, ml) in enumerate(parts):
        pe.matmul(out, sh, mh, start=first and i == 0, stop=False)
        pe.matmul(out, sh, ml, start=False, stop=False)
        mm = pe.matmul(out, sl, mh, start=False, stop=last and i == n - 1)
    return mm


def project_norm(nc, io, mem):
    hT_hi, hT_lo, ident = mem["hT_hi"], mem["hT_lo"], mem["ident"]
    q_chunk, k_chunk = 0, 1
    with ExitStack() as ctx:
        def sb(name, shape, dt=F32):
            return ctx.enter_context(nc.sbuf_tensor("pn_" + name, shape, dt))

        def sem(name):
            return ctx.enter_context(nc.semaphore("pn_" + name))

        WV_RING = 3
        x_in, xn = mem["x_in"], mem["xn"]
        gain = sb("gain", [P, D])
        sumsq = sb("sumsq", [P, NB])
        meansq = sb("meansq", [P, NB])
        minus_half = sb("minus_half", [P, NB])
        rstd = sb("rstd", [P, NB])
        wv_raw = sb("wv_raw", [P, WV_RING, 512])
        wv_hi = sb("wv_hi", [P, KD, 512], F32R)
        wv_lo = sb("wv_lo", [P, KD, 512], F32R)
        wc_raw = mem["w_raw"]
        wc_hi = sb("wc_hi", [P, KD, P], F32R)
        wc_lo = sb("wc_lo", [P, KD, P], F32R)
        chunk_hi, chunk_lo = ([own[:], old[:, 0:2].rearrange("p a (b c) -> p (a b) c", c=P)]
                              for own, old in ((wc_hi, wv_hi), (wc_lo, wv_lo)))
        staged = sb("staged", [P, 2, 2 * TW])
        v_out = [staged[:, n].rearrange("s (h a e) -> s h a e", h=NHB, a=2) for n in range(2)]
        qk_out = [staged[:, n].rearrange("c (a t) -> c a t", a=2) for n in range(2)]
        turned = [ctx.enter_context(nc.psum_tensor(f"pn_turned{i}", [P, TW], F32)) for i in range(4)]
        prod = [ctx.enter_context(nc.psum_tensor(f"pn_prod{i}", [P, TW], F32)) for i in range(2)]

        x_loaded = [sem("x_loaded0"), sem("x_loaded1")]
        gain_loaded = sem("gain_loaded")
        wv_loaded = [sem(f"wv_loaded{i}") for i in range(WV_RING)]
        wc_loaded = sem("wc_loaded")
        wv_high, wv_split, wc_high, wc_split = sem("wv_high"), sem("wv_split"), sem("wc_high"), sem("wc_split")
        ident_zero, ident_ready = sem("ident_zero"), sem("ident_ready")
        sumsq_done, meansq_done, rstd_done = sem("sumsq_done"), sem("meansq_done"), sem("rstd_done")
        xn_done = sem("xn_done")
        turned_done, turned_high, turned_split = sem("turned_done"), sem("turned_high"), sem("turned_split")
        prod_done, prod_high, prod_split = sem("prod_done"), sem("prod_high"), sem("prod_split")
        stored = [sem("stored0"), sem("stored1")]
        NQK = 2 * NT

        block = ctx.enter_context(nc.Block())

        @block.sync
        def _(sp):
            def load_x(b):
                if b >= 2:
                    sp.wait_ge(xn_done, b - 1)
                sp.dma_start(x_in[:, b % 2], io["x"][b * P:(b + 1) * P, :]).then_inc(x_loaded[b % 2], 16)

            load_x(0)
            sp.dma_start(gain[:], io["norm1_g"].to_broadcast([P, D])).then_inc(gain_loaded, 16)
            for k in range(KD):
                if k >= WV_RING:
                    sp.wait_ge(wv_split, k - WV_RING + 1)
                sp.dma_start(wv_raw[:, k % WV_RING], io["w_v"][k]).then_inc(wv_loaded[k % WV_RING], 16)
                if k == 1:
                    load_x(1)
            load_x(2)
            load_x(3)
            sp.dma_start(wc_raw[:], io["w_chunks"][q_chunk]).then_inc(wc_loaded, 16)
            for b in range(NB):
                if b + 4 < NB:
                    load_x(b + 4)
                sp.wait_ge(prod_split, b + 1)
                sp.dma_start(io["v_hbm"][:, b // BPT, :, b % BPT, :].rearrange("h s e -> s h e"),
                             staged[:, b % 2].rearrange("s (h a) -> s h a", h=NHB)).then_inc(stored[b % 2], 16)
                if b == 1:
                    sp.wait_ge(wc_split, 1)
                    sp.dma_start(wc_raw[:], io["w_chunks"][k_chunk]).then_inc(wc_loaded, 16)
            for n in range(NQK):
                dst = io["q_hbm"] if n < NT else io["k_hbm"]
                cols = slice(n % NT * TW, (n % NT + 1) * TW)
                sp.wait_ge(prod_split, NB + n + 1)
                sp.dma_start(dst[:, 0:P, cols].rearrange("a c t -> c a t"),
                             staged[:, n % 2].rearrange("c (a t) -> c a t", a=2)).then_inc(stored[n % 2], 16)
                if n == NQK - 2:
                    sp.wait_ge(stored[0], 16 * (NB + NT + 2) // 2)
                    sp.wait_ge(turned_done, 2 * NB)
                    load_q(sp, io, mem, 0, 0, 0)
                    load_k(sp, io, mem, 0, 0)
                    load_v(sp, io, mem, 0, 0)
                    sp.wait_ge(wc_split, 2)
                    sp.dma_start(wc_raw[:], io["w_chunks"][2]).then_inc(mem["w_loaded"], 16)
            for slot in range(2):
                sp.wait_ge(stored[slot], 16 * (NB + NQK) // 2)

        @block.gpsimd
        def _(pool):
            pool.memset(ident[:], 0.0).then_inc(ident_zero, 1)
            pool.wait_ge(ident_zero, 1)
            pool.affine_select(out=ident[:], in_=ident[:], compare_op=ALU.not_equal, fill=1.0, base=0,
                               pattern=[[-1, P]], channel_multiplier=1).then_inc(ident_ready, 1)
            pool.memset(minus_half[:], -0.5).then_inc(ident_ready, 1)
            pool.wait_ge(ident_ready, 2)

            def inverse_root(b):
                pool.wait_ge(meansq_done, b + 1)
                pool.tensor_tensor(rstd[:, b:b + 1], meansq[:, b:b + 1], minus_half[:, b:b + 1], ALU.pow).then_inc(rstd_done, 1)

            def split_chunk(n):
                pool.wait_ge(wc_loaded, 16 * (n + 1))
                pool.tensor_copy(chunk_hi[n], wc_raw[:]).then_inc(wc_high, 1)
                pool.wait_ge(wc_high, n + 1)
                pool.tensor_tensor(chunk_lo[n], wc_raw[:], chunk_hi[n].bitcast(F32), ALU.subtract).then_inc(wc_split, 1)

            for b in range(NB):
                inverse_root(b)
                if b == 5:
                    split_chunk(0)
            pool.wait_ge(prod_done, NB)
            split_chunk(1)

        @block.scalar
        def _(act):
            for b in range(NB + 2):
                if b < NB:
                    act.wait_ge(x_loaded[b % 2], 16 * (b // 2 + 1))
                    if b >= 2:
                        act.wait_ge(turned_done, 2 * (b - 1))
                    act.activation(xn[:, b % 2], x_in[:, b % 2], ACT.Square, accum_out=sumsq[:, b:b + 1]).then_inc(sumsq_done, 1)
                if b < 2:
                    for k in range(4 * b, 4 * b + 4):
                        act.wait_ge(wv_loaded[k % WV_RING], 16 * (k // WV_RING + 1))
                        act.activation(wv_hi[:, k], wv_raw[:, k % WV_RING], ACT.Copy).then_inc(wv_high, 1)
                if 1 <= b <= NB:
                    for n in (2 * (b - 1), 2 * (b - 1) + 1):
                        act.wait_ge(turned_done, n + 1)
                        dst = hT_hi[:, 4 * (n % 2):4 * (n % 2) + 4, (b - 1) * P:b * P]
                        act.activation(dst, turned[n % 4][:].rearrange("p (k t) -> p k t", k=4), ACT.Copy).then_inc(turned_high, 1)
                if b >= 2:
                    n = b - 2
                    act.wait_ge(prod_done, n + 1)
                    if n >= 2:
                        act.wait_ge(stored[n % 2], 16 * (n // 2))
                    act.activation(v_out[n % 2][:, :, 0, :].bitcast(F32R), prod[n % 2][:].rearrange("p (h e) -> p h e", h=NHB),
                                   ACT.Copy).then_inc(prod_high, 1)
            for n in range(NQK):
                act.wait_ge(prod_done, NB + n + 1)
                act.wait_ge(stored[n % 2], 16 * ((NB + n) // 2))
                act.activation(qk_out[n % 2][:, 0].bitcast(F32R), prod[n % 2][:], ACT.Copy,
                               scale=QSCALE if n < NT else 1.0).then_inc(prod_high, 1)

        @block.vector
        def _(dve):
            dve.wait_ge(gain_loaded, 16)
            for b in range(NB + 2):
                if b < NB:
                    dve.wait_ge(sumsq_done, b + 1)
                    dve.tensor_scalar(meansq[:, b:b + 1], sumsq[:, b:b + 1], 1.0 / D, EPS, ALU.mult, ALU.add).then_inc(meansq_done, 1)
                    dve.wait_ge(rstd_done, b + 1)
                    dve.scalar_tensor_tensor(out=xn[:, b % 2], in0=x_in[:, b % 2], scalar=rstd[:, b:b + 1], in1=gain[:],
                                             op0=ALU.mult, op1=ALU.mult).then_inc(xn_done, 1)
                if b < 2:
                    for k in range(4 * b, 4 * b + 4):
                        dve.wait_ge(wv_high, k + 1)
                        dve.tensor_tensor(wv_lo[:, k], wv_raw[:, k % WV_RING], wv_hi[:, k].bitcast(F32), ALU.subtract).then_inc(wv_split, 1)
                if 1 <= b <= NB:
                    for n in (2 * (b - 1), 2 * (b - 1) + 1):
                        dve.wait_ge(turned_high, n + 1)
                        ks = slice(4 * (n % 2), 4 * (n % 2) + 4)
                        dve.tensor_tensor(hT_lo[:, ks, (b - 1) * P:b * P], turned[n % 4][:].rearrange("p (k t) -> p k t", k=4),
                                          hT_hi[:, ks, (b - 1) * P:b * P].bitcast(F32), ALU.subtract).then_inc(turned_split, 1)
                if b >= 2:
                    n = b - 2
                    dve.wait_ge(prod_high, n + 1)
                    dve.tensor_tensor(v_out[n % 2][:, :, 1, :].bitcast(F32R), prod[n % 2][:].rearrange("p (h e) -> p h e", h=NHB),
                                      v_out[n % 2][:, :, 0, :], ALU.subtract).then_inc(prod_split, 1)
            for n in range(NQK):
                dve.wait_ge(prod_high, NB + n + 1)
                dve.scalar_tensor_tensor(out=qk_out[n % 2][:, 1].bitcast(F32R), in0=prod[n % 2][:], scalar=QSCALE if n < NT else 1.0,
                                         in1=qk_out[n % 2][:, 0], op0=ALU.mult, op1=ALU.subtract).then_inc(prod_split, 1)

        @block.tensor
        def _(pe):
            pe.wait_ge(ident_ready, 1)

            def turn(b):
                pe.wait_ge(xn_done, b + 1)
                for n in (2 * b, 2 * b + 1):
                    if n >= 4:
                        pe.wait_ge(turned_split, n - 3)
                    for j in range(4):
                        k = 4 * (n % 2) + j
                        mm = pe.transpose(turned[n % 4][:, j * P:(j + 1) * P], xn[:, b % 2, k * P:(k + 1) * P], ident[:])
                    mm.then_inc(turned_done, 1)

            turn(0)
            turn(1)
            for b in range(NB):
                if b == 0:
                    pe.wait_ge(wv_split, KD)
                pe.wait_ge(turned_split, 2 * b + 2)
                if b >= 2:
                    pe.wait_ge(prod_split, b - 1)
                ts = slice(b * P, (b + 1) * P)
                split_products(pe, prod[b % 2][:], [(hT_hi[:, k, ts], hT_lo[:, k, ts], wv_hi[:, k], wv_lo[:, k])
                                                    for k in range(KD)]).then_inc(prod_done, 1)
                if b + 2 < NB:
                    turn(b + 2)
            for n in range(NQK):
                T = n % NT
                pe.wait_ge(wc_split, n // NT + 1)
                pe.wait_ge(prod_split, NB + n - 1)
                ts = slice(T * TW, (T + 1) * TW)
                split_products(pe, prod[n % 2][:], [(chunk_hi[n // NT][:, k], chunk_lo[n // NT][:, k], hT_hi[:, k, ts],
                                                     hT_lo[:, k, ts]) for k in range(KD)]).then_inc(prod_done, 1)


def load_q(sp, io, mem, p, e, T):
    slot = T % 2
    for a in (1, 0):
        for half in range(2):
            sp.dma_start(mem["q_t"][half * HD:(half + 1) * HD, slot, a].bitcast(F32),
                         io["q_hbm"][a, bass.ds(p * P + e * HD, HD), T * TW:(T + 1) * TW]).then_inc(mem["q_loaded"][slot], 16)


def load_k(sp, io, mem, p, g):
    slots = attention_slots()
    e, at = divmod(BPT * g, len(slots))
    c = slots[at][1]
    for half in (1, 0):
        sp.dma_start(mem["k_t"][half * HD:(half + 1) * HD, g % 2].bitcast(F32),
                     io["k_hbm"][half, bass.ds(p * P + e * HD, HD), c * TW:(c + 1) * TW]).then_inc(mem["k_loaded"][g % 2], 16)


def load_v(sp, io, mem, p, g):
    slots = attention_slots()
    e, at = divmod(BPT * g, len(slots))
    sp.dma_start(mem["v_t"][:, g % 2].bitcast(F32).rearrange("s j e -> s (j e)"),
                 io["v_hbm"][bass.ds(2 * p + e, 1), slots[at][1]].rearrange("h s j e -> s (h j e)")).then_inc(mem["v_loaded"][g % 2], 16)


def attend(nc, io, mem):
    hT_hi, hT_lo, ident = mem["hT_hi"], mem["hT_lo"], mem["ident"]
    HEAD = attention_slots()
    PER_HEAD, PER_PAIR = len(HEAD), 2 * len(HEAD)
    GROUPS = PER_HEAD // BPT
    CARRY_LAG, TURN_LAG, AV_LAG = 2, 6, 8
    NFILL = 12
    FILL_STEPS = 6
    MM_PER_STEP = 3 * KD // FILL_STEPS
    CHUNK_START = [1, 28, 55]
    FILL_START = [CHUNK_START[f // NT] + f % NT * FILL_STEPS for f in range(NFILL)]
    SPLIT = [25, 52, 79]
    LOAD_RAW = [1, 8, 15]
    Z_RING, W_RING = 3, 3

    def before_in_ring(n, ring, length):
        return n - ring if n >= ring else n - length + (length - 1 - n) // ring * ring

    RINGED = [g for g in range(2 * GROUPS) if g % GROUPS]

    def group_before(g):
        if g % GROUPS == 0:
            return g - GROUPS
        n = RINGED.index(g) - W_RING
        return RINGED[n] if n >= 0 else RINGED[n] - 2 * GROUPS

    def is_diag(s):
        T, c, _, _ = HEAD[s % PER_HEAD]
        return c == T

    def ends_tile(s):
        _, c, i, _ = HEAD[s % PER_HEAD]
        return c == 0 and i == BPT - 1

    def tile_number(s):
        return sum(ends_tile(r) for r in range(s))

    with ExitStack() as ctx:
        def sb(name, shape, dt=F32):
            return ctx.enter_context(nc.sbuf_tensor("at_" + name, shape, dt))

        def sem(name):
            return ctx.enter_context(nc.semaphore("at_" + name))

        def bank(name):
            return ctx.enter_context(nc.psum_tensor("at_" + name, [P, TW], F32))

        keep = sb("keep", [P, BPT, TW + 1])
        weight = sb("weight", [P, W_RING * BPT, TW])
        weight_first = sb("weight_first", [P, sum(w for _, _, _, w in HEAD[:BPT])])
        att_hi = sb("att_hi", [P, 2, TW], F32R)
        att_lo = sb("att_lo", [P, 2, TW], F32R)
        q_t, k_t, v_t, w_raw = mem["q_t"], mem["k_t"], mem["v_t"], mem["w_raw"]
        y_out = sb("y_out", [P, TW])
        w_hi = sb("w_hi", [P, KD, P], F32R)
        w_lo = sb("w_lo", [P, KD, P], F32R)
        staged = sb("staged", [P, 2, TW])
        mask = sb("mask", [P, P], BF16)
        ident_bf = ident[:].bitcast(BF16).rearrange("p (n half) -> p n half", half=2)[:, :, 1]
        z = [bank(f"z{i}") for i in range(Z_RING)]
        turned = [bank(f"turned{i}") for i in range(2)]
        y_acc, filled = bank("y_acc"), [bank(f"filled{i}") for i in range(2)]

        q_loaded, k_loaded, v_loaded, w_loaded = mem["q_loaded"], mem["k_loaded"], mem["v_loaded"], mem["w_loaded"]
        mask_zero, mask_set, mask_ready = sem("mask_zero"), sem("mask_set"), sem("mask_ready")
        scores_done, keep_done, gate_done = sem("scores_done"), sem("keep_done"), sem("gate_done")
        scan_done, weight_done, carry_done = sem("scan_done"), sem("weight_done"), sem("carry_done")
        turned_done, turned_high, turned_split = sem("turned_done"), sem("turned_high"), sem("turned_split")
        av_done, y_copied, y_stored = sem("av_done"), sem("y_copied"), sem("y_stored")
        w_high, w_split = sem("w_high"), sem("w_split")
        fill_done, fill_high, fill_split, fill_stored = sem("fill_done"), sem("fill_high"), sem("fill_split"), sem("fill_stored")

        def weight_of(s, i, cols):
            g = s % PER_PAIR // BPT
            if g % GROUPS == 0:
                start = sum(w for _, _, _, w in HEAD[:i])
                return weight_first[:, start + cols.start:start + cols.stop]
            return weight[:, RINGED.index(g) % W_RING * BPT + i, cols]

        def pairs(engine, body):
            body(0)
            with engine.Fori(1, 3) as p:
                body(p)
            body(3)

        def has(p, s):
            return s < PER_PAIR and not (isinstance(p, int) and p == 0 and s < 0)

        def last(p):
            return isinstance(p, int) and p == 3

        block = ctx.enter_context(nc.Block())

        @block.sync
        def _(sp):
            def store_y(p, s):
                e, T = s % PER_PAIR // PER_HEAD, HEAD[s % PER_HEAD][0]
                head = 2 * p + e if s >= 0 else 2 * p - 1
                sp.wait_ge(y_copied, p * 8 + tile_number(s) + 1 if s >= 0 else p * 8)
                sp.dma_start(io["o_hbm"][bass.ds(head, 1), :, T * TW:(T + 1) * TW].rearrange("h e t -> (h e) t"), y_out[:]).then_inc(y_stored, 16)

            def store_fill(p, f):
                sp.wait_ge(fill_split, p * NFILL + f + 1)
                cols = slice(f % NT * TW, (f % NT + 1) * TW)
                if last(p) or f // NT == 2:
                    row = p + (f // NT if last(p) else 0)
                    sp.dma_start(io["ap_hbm"][bass.ds(row, 1), :, cols].rearrange("n c t -> (n c) t"), staged[:, 0]).then_inc(fill_stored, 16)
                else:
                    dst = io["q_hbm"] if f // NT == 0 else io["k_hbm"]
                    sp.dma_start(dst[:, bass.ds(p * P + P, P), cols].rearrange("a c t -> c a t"), staged[:]).then_inc(fill_stored, 16)

            def pair(p):
                for g in range(2 * GROUPS):
                    s = BPT * g
                    T = HEAD[s % PER_HEAD][0]
                    if is_diag(s) and not (last(p) and s // PER_HEAD == 1 and T == NT - 1):
                        e, T1 = (s // PER_HEAD, T + 1) if T < NT - 1 else (s // PER_HEAD + 1, 0)
                        if has(p, s - 1):
                            sp.wait_ge(scores_done, p * PER_PAIR + s)
                        if e == 2:
                            sp.wait_ge(fill_stored, p * (NFILL * 16) + 8 * 16)
                        load_q(sp, io, mem, p, e, T1)
                    if not (last(p) and g == 2 * GROUPS - 1):
                        if not (isinstance(p, int) and p == 0 and g == 0):
                            sp.wait_ge(scores_done, p * PER_PAIR + s)
                        load_k(sp, io, mem, p, g + 1)
                    for w in range(3):
                        if g == LOAD_RAW[w] and not (last(p) and w == 2):
                            sp.wait_ge(w_split, p * 3 + w + 1)
                            sp.dma_start(w_raw[:], io["w_chunks"][bass.ds(p * 3 + w + 3, 1)].rearrange("n c k m -> c (n k) m")).then_inc(w_loaded, 16)
                    for r in range(-AV_LAG, PER_PAIR):
                        if ends_tile(r % PER_PAIR) and (r + AV_LAG + 1) // BPT == g and has(p, r):
                            store_y(p, r)
                    for f in range(NFILL):
                        if g == min((FILL_START[f] + FILL_STEPS + 1) // BPT, 2 * GROUPS - 1):
                            store_fill(p, f)
                    if not (isinstance(p, int) and p == 0 and g < 2):
                        sp.wait_ge(av_done, p * PER_PAIR + s - BPT)
                    if not (isinstance(p, int) and p == 0 and g == 0):
                        load_v(sp, io, mem, p, g)

            pairs(sp, pair)
            store_y(3, PER_PAIR - 1)
            sp.wait_ge(y_stored, 16 * NHB * NT)
            sp.wait_ge(fill_stored, 16 * 4 * NFILL)

        @block.gpsimd
        def _(pool):
            pool.memset(y_out[:, 0:P], 0.0).then_inc(mask_zero, 1)
            pool.wait_ge(mask_zero, 1)
            pool.affine_select(out=y_out[:, 0:P], in_=y_out[:, 0:P], compare_op=ALU.is_gt, fill=-BIG, base=0,
                               pattern=[[-1, P]], channel_multiplier=1).then_inc(mask_set, 1)

            def pair(p):
                for s in range(PER_PAIR):
                    _, _, i, w = HEAD[s % PER_HEAD]
                    at = p * PER_PAIR + s
                    pool.wait_ge(scan_done, at + 1)
                    pool.wait_ge(gate_done, at + 1)
                    gate = weight_of(s, i, slice(0, w))
                    pool.tensor_tensor(gate, keep[:, i, 1:w + 1], gate, ALU.mult).then_inc(weight_done, 1)

            pairs(pool, pair)

        @block.scalar
        def _(act):
            def pair(p):
                for s in range(PER_PAIR + (TURN_LAG if last(p) else 0)):
                    if s < PER_PAIR:
                        _, _, i, w = HEAD[s % PER_HEAD]
                        at = p * PER_PAIR + s
                        act.wait_ge(scores_done, at + 1)
                        if has(p, s - BPT):
                            act.wait_ge(carry_done, at - BPT + 1)
                        act.activation(keep[:, i, 0:w], z[s % Z_RING][:, 0:w], ACT.Sigmoid, scale=-1.0).then_inc(keep_done, 1)
                        g = s // BPT
                        before = group_before(g)
                        if i == 0 and has(p, before):
                            act.wait_ge(turned_done, p * PER_PAIR + before * BPT + BPT)
                        act.activation(weight_of(s, i, slice(0, w)), z[s % Z_RING][:, 0:w], ACT.Sigmoid).then_inc(gate_done, 1)
                    for f in range(8):
                        if s == FILL_START[f] + FILL_STEPS and not last(p):
                            act.wait_ge(fill_done, p * NFILL + f + 1)
                            if has(p, f - 1):
                                act.wait_ge(fill_stored, (p * NFILL + f) * 16)
                            act.activation(staged[:, 0].bitcast(F32R), filled[f % 2][:], ACT.Copy,
                                           scale=QSCALE if f < NT else 1.0).then_inc(fill_high, 1)
                    r = s - TURN_LAG
                    if has(p, r):
                        n0 = r % BPT * P if is_diag(r) else 0
                        at = p * PER_PAIR + r
                        act.wait_ge(turned_done, at + 1)
                        if has(p, r - 2):
                            act.wait_ge(av_done, at - 1)
                        act.activation(att_hi[:, r % 2, n0:TW], turned[r % 2][:, n0:TW], ACT.Copy).then_inc(turned_high, 1)

            pairs(act, pair)

        @block.vector
        def _(dve):
            def split(n):
                dve.wait_ge(w_loaded, 16 * n)
                dve.tensor_copy(w_hi[:], w_raw[:]).then_inc(w_high, 1)
                dve.wait_ge(w_high, n)
                dve.tensor_tensor(w_lo[:], w_raw[:], w_hi[:].bitcast(F32), ALU.subtract).then_inc(w_split, 1)

            def pair(p):
                for s in range(PER_PAIR + (AV_LAG if last(p) else 0)):
                    if s < PER_PAIR:
                        _, _, i, w = HEAD[s % PER_HEAD]
                        at = p * PER_PAIR + s
                        dve.wait_ge(keep_done, at + 1)
                        if is_diag(s):
                            dve.memset(keep[:, i, w:w + 1], 1.0)
                            n = w
                        else:
                            n = w + 1
                        back = keep[:, i, 0:n][:, ::-1]
                        dve.tensor_tensor_scan(back, back, back, 1.0, ALU.mult, ALU.bypass).then_inc(scan_done, 1)
                        if has(p, s - CARRY_LAG):
                            query_block = HEAD[(s - CARRY_LAG) % PER_HEAD][2]
                            dve.wait_ge(weight_done, at - CARRY_LAG + 1)
                            dve.tensor_copy(keep[:, query_block, TW:TW + 1], keep[:, query_block, 0:1]).then_inc(carry_done, 1)
                    r = s - AV_LAG
                    if has(p, r) and ends_tile(r % PER_PAIR):
                        dve.wait_ge(av_done, p * PER_PAIR + r + 1)
                        tiles = tile_number(r) if r >= 0 else -1
                        if not (isinstance(p, int) and p == 0 and tiles == 0):
                            dve.wait_ge(y_stored, (p * 8 + tiles) * 16)
                        dve.tensor_copy(y_out[:], y_acc[:]).then_inc(y_copied, 1)
                    for f in range(NFILL):
                        if s == FILL_START[f] + FILL_STEPS:
                            if f < 8 and not last(p):
                                dve.wait_ge(fill_high, p * 8 + f + 1)
                                dve.scalar_tensor_tensor(out=staged[:, 1].bitcast(F32R), in0=filled[f % 2][:], scalar=QSCALE if f < NT else 1.0,
                                                         in1=staged[:, 0], op0=ALU.mult, op1=ALU.subtract).then_inc(fill_split, 1)
                            else:
                                dve.wait_ge(fill_done, p * NFILL + f + 1)
                                dve.wait_ge(fill_stored, (p * NFILL + f) * 16)
                                dve.tensor_copy(staged[:, 0], filled[f % 2][:]).then_inc(fill_split, 1)
                    r = s - TURN_LAG
                    if has(p, r):
                        n0 = r % BPT * P if is_diag(r) else 0
                        dve.wait_ge(turned_high, p * PER_PAIR + r + 1)
                        dve.tensor_tensor(att_lo[:, r % 2, n0:TW], turned[r % 2][:, n0:TW], att_hi[:, r % 2, n0:TW].bitcast(F32),
                                          ALU.subtract).then_inc(turned_split, 1)
                    for w in range(3):
                        if s == SPLIT[w] and not (last(p) and w == 2):
                            dve.wait_ge(fill_done, p * NFILL + (w + 1) * NT)
                            split(p * 3 + w + 2)

            dve.wait_ge(mask_set, 1)
            dve.tensor_copy(mask[:], y_out[:, 0:P]).then_inc(mask_ready, 1)
            split(1)
            pairs(dve, pair)

        @block.tensor
        def _(pe):
            def scores(p, s):
                T, _, i, w = HEAD[s % PER_HEAD]
                g = s // BPT
                if i == 0:
                    pe.wait_ge(k_loaded[g % 2], 32 * (p * GROUPS + g // 2 + 1))
                    if is_diag(s):
                        tiles = tile_number(s)
                        pe.wait_ge(q_loaded[T % 2], 64 * (p * 4 + tiles // 2 + 1))
                before = before_in_ring(s, Z_RING, PER_PAIR)
                if has(p, before):
                    pe.wait_ge(gate_done, p * PER_PAIR + before + 1)
                bank = z[s % Z_RING]
                keys = k_t[:, g % 2, 0:w]
                pe.matmul(bank[:, 0:w], q_t[:, T % 2, 0, i * P:(i + 1) * P], keys, start=True, stop=False)
                mm = pe.matmul(bank[:, 0:w], q_t[:, T % 2, 1, i * P:(i + 1) * P], keys, start=False, stop=not is_diag(s))
                if is_diag(s):
                    mm = pe.matmul(bank[:, w - P:w], ident_bf, mask[:], start=False, stop=True)
                mm.then_inc(scores_done, 1)

            def turn(p, r):
                j = r % BPT
                if j == 0:
                    pe.wait_ge(weight_done, p * PER_PAIR + r + BPT)
                if has(p, r - 2):
                    pe.wait_ge(turned_split, p * PER_PAIR + r - 1)
                for i in range(j if is_diag(r) else 0, BPT):
                    mm = pe.transpose(turned[r % 2][:, i * P:(i + 1) * P],
                                      weight_of(r, i, slice(j * P, (j + 1) * P)), ident[:])
                mm.then_inc(turned_done, 1)

            def multiply_v(p, r):
                j, g = r % BPT, r // BPT
                n0 = j * P if is_diag(r) else 0
                pe.wait_ge(turned_split, p * PER_PAIR + r + 1)
                if j == 0:
                    pe.wait_ge(v_loaded[g % 2], 16 * (p * GROUPS + g // 2 + 1))
                starts = is_diag(r) and j == 0
                if starts:
                    tiles = tile_number(r)
                    if not (isinstance(p, int) and p == 0 and tiles == 0):
                        pe.wait_ge(y_copied, p * 8 + tiles)
                v = v_t[:, g % 2, j]
                pe.matmul(y_acc[:, n0:TW], v, att_hi[:, r % 2, n0:TW], start=starts, stop=False)
                pe.matmul(y_acc[:, n0:TW], v, att_lo[:, r % 2, n0:TW], start=False,
                          stop=ends_tile(r % PER_PAIR)).then_inc(av_done, 1)

            def project(p, s):
                for f in range(NFILL):
                    part = s - FILL_START[f]
                    if not 0 <= part < FILL_STEPS:
                        continue
                    w, T = f // NT, f % NT
                    if part == 0:
                        if T == 0:
                            pe.wait_ge(w_split, p * 3 + w + 1)
                        if has(p, f - 2):
                            pe.wait_ge(fill_split, p * NFILL + f - 1)
                    for m in range(part * MM_PER_STEP, (part + 1) * MM_PER_STEP):
                        k, kind = m // 3, m % 3
                        wt = (w_hi, w_hi, w_lo)[kind][:, k]
                        ht = (hT_hi, hT_lo, hT_hi)[kind][:, k, T * TW:(T + 1) * TW]
                        mm = pe.matmul(filled[f % 2][:], wt, ht, start=m == 0, stop=m == 3 * KD - 1)
                    if part == FILL_STEPS - 1:
                        mm.then_inc(fill_done, 1)

            def pair(p):
                for s in range(PER_PAIR + (AV_LAG if last(p) else 0)):
                    if s < PER_PAIR:
                        scores(p, s)
                    if has(p, s - TURN_LAG):
                        turn(p, s - TURN_LAG)
                    if has(p, s - AV_LAG):
                        multiply_v(p, s - AV_LAG)
                    if s < PER_PAIR:
                        project(p, s)

            pe.wait_ge(mask_ready, 1)
            pairs(pe, pair)


HALO = 16
POOL_WINDOWS = (2, 4, 8, 16)


def mix(nc, io, mem):
    ident = mem["ident"]
    with ExitStack() as ctx:
        def sb(name, shape, dt=F32):
            return ctx.enter_context(nc.sbuf_tensor("mx_" + name, shape, dt))

        def sem(name):
            return ctx.enter_context(nc.semaphore("mx_" + name))

        def sem2(name):
            return [sem(name + "0"), sem(name + "1")]

        x_t = sb("x_t", [P, 2, D])
        h_out = sb("h_out", [P, 2, 2, KD, P])
        wo_raw = mem["wo_raw"]
        wo_hi, wo_lo = sb("wo_hi", [P, KD, D], F32R), sb("wo_lo", [P, KD, D], F32R)
        a_t = sb("a_t", [P, 2, 4, P])
        p_t = sb("p_t", [P, 2, 2, HALO + P])
        o_t = sb("o_t", [P, 2, NHB, P])
        y_t, y_sq = mem["gated"][:].rearrange("p (a d) -> p a d", a=2), mem["g_raw"][:].rearrange("p a t -> p (a t)")
        yT_hi, yT_lo = sb("yT_hi", [P, 2, KD, P], F32R), sb("yT_lo", [P, 2, KD, P], F32R)
        xn = sb("xn", [P, D])
        sum2, sum4, sum8 = (sb(n, [P, 2, HALO + P]) for n in ("sum2", "sum4", "sum8"))
        window = sb("window", [P, 2, P])
        mean = sb("mean", [P, 2, P])
        pooled = sb("pooled", [P, 2, P])
        v_sq, v_n, v_g, s_b = (sb(n, [P, 256]) for n in ("v_sq", "v_n", "v_g", "s_b"))
        v_stat, y_stat, x_stat = sb("v_stat", [P, 3, 4]), sb("y_stat", [P, 3, NHT]), sb("x_stat", [P, 3, 1])
        minus_half = sb("minus_half", [P, NHT])
        sgu_w, sgu_g, sgu_b = sb("sgu_w", [P, 4, P]), sb("sgu_g", [P, 256]), sb("sgu_b", [P, 4])
        pool_w, pool_scale = sb("pool_w", [P, 2, P]), sb("pool_scale", [P, 256])
        inv_first, inv_rest = sb("inv_first", [P, 2, P]), sb("inv_rest", [P, 2, P])
        mix_g, norm2_g = sb("mix_g", [P, D]), sb("norm2_g", [P, D])
        two_ident = sb("two_ident", [P, HD])

        proj = ctx.enter_context(nc.psum_tensor("mx_proj", [P, 2, TW], F32))
        gelu_turned, y_b, small = (ctx.enter_context(nc.psum_tensor("mx_" + n, [P, TW], F32)) for n in ("gelu_turned", "y_b", "small"))
        turned = ctx.enter_context(nc.psum_tensor("mx_turned", [P, 2, TW], F32))

        const_loaded, pool_w_zero, const_ready = sem("const_loaded"), sem("pool_w_zero"), sem("const_ready")
        N_CONST = 10
        mix_g_loaded, norm2_g_loaded, two_ident_ready = sem("mix_g_loaded"), sem("norm2_g_loaded"), sem("two_ident_ready")
        wo_loaded, wo_high, wo_split = sem2("wo_loaded"), sem("wo_high"), sem("wo_split")
        a_loaded, p_loaded, o_loaded, x_loaded = (sem2(n + "_loaded") for n in "apox")
        halo_zero = sem("halo_zero")
        gelu_done, window_step, mean_done, pooled_done = (sem(n) for n in ("gelu_done", "window_step", "mean_done", "pooled_done"))
        gelu_turned_done, yb_done, yb_copied = sem("gelu_turned_done"), sem("yb_done"), sem("yb_copied")
        vsq_done, vsum_done, vmean_done, vstd_done, vn_done, vg_done = (sem(n) for n in ("vsq_done", "vsum_done", "vmean_done", "vstd_done", "vn_done", "vg_done"))
        small_done, sb_done, y_done = sem("small_done"), sem("sb_done"), sem("y_done")
        ysq_done, ysum_done, ymean_done, ystd_done, yn_done, yg_done = (sem(n) for n in ("ysq_done", "ysum_done", "ymean_done", "ystd_done", "yn_done", "yg_done"))
        yT_turned, yT_high, yT_split = sem("yT_turned"), sem("yT_high"), sem("yT_split")
        proj_done, x2_done, x2_stored = sem("proj_done"), sem("x2_done"), mem["x2_stored"]
        xsq_done, xmean_done, xstd_done, xn_done = sem("xsq_done"), sem("xmean_done"), sem("xstd_done"), sem("xn_done")
        hT_turned, hT_high, hT_split, h_stored = sem("hT_turned"), sem("hT_high"), sem("hT_split"), mem["h_stored"]

        def pipeline(engine, slot, start, end):
            for b in range(start, 4):
                slot(b // 2, b % 2)
            with engine.Fori(2, 6) as i:
                slot(i, 0)
                slot(i, 1)
            for b in range(12, end + 1):
                slot(b // 2, b % 2)

        def stage(i, parity, ahead):
            if isinstance(i, int) and not 0 <= 2 * i + parity + ahead < NB:
                return None
            n = parity + ahead
            return i * 2 + n, i + n // 2, n % 2

        def early(k, n=1):
            return isinstance(k, int) and k < n

        def wo_share(i, parity):
            if isinstance(i, int) and i == -1:
                return range(parity * KD // 2, (parity + 1) * KD // 2)
            return ()

        block = ctx.enter_context(nc.Block())

        @block.sync
        def _(sp):
            def tokens(k):
                return bass.ds(k * P, P)

            def load_a_o(k, q):
                sp.dma_start(a_t[:, q], io["ap_hbm"][0:4, :, tokens(k)].rearrange("n c t -> c n t")).then_inc(a_loaded[q], 16)
                sp.dma_start(o_t[:, q], io["o_hbm"][:, :, tokens(k)].rearrange("h e t -> e h t")).then_inc(o_loaded[q], 16)

            def load_p(k, q):
                if early(k):
                    src, dst = io["ap_hbm"][4:6, :, 0:P], p_t[:, q, :, HALO:HALO + P]
                else:
                    src, dst = io["ap_hbm"][4:6, :, bass.ds(k * P - HALO, HALO + P)], p_t[:, q]
                sp.dma_start(dst, src.rearrange("n c t -> c n t")).then_inc(p_loaded[q], 16)

            def load_x(k, q):
                sp.dma_start(x_t[:, q], io["x"][tokens(k), :]).then_inc(x_loaded[q], 16)

            def load_for_ffn_up():
                for half in range(2):
                    sp.dma_start(mem["w_raw"][:, half], io["w_up"][0, half].rearrange("c k m -> c (k m)")).then_inc(mem["w_loaded"][half], 16)
                for q in range(2):
                    sp.wait_ge(h_stored[q], 32 * BPT // 2)
                for piece in range(FIRST_PIECES):
                    ks = slice(piece * KD // FIRST_PIECES, (piece + 1) * KD // FIRST_PIECES)
                    for a in range(2):
                        sp.dma_start(mem["first_tile"][:, a, ks].bitcast(F32), io["h2_hbm"][a, ks, :, 0:TW].rearrange("k c t -> c k t")).then_inc(mem["first_loaded"][piece], 16)

            def slot(i, parity):
                if isinstance(i, int) and (i, parity) == (6, 0):
                    load_for_ffn_up()
                ahead = stage(i, parity, 4)
                if ahead and not early(ahead[0], 2):
                    k, h, q = ahead
                    sp.wait_ge(gelu_turned_done, k - 1)
                    sp.wait_ge(yb_done, k - 1)
                    load_a_o(k, q)
                at = stage(i, parity, -1)
                if at:
                    sp.wait_ge(x2_done, at[0] * 2 + 2)
                    sp.dma_start(io["x2_hbm"][tokens(at[0]), :], x_t[:, at[2]]).then_inc(x2_stored[at[2]], 16)
                at = stage(i, parity, -2)
                if at:
                    k, h, q = at
                    sp.wait_ge(hT_split, k * 2 + 2)
                    for a in (1, 0):
                        sp.dma_start(io["h2_hbm"][a, :, :, tokens(k)].rearrange("k c t -> c k t"), h_out[:, q, a]).then_inc(h_stored[q], 16)
                if ahead and not early(ahead[0], 2):
                    k, h, q = ahead
                    sp.wait_ge(pooled_done, k - 1)
                    load_p(k, q)
                at = stage(i, parity, -1)
                if at and stage(i, parity, 1):
                    k, h, q = at
                    sp.wait_ge(xn_done, k + 1)
                    sp.wait_ge(x2_stored[q], h * 16 + 16)
                    load_x(k + 2, q)

            load_a_o(0, 0)
            load_p(0, 0)
            for n, c in (("sgu_w", sgu_w), ("sgu_b", sgu_b), ("inv_first", inv_first), ("inv_rest", inv_rest)):
                sp.dma_start(c[:], io[n]).then_inc(const_loaded, 16)
            for n, c in (("sgu_g", sgu_g), ("pool_scale", pool_scale)):
                sp.dma_start(c[:], io[n].to_broadcast([P, 256])).then_inc(const_loaded, 16)
            sp.wait_ge(pool_w_zero, 1)
            for g in range(4):
                rows = slice(g % 2 * HD, g % 2 * HD + HD)
                sp.dma_start(pool_w[rows, g // 2, rows], io["pool_w"][g]).then_inc(const_loaded, 16)
            load_a_o(1, 1)
            load_p(1, 1)
            for n in range(2):
                sp.dma_start(wo_raw[:, 4 * n:4 * n + 4], io["w_o"][4 * n:4 * n + 4].rearrange("k c d -> c k d")).then_inc(wo_loaded[n], 16)
                if n == 0:
                    sp.dma_start(mix_g[:], io["mix_g"].to_broadcast([P, D])).then_inc(mix_g_loaded, 16)
            sp.dma_start(norm2_g[:], io["norm2_g"].to_broadcast([P, D])).then_inc(norm2_g_loaded, 16)
            for k in range(2):
                load_x(k, k)
            pipeline(sp, slot, -3, NB + 1)

        @block.gpsimd
        def _(pool):
            pool.memset(pool_w[:], 0.0).then_inc(pool_w_zero, 1)
            pool.memset(p_t[:, 0, :, 0:HALO], 0.0).then_inc(halo_zero, 1)
            pool.memset(minus_half[:], -0.5).then_inc(halo_zero, 1)

            def add_windows(k, h, q):
                tok, p = p_t[:, q], HALO + P
                lo, hi = slice(0, HD), slice(HD, P)
                steps = [
                    (sum2[:, :, 1:p], tok[:, :, 1:p], tok[:, :, 0:p - 1]),
                    (window[lo, 0], tok[lo, 0, HALO:p], tok[lo, 0, HALO - 1:p - 1]),
                    (window[hi, 0], sum2[hi, 0, HALO:p], sum2[hi, 0, HALO - 2:p - 2]),
                    (sum4[:, 1, 3:p], sum2[:, 1, 3:p], sum2[:, 1, 1:p - 2]),
                    (window[lo, 1], sum4[lo, 1, HALO:p], sum4[lo, 1, HALO - 4:p - 4]),
                    (sum8[hi, 1, 7:p], sum4[hi, 1, 7:p], sum4[hi, 1, 3:p - 4]),
                    (window[hi, 1], sum8[hi, 1, HALO:p], sum8[hi, 1, HALO - 8:p - 8]),
                ]
                pool.wait_ge(p_loaded[q], h * 16 + 16)
                if not early(k):
                    pool.wait_ge(mean_done, k)
                for n, (out, x, y) in enumerate(steps):
                    if n:
                        pool.wait_ge(window_step, k * 7 + n)
                    pool.tensor_tensor(out, x, y, ALU.add).then_inc(window_step, 1)
                pool.wait_ge(window_step, k * 7 + 7)

            def inverse_root(stat, ready, done, k):
                w = stat.shape[-1]
                pool.wait_ge(ready, k + 1)
                pool.tensor_tensor(stat[:, 2], stat[:, 1], minus_half[:, 0:w], ALU.pow).then_inc(done, 1)

            def slot(i, parity):
                at = stage(i, parity, 2)
                if at:
                    inverse_root(v_stat, vmean_done, vstd_done, at[0])
                at = stage(i, parity, -1)
                if at:
                    inverse_root(x_stat, xmean_done, xstd_done, at[0])
                at = stage(i, parity, 3)
                if at:
                    add_windows(*at)
                    if early(at[0]):
                        pool.wait_ge(const_loaded, 16 * N_CONST)
                        pool.affine_select(out=sgu_w[:], in_=sgu_w[:], compare_op=ALU.is_ge, fill=0.0, base=0,
                                           pattern=[[0, 4], [1, P]], channel_multiplier=-1).then_inc(const_ready, 1)
                at = stage(i, parity, 2)
                if at:
                    inverse_root(y_stat, ymean_done, ystd_done, at[0])
                    pool.wait_ge(yn_done, at[0] + 1)
                    if early(at[0]):
                        pool.wait_ge(mix_g_loaded, 16)
                    pool.tensor_tensor(y_t[:, at[2]], y_t[:, at[2]], mix_g[:], ALU.mult).then_inc(yg_done, 1)

            pool.wait_ge(halo_zero, 2)
            pipeline(pool, slot, -3, NB + 1)

        @block.scalar
        def _(act):
            def slot(i, parity):
                at = stage(i, parity, 2)
                if at:
                    act.wait_ge(gelu_turned_done, at[0] + 1)
                    act.activation(v_sq[:], gelu_turned[:, 256:512], ACT.Square).then_inc(vsq_done, 1)
                at = stage(i, parity, -2)
                if at:
                    k, h, q = at
                    for n in range(2):
                        act.wait_ge(hT_turned, k * 2 + n + 1)
                        if n == 0 and not early(k, 2):
                            act.wait_ge(h_stored[q], h * 32)
                        act.activation(h_out[:, q, 0, 4 * n:4 * n + 4].bitcast(F32R),
                                       turned[:, n].rearrange("p (k t) -> p k t", k=4), ACT.Copy).then_inc(hT_high, 1)
                at = stage(i, parity, 2)
                if at:
                    k, h, q = at
                    act.wait_ge(yb_done, k + 1)
                    if not early(k, 2):
                        act.wait_ge(yT_turned, k * 2 - 2)
                    act.activation(y_t[:, q, 256:768], y_b[:], ACT.Copy).then_inc(yb_copied, 1)
                at = stage(i, parity, -1)
                if at:
                    k, h, q = at
                    act.wait_ge(x2_done, k * 2 + 2)
                    if not early(k):
                        act.wait_ge(hT_turned, k * 2)
                    act.activation(xn[:], x_t[:, q], ACT.Square, accum_out=x_stat[:, 0]).then_inc(xsq_done, 1)
                at = stage(i, parity, 3)
                if at:
                    k, h, q = at
                    act.wait_ge(a_loaded[q], h * 16 + 16)
                    act.activation(a_t[:, q], a_t[:, q], ACT.Gelu).then_inc(gelu_done, 1)
                at = stage(i, parity, 1)
                if at:
                    k, h, q = at
                    for n in range(2):
                        act.wait_ge(yT_turned, k * 2 + n + 1)
                        if n == 0 and not early(k, 2):
                            act.wait_ge(proj_done, k * 2 - 2)
                        act.activation(yT_hi[:, q, 4 * n:4 * n + 4], turned[:, n].rearrange("p (k t) -> p k t", k=4),
                                       ACT.Copy).then_inc(yT_high, 1)
                heads, share = stage(i, parity, 2), wo_share(i, parity)
                def wo_highs():
                    for k in share:
                        act.wait_ge(wo_loaded[k // 4], 16)
                        act.activation(wo_hi[:, k], wo_raw[:, k], ACT.Copy).then_inc(wo_high, 1)

                if share and share[0] > 0:
                    wo_highs()
                if heads:
                    act.wait_ge(y_done, heads[0] + 1)
                    act.activation(y_sq, y_t[:, heads[2]], ACT.Square).then_inc(ysq_done, 1)
                if share and share[0] == 0:
                    wo_highs()

            pipeline(act, slot, -3, NB + 1)

        @block.vector
        def _(dve):
            dve.tensor_copy(two_ident[0:HD], ident[0:HD, 0:HD]).then_inc(two_ident_ready, 1)
            dve.tensor_copy(two_ident[HD:P], ident[HD:P, HD:P]).then_inc(two_ident_ready, 1)

            def mean_plus_eps(stat, n, done):
                dve.tensor_scalar(stat[:, 1], stat[:, 0], 1.0 / n, EPS, ALU.mult, ALU.add).then_inc(done, 1)

            def per_head(ap, n):
                return ap.rearrange("t (h e) -> t h e", h=n)

            def spread(ap, n):
                return ap.unsqueeze(2).to_broadcast([P, n, HD])

            def add_residual(k, h, q, n):
                cols = slice(n * TW, (n + 1) * TW)
                dve.wait_ge(proj_done, k * 2 + n + 1)
                if n == 0:
                    dve.wait_ge(x_loaded[q], h * 16 + 16)
                dve.tensor_tensor(x_t[:, q, cols], proj[:, n], x_t[:, q, cols], ALU.add).then_inc(x2_done, 1)

            def slot(i, parity):
                second_norm, heads = stage(i, parity, -1), stage(i, parity, 2)
                if second_norm:
                    add_residual(*second_norm, 1)
                at = stage(i, parity, -2)
                if at:
                    k, h, q = at
                    for n in range(2):
                        dve.wait_ge(hT_high, k * 2 + n + 1)
                        dve.tensor_tensor(h_out[:, q, 1, 4 * n:4 * n + 4].bitcast(F32R), turned[:, n].rearrange("p (k t) -> p k t", k=4),
                                          h_out[:, q, 0, 4 * n:4 * n + 4], ALU.subtract).then_inc(hT_split, 1)
                if heads:
                    k, h, q = heads
                    dve.wait_ge(vsq_done, k + 1)
                    dve.tensor_reduce(v_stat[:, 0], per_head(v_sq[:], 4), AX_X, ALU.add).then_inc(vsum_done, 1)
                    dve.wait_ge(vsum_done, k + 1)
                    mean_plus_eps(v_stat, HD, vmean_done)
                    dve.wait_ge(window_step, k * 7 + 7)
                    if early(k):
                        dve.wait_ge(const_loaded, 16 * N_CONST)
                    dve.tensor_tensor(mean[:], window[:], (inv_first if early(k) else inv_rest)[:], ALU.mult).then_inc(mean_done, 1)
                    dve.wait_ge(mean_done, k + 1)
                    if not early(k):
                        dve.wait_ge(small_done, k)
                    dve.tensor_tensor(pooled[:], mean[:], p_t[:, q, :, HALO:HALO + P], ALU.subtract).then_inc(pooled_done, 1)
                    dve.wait_ge(vstd_done, k + 1)
                    dve.tensor_tensor(per_head(v_n[:], 4), per_head(gelu_turned[:, 256:512], 4), spread(v_stat[:, 2], 4), ALU.mult).then_inc(vn_done, 1)
                if second_norm:
                    dve.wait_ge(xsq_done, second_norm[0] + 1)
                    mean_plus_eps(x_stat, D, xmean_done)
                if heads:
                    dve.wait_ge(vn_done, k + 1)
                    dve.tensor_tensor(v_g[:], v_n[:], sgu_g[:], ALU.mult).then_inc(vg_done, 1)
                if second_norm:
                    k, h, q = second_norm
                    dve.wait_ge(xstd_done, k + 1)
                    if early(k):
                        dve.wait_ge(norm2_g_loaded, 16)
                    dve.scalar_tensor_tensor(out=xn[:], in0=x_t[:, q], scalar=x_stat[:, 2], in1=norm2_g[:],
                                             op0=ALU.mult, op1=ALU.mult).then_inc(xn_done, 1)
                at = stage(i, parity, 0)
                if at:
                    add_residual(*at, 0)
                at = stage(i, parity, 1)
                if at:
                    k, h, q = at
                    for n in range(2):
                        dve.wait_ge(yT_high, k * 2 + n + 1)
                        dve.tensor_tensor(yT_lo[:, q, 4 * n:4 * n + 4], turned[:, n].rearrange("p (k t) -> p k t", k=4),
                                          yT_hi[:, q, 4 * n:4 * n + 4].bitcast(F32), ALU.subtract).then_inc(yT_split, 1)
                if heads:
                    k, h, q = heads
                    dve.wait_ge(small_done, k + 1)
                    dve.tensor_tensor(per_head(s_b[:], 4), per_head(small[:, 0:256], 4), spread(sgu_b[:], 4), ALU.add).then_inc(sb_done, 1)
                    dve.tensor_tensor(y_t[:, q, 768:1024], small[:, 256:512], pool_scale[:], ALU.mult)
                    dve.wait_ge(sb_done, k + 1)
                    dve.wait_ge(yb_copied, k + 1)
                    dve.tensor_tensor(y_t[:, q, 0:256], s_b[:], gelu_turned[:, 0:256], ALU.mult).then_inc(y_done, 1)
                    dve.wait_ge(ysq_done, k + 1)
                    dve.tensor_reduce(y_stat[:, 0], per_head(y_sq, NHT), AX_X, ALU.add).then_inc(ysum_done, 1)
                    dve.wait_ge(ysum_done, k + 1)
                    mean_plus_eps(y_stat, HD, ymean_done)
                    for wo in wo_share(i, parity):
                        dve.wait_ge(wo_high, wo + 1)
                        dve.tensor_tensor(wo_lo[:, wo], wo_raw[:, wo], wo_hi[:, wo].bitcast(F32), ALU.subtract).then_inc(wo_split, 1)
                    dve.wait_ge(ystd_done, k + 1)
                    dve.tensor_tensor(per_head(y_t[:, q], NHT), per_head(y_t[:, q], NHT), spread(y_stat[:, 2], NHT), ALU.mult).then_inc(yn_done, 1)

            pipeline(dve, slot, -3, NB + 1)

        @block.tensor
        def _(pe):
            def project(k, q, n):
                if n == 0:
                    if early(k):
                        pe.wait_ge(wo_split, KD)
                    pe.wait_ge(yT_split, k * 2 + 2)
                if not early(k):
                    pe.wait_ge(x2_done, k * 2 + (n - 1))
                cols = slice(n * TW, (n + 1) * TW)
                split_products(pe, proj[:, n], [(yT_hi[:, q, c], yT_lo[:, q, c], wo_hi[:, c, cols], wo_lo[:, c, cols])
                                                for c in range(KD)]).then_inc(proj_done, 1)

            def turn(src, done):
                for n in range(2):
                    for j in range(4):
                        c = 4 * n + j
                        mm = pe.transpose(turned[:, n, j * P:(j + 1) * P], src[:, c * P:(c + 1) * P], ident[:])
                    mm.then_inc(done, 1)

            def slot(i, parity):
                at = stage(i, parity, 0)
                if at:
                    project(at[0], at[2], 0)
                at = stage(i, parity, 1)
                if at:
                    k, h, q = at
                    pe.wait_ge(yg_done, k + 1)
                    if not early(k, 3):
                        pe.wait_ge(hT_split, k * 2 - 4)
                    turn(y_t[:, q], yT_turned)
                at = stage(i, parity, 2)
                if at:
                    k, h, q = at
                    if early(k):
                        pe.wait_ge(const_ready, 1)
                    pe.wait_ge(vg_done, k + 1)
                    pe.wait_ge(pooled_done, k + 1)
                    if not early(k):
                        pe.wait_ge(y_done, k)
                    for j in range(4):
                        pe.matmul(small[:, j * HD:(j + 1) * HD], sgu_w[:, j], v_g[:, j * HD:(j + 1) * HD], start=True, stop=True)
                    for j in range(2):
                        mm = pe.matmul(small[:, 256 + j * P:256 + (j + 1) * P], pooled[:, j], pool_w[:, j], start=True, stop=True)
                    mm.then_inc(small_done, 1)
                at = stage(i, parity, 0)
                if at:
                    project(at[0], at[2], 1)
                at = stage(i, parity, 3)
                if at:
                    k, h, q = at
                    pe.wait_ge(gelu_done, k + 1)
                    if not early(k):
                        pe.wait_ge(y_done, k)
                    for j in range(4):
                        mm = pe.transpose(gelu_turned[:, j * P:(j + 1) * P], a_t[:, q, j], ident[:])
                    mm.then_inc(gelu_turned_done, 1)
                    pe.wait_ge(o_loaded[q], h * 16 + 16)
                    if not early(k):
                        pe.wait_ge(yb_copied, k)
                    for j in range(NHB):
                        mm = pe.matmul(y_b[:, j * HD:(j + 1) * HD], o_t[:, q, j], two_ident[:], start=True, stop=True)
                    mm.then_inc(yb_done, 1)
                at = stage(i, parity, -1)
                if at:
                    k = at[0]
                    pe.wait_ge(xn_done, k + 1)
                    if stage(i, parity, 1):
                        pe.wait_ge(yT_split, k * 2 + 6)
                    else:
                        pe.wait_ge(hT_split, k * 2)
                    turn(xn[:], hT_turned)

            pe.wait_ge(two_ident_ready, 2)
            pipeline(pe, slot, -3, NB + 1)


def ffn_up(nc, io, mem):
    with ExitStack() as ctx:
        def sb(name, shape, dt=F32):
            return ctx.enter_context(nc.sbuf_tensor("up_" + name, shape, dt))

        def sem(name):
            return ctx.enter_context(nc.semaphore("up_" + name))

        first_tile = mem["first_tile"]
        h_hi, h_lo = sb("h_hi", [P, KD, S - TW], F32R), sb("h_lo", [P, KD, S - TW], F32R)
        w_raw = mem["w_raw"][:].rearrange("c n (k m) -> c n k m", k=KD)
        w_hi, w_lo = sb("w_hi", [P, 2, KD, P], F32R), sb("w_lo", [P, 2, KD, P], F32R)
        conv = sb("conv", [P, NF, 2, 4])
        z_c = sb("z_c", [P, 2, S])
        gated = mem["gated"]
        z = [ctx.enter_context(nc.psum_tensor(f"up_z{i}", [P, S], F32)) for i in range(2)]

        h_loaded = [sem(f"h_loaded{T}") for T in range(NT)]
        conv_loaded = sem("conv_loaded")
        w_loaded, first_loaded, gated_stored = mem["w_loaded"], mem["first_loaded"], mem["gated_stored"]
        w_high, w_split = sem("w_high"), sem("w_split")
        z_done = [sem("z_done0"), sem("z_done1")]
        tap2_done, tap1_done, conv_done = sem("tap2_done"), sem("tap1_done"), sem("conv_done")
        silu_done, gated_done = sem("silu_done"), sem("gated_done")

        LAST = NF - 1

        def tile_cols(T, back=0):
            return slice(max(back, T * TW), (T + 1) * TW)

        block = ctx.enter_context(nc.Block())

        @block.sync
        def _(sp):
            def load_w(c):
                for half in range(2):
                    sp.dma_start(w_raw[:, half], io["w_up"][bass.ds(c, 1), half].rearrange("n c k m -> c (n k) m")).then_inc(w_loaded[half], 16)

            for q in range(2):
                sp.wait_ge(mem["x2_stored"][q], 16 * NB // 2)
                sp.wait_ge(mem["h_stored"][q], 32 * NB // 2)
            sp.dma_start(conv[:], io["conv"]).then_inc(conv_loaded, 16)
            for T in range(1, NT):
                for a, h in enumerate((h_hi, h_lo)):
                    own, src = slice((T - 1) * TW, T * TW), slice(T * TW, (T + 1) * TW)
                    sp.dma_start(h[:, :, own].bitcast(F32), io["h2_hbm"][a, :, :, src].rearrange("k c t -> c k t")).then_inc(h_loaded[T], 16)
            with sp.Fori(0, LAST) as c:
                sp.wait_ge(w_split, c * 2 + 2)
                load_w(c + 1)
                sp.wait_ge(gated_done, c + 1)
                sp.dma_start(io["gated_hbm"][bass.ds(c, 1)].rearrange("n f t -> f (n t)"), gated[:]).then_inc(gated_stored, 16)
            sp.wait_ge(w_split, NF * 2)
            sp.wait_ge(gated_stored, 16 * 2)
            for f in range(2):
                sp.dma_start(mem["g_raw"][:, f], io["gated_hbm"][f, :, 0:TW]).then_inc(mem["g_loaded"][f], 16)
                sp.dma_start(mem["w_raw"][:, f], io["w_down"][f]).then_inc(mem["down_loaded"][f], 16)
            sp.wait_ge(gated_stored, 16 * LAST)
            for T in range(NT):
                sp.wait_ge(gated_done, LAST + T + 1)
                sp.dma_start(io["gated_hbm"][LAST, :, tile_cols(T)], gated[:, tile_cols(T)]).then_inc(gated_stored, 16)

        @block.gpsimd
        def _(pool):
            def split(c, half):
                pool.wait_ge(w_high, c * 2 + half + 1)
                pool.tensor_tensor(w_lo[:, half], w_raw[:, half], w_hi[:, half].bitcast(F32), ALU.subtract).then_inc(w_split, 1)

            def gate(c):
                pool.wait_ge(silu_done, c + 1)
                pool.wait_ge(conv_done, c * 2 + 2)
                if not isinstance(c, int) or c > 0:
                    pool.wait_ge(gated_stored, c * 16)
                pool.tensor_tensor(gated[:], z_c[:, 0], z_c[:, 1], ALU.mult).then_inc(gated_done, 1)

            split(0, 0)
            split(0, 1)
            def chunk(c):
                split(c + 1, 0)
                split(c + 1, 1)
                gate(c)

            chunk(0)
            with pool.Fori(1, LAST) as c:
                chunk(c)
            pool.wait_ge(gated_stored, LAST * 16)
            for T in range(NT):
                pool.wait_ge(silu_done, LAST + T + 1)
                pool.wait_ge(conv_done, LAST * 2 + NT + T + 1)
                pool.tensor_tensor(gated[:, tile_cols(T)], z_c[:, 0, tile_cols(T)], z_c[:, 1, tile_cols(T)], ALU.mult).then_inc(gated_done, 1)

        @block.scalar
        def _(act):
            def high(c, half):
                act.wait_ge(w_loaded[half], c * 16 + 16)
                act.activation(w_hi[:, half], w_raw[:, half], ACT.Copy).then_inc(w_high, 1)

            def per_channel(c, half, n):
                return conv[:, bass.ds(c, 1), half, n:n + 1].rearrange("p a b -> p (a b)")

            def last_tap(c, half):
                act.wait_ge(z_done[half], c * NT + NT)
                if not isinstance(c, int) or c > 0:
                    act.wait_ge(gated_done, c)
                act.activation(z_c[:, half], z[half][:], ACT.Identity, bias=per_channel(c, half, 3),
                               scale=per_channel(c, half, 2)).then_inc(tap2_done, 1)

            def silu(c):
                act.wait_ge(conv_done, c * 2 + 1)
                act.activation(z_c[:, 0], z_c[:, 0], ACT.Silu).then_inc(silu_done, 1)

            high(0, 0)
            high(0, 1)
            act.wait_ge(conv_loaded, 16)

            def chunk(c):
                last_tap(c, 0)
                high(c + 1, 0)
                silu(c)
                last_tap(c, 1)
                high(c + 1, 1)

            chunk(0)
            with act.Fori(1, LAST) as c:
                chunk(c)
            act.wait_ge(gated_done, LAST)
            for half in range(2):
                for T in range(NT):
                    act.wait_ge(z_done[half], LAST * NT + T + 1)
                    act.activation(z_c[:, half, tile_cols(T)], z[half][:, tile_cols(T)], ACT.Identity, bias=per_channel(LAST, half, 3),
                                   scale=per_channel(LAST, half, 2)).then_inc(tap2_done, 1)
                    if half == 0:
                        act.wait_ge(conv_done, LAST * 2 + T + 1)
                        act.activation(z_c[:, 0, tile_cols(T)], z_c[:, 0, tile_cols(T)], ACT.Silu).then_inc(silu_done, 1)

        @block.vector
        def _(dve):
            def taps(c, half, n, cols):
                for tap, done, ready in ((1, tap1_done, tap2_done), (0, conv_done, tap1_done)):
                    back = 2 - tap
                    out = cols(back)
                    dve.wait_ge(ready, n + 1)
                    dve.scalar_tensor_tensor(out=z_c[:, half, out], in0=z[half][:, out.start - back:out.stop - back],
                                             scalar=conv[:, bass.ds(c, 1), half, tap:tap + 1].rearrange("p a b -> p (a b)"),
                                             in1=z_c[:, half, out], op0=ALU.mult, op1=ALU.add).then_inc(done, 1)

            dve.wait_ge(conv_loaded, 16)
            with dve.Fori(0, LAST) as c:
                for half in range(2):
                    taps(c, half, c * 2 + half, lambda back: slice(back, S))
            for half in range(2):
                for T in range(NT):
                    taps(LAST, half, LAST * 2 + half * NT + T, lambda back: tile_cols(T, back))

        @block.tensor
        def _(pe):
            def product(half, T):
                cols = slice(T * TW, (T + 1) * TW)
                if T == 0:
                    moving = [(first_tile[:, 0, k], first_tile[:, 1, k]) for k in range(KD)]
                else:
                    own = slice((T - 1) * TW, T * TW)
                    moving = [(h_hi[:, k, own], h_lo[:, k, own]) for k in range(KD)]
                split_products(pe, z[half][:, cols], [(w_hi[:, half, k], w_lo[:, half, k], *moving[k])
                                                      for k in range(KD)]).then_inc(z_done[half], 1)

            for part in first_loaded:
                pe.wait_ge(part, 32)
            for T in range(NT):
                for half in range(2):
                    if T == 0:
                        pe.wait_ge(w_split, half + 1)
                    elif half == 0:
                        pe.wait_ge(h_loaded[T], 32)
                    product(half, T)
            with pe.Fori(1, NF) as c:
                for half in range(2):
                    pe.wait_ge(w_split, c * 2 + half + 1)
                    pe.wait_ge(conv_done, c * 2 + half - 1)
                    for T in range(NT):
                        product(half, T)


def ffn_down(nc, io, mem):
    with ExitStack() as ctx:
        def sb(name, shape, dt=F32):
            return ctx.enter_context(nc.sbuf_tensor("dn_" + name, shape, dt))

        def sem(name):
            return ctx.enter_context(nc.semaphore("dn_" + name))

        w_first, w_rest = mem["w_raw"], sb("w_rest", [P, NF - 2, D])
        w_hi, w_lo = sb("w_hi", [P, 2, D], F32R), sb("w_lo", [P, 2, D], F32R)
        g_raw = mem["g_raw"]
        g_hi, g_lo = sb("g_hi", [P, 2, TW], F32R), sb("g_lo", [P, 2, TW], F32R)
        x_t = sb("x_t", [P, BPT, D])
        squares = sb("squares", [P, BPT, D])
        stat = sb("stat", [P, 3, BPT])
        minus_half = sb("minus_half", [P, BPT])
        final_g = sb("final_g", [P, D])
        acc = [ctx.enter_context(nc.psum_tensor(f"dn_acc{j}", [P, D], F32)) for j in range(BPT)]

        w_loaded, g_loaded, gated_stored = mem["down_loaded"], mem["g_loaded"], mem["gated_stored"]
        x_loaded, out_stored, last_stored = sem("x_loaded"), sem("out_stored"), sem("last_stored")
        gain_loaded, half_set = sem("gain_loaded"), sem("half_set")
        high_done, split_done, used = sem("high_done"), sem("split_done"), sem("used")
        acc_done, x3_done, sq_done, mean_done, std_done, out_done = (sem(n) for n in ("acc_done", "x3_done", "sq_done", "mean_done", "std_done", "out_done"))

        block = ctx.enter_context(nc.Block())

        HEAD = 4

        def w_chunk(f):
            if isinstance(f, int) and f < 2:
                return w_first[:, f]
            return w_rest[:, bass.ds(f - 2, 1)].rearrange("f n d -> f (n d)")

        def steps(engine, step, between=None):
            def tile(T):
                for f in range(HEAD):
                    step(T, f, f % 2)
                    if between:
                        between(T, f)
                with engine.Fori(HEAD // 2, NF // 2) as j:
                    step(T, j * 2, 0)
                    step(T, j * 2 + 1, 1)

            tile(0)
            with engine.Fori(1, NT) as T:
                tile(T)

        @block.sync
        def _(sp):
            def load_w(f, q):
                sp.dma_start(w_chunk(f), io["w_down"][bass.ds(f, 1)].rearrange("n f d -> f (n d)")).then_inc(w_loaded[q], 16)

            def load_g(T, f, q):
                sp.dma_start(g_raw[:, q], io["gated_hbm"][bass.ds(f, 1), :, bass.ds(T * TW, TW)].rearrange("n f t -> f (n t)")).then_inc(g_loaded[q], 16)

            sp.dma_start(final_g[:], io["final_g"].to_broadcast([P, D])).then_inc(gain_loaded, 16)
            for q in range(2):
                sp.wait_ge(w_loaded[q], 16)
                load_w(2 + q, q)
            with sp.Fori(1, NF // 2 - 1) as j:
                for q in range(2):
                    sp.wait_ge(split_done, j * 4 + (2 * q - 2))
                    load_g(0, j * 2 + q, q)
                    sp.wait_ge(w_loaded[q], j * 16 + 16)
                    load_w(j * 2 + (q + 2), q)
            for q in range(2):
                sp.wait_ge(split_done, NF * 2 + 2 * q - 6)
                if q == 1:
                    sp.wait_ge(gated_stored, 16 * (NF - 1 + NT))
                load_g(0, NF - 2 + q, q)
            with sp.Fori(1, NT) as T:
                with sp.Fori(0, NF // 2) as j:
                    for q in range(2):
                        sp.wait_ge(split_done, T * (2 * NF) + j * 4 + (2 * q - 2))
                        load_g(T, j * 2 + q, q)
            for j in range(BPT):
                sp.wait_ge(out_done, NT * BPT - BPT + j + 1)
                sp.dma_start(io["out"][S - TW + j * P:S - TW + (j + 1) * P, :], x_t[:, j]).then_inc(last_stored, 16)
            sp.wait_ge(last_stored, 16 * BPT)

        @block.gpsimd
        def _(pool):
            def x_rows(name, T):
                return io[name][bass.ds(T * TW, TW), :].rearrange("(j t) d -> t j d", t=P)

            pool.memset(minus_half[:], -0.5).then_inc(half_set, 1)
            pool.wait_ge(half_set, 1)
            pool.dma_start(x_t[:], x_rows("x2_hbm", 0)).then_inc(x_loaded, 16)

            def inverse_roots(T):
                for j in range(BPT):
                    pool.wait_ge(mean_done, T * BPT + j + 1)
                    pool.tensor_tensor(stat[:, 2, j:j + 1], stat[:, 1, j:j + 1], minus_half[:, j:j + 1], ALU.pow).then_inc(std_done, 1)

            with pool.Fori(0, NT - 1) as T:
                inverse_roots(T)
                pool.wait_ge(out_done, T * BPT + BPT)
                pool.dma_start(x_rows("out", T), x_t[:]).then_inc(out_stored, 16)
                pool.wait_ge(out_stored, T * 16 + 16)
                pool.dma_start(x_t[:], x_rows("x2_hbm", T + 1)).then_inc(x_loaded, 16)
            inverse_roots(NT - 1)

        @block.scalar
        def _(act):
            def step(T, f, q):
                if isinstance(T, int):
                    act.wait_ge(w_loaded[q], f * 8 + (16 - 8 * q))
                act.wait_ge(g_loaded[q], T * (NF // 2 * 16) + f * 8 + (16 - 8 * q))
                if not isinstance(f, int):
                    act.wait_ge(used, T * (NF - 1) + f - 1)
                elif f >= 2:
                    act.wait_ge(used, T * (NF - 1) + (f - 1))
                elif not isinstance(T, int):
                    if f == 1:
                        act.wait_ge(acc_done, T * BPT)
                    else:
                        act.wait_ge(used, T * (NF - 1))
                act.activation(g_hi[:, q], g_raw[:, q], ACT.Copy).then_inc(high_done, 1)
                act.activation(w_hi[:, q], w_chunk(f), ACT.Copy).then_inc(high_done, 1)

            def squared(T):
                for j in range(BPT):
                    act.wait_ge(x3_done, T * BPT + j + 1)
                    act.activation(squares[:, j], x_t[:, j], ACT.Square, accum_out=stat[:, 0, j:j + 1]).then_inc(sq_done, 1)

            def between(T, f):
                if not isinstance(T, int) and f == 1:
                    squared(T - 1)

            steps(act, step, between)
            squared(NT - 1)

        @block.vector
        def _(dve):
            def step(T, f, q):
                n = T * (2 * NF) + f * 2
                dve.wait_ge(high_done, n + 1)
                dve.tensor_tensor(g_lo[:, q], g_raw[:, q], g_hi[:, q].bitcast(F32), ALU.subtract).then_inc(split_done, 1)
                dve.wait_ge(high_done, n + 2)
                dve.tensor_tensor(w_lo[:, q], w_chunk(f), w_hi[:, q].bitcast(F32),
                                  ALU.subtract).then_inc(split_done, 1)

            def add_residual(T, j):
                dve.wait_ge(acc_done, T * BPT + j + 1)
                dve.tensor_tensor(x_t[:, j], acc[j][:], x_t[:, j], ALU.add).then_inc(x3_done, 1)

            def mean(T, j):
                dve.wait_ge(sq_done, T * BPT + j + 1)
                dve.tensor_scalar(stat[:, 1, j:j + 1], stat[:, 0, j:j + 1], 1.0 / D, EPS, ALU.mult, ALU.add).then_inc(mean_done, 1)

            def normalise(T, j):
                dve.wait_ge(std_done, T * BPT + j + 1)
                dve.scalar_tensor_tensor(out=x_t[:, j], in0=x_t[:, j], scalar=stat[:, 2, j:j + 1], in1=final_g[:],
                                         op0=ALU.mult, op1=ALU.mult).then_inc(out_done, 1)

            def between(T, f):
                if not isinstance(T, int):
                    if f == 0:
                        dve.wait_ge(x_loaded, T * 16)
                        for j in range(BPT):
                            add_residual(T - 1, j)
                    if f == 2:
                        dve.wait_ge(gain_loaded, 16)
                        for j in range(BPT):
                            mean(T - 1, j)
                        for j in range(BPT):
                            normalise(T - 1, j)

            steps(dve, step, between)
            dve.wait_ge(x_loaded, NT * 16)
            for j in range(BPT + 2):
                if j < BPT:
                    add_residual(NT - 1, j)
                if 1 <= j <= BPT:
                    mean(NT - 1, j - 1)
                if j >= 2:
                    normalise(NT - 1, j - 2)

        @block.tensor
        def _(pe):
            def step(T, n, q, start, stop):
                pe.wait_ge(split_done, n * 2 + 2)
                for j in range(BPT):
                    if start and not isinstance(T, int):
                        pe.wait_ge(x3_done, T * BPT - BPT + j + 1)
                    t = slice(j * P, (j + 1) * P)
                    for half in range(2):
                        cols = slice(half * TW, (half + 1) * TW)
                        mm = split_products(pe, acc[j][:, cols], [(g_hi[:, q, t], g_lo[:, q, t], w_hi[:, q, cols], w_lo[:, q, cols])],
                                            first=start, last=stop)
                    if stop:
                        mm.then_inc(acc_done, 1)
                if not stop:
                    mm.then_inc(used, 1)

            def tile(T):
                step(T, T * NF, 0, True, False)
                step(T, T * NF + 1, 1, False, False)
                with pe.Fori(1, NF // 2 - 1) as i:
                    step(T, T * NF + i * 2, 0, False, False)
                    step(T, T * NF + i * 2 + 1, 1, False, False)
                step(T, T * NF + NF - 2, 0, False, False)
                step(T, T * NF + NF - 1, 1, False, True)

            tile(0)
            with pe.Fori(1, NT) as T:
                tile(T)


def build(nc, io, upto=5):
    def hbm(name, shape):
        io[name] = nc.dram_tensor(name, shape, F32, kind="Internal").ap()

    hbm("q_hbm", (2, NHB * HD, S))
    hbm("k_hbm", (2, NHB * HD, S))
    hbm("v_hbm", (NHB, NT, P, BPT, 2 * HD))
    hbm("ap_hbm", (6, P, S))
    hbm("o_hbm", (NHB, P, S))
    hbm("x2_hbm", (S, D))
    hbm("h2_hbm", (2, KD, P, S))
    hbm("gated_hbm", (NF, P, S))
    with ExitStack() as ctx:
        mem = {"ident": ctx.enter_context(nc.sbuf_tensor("ident", [P, P], F32))}
        with ExitStack() as front:
            for n in ("hT_hi", "hT_lo"):
                mem[n] = front.enter_context(nc.sbuf_tensor(n, [P, KD, S], F32R))
            with nc.sbuf_tensor("x_in", [P, 2, D], F32) as mem["x_in"], nc.sbuf_tensor("xn", [P, 2, D], F32) as mem["xn"]:
                pass
            for n, shape, dt in (("q_t", [P, 2, 2, TW], F32R), ("k_t", [P, 2, TW], F32R), ("v_t", [P, 2, BPT, 2 * HD], F32R),
                                 ("w_raw", [P, KD, P], F32)):
                mem[n] = front.enter_context(nc.sbuf_tensor("at_" + n, shape, dt))
            for n in "qkv":
                mem[n + "_loaded"] = [front.enter_context(nc.semaphore(f"at_{n}_loaded{i}")) for i in range(2)]
            mem["w_loaded"] = front.enter_context(nc.semaphore("at_w_loaded"))
            project_norm(nc, io, mem)
            if upto >= 2:
                attend(nc, io, mem)
        def sem(name):
            return ctx.enter_context(nc.semaphore(name))

        with nc.sbuf_tensor("wo_raw", [P, KD, D], F32) as mem["wo_raw"]:
            pass
        for n, shape, dt in (("first_tile", [P, 2, KD, TW], F32R), ("w_raw", [P, 2, D], F32), ("g_raw", [P, 2, TW], F32), ("gated", [P, S], F32)):
            mem[n] = ctx.enter_context(nc.sbuf_tensor(n, shape, dt))
        mem["w_loaded"] = [sem("w_up_loaded0"), sem("w_up_loaded1")]
        mem["first_loaded"] = [sem(f"first_loaded{n}") for n in range(FIRST_PIECES)]
        mem["x2_stored"], mem["h_stored"] = ([sem(n + "0"), sem(n + "1")] for n in ("x2_stored", "h_stored"))
        mem["gated_stored"] = sem("gated_stored")
        mem["down_loaded"], mem["g_loaded"] = ([sem(n + "0"), sem(n + "1")] for n in ("down_loaded", "g_loaded"))
        if upto >= 3:
            mix(nc, io, mem)
        if upto >= 4:
            ffn_up(nc, io, mem)
        if upto >= 5:
            ffn_down(nc, io, mem)


def laid_out(inputs):
    import numpy as np

    a = {n: np.asarray(v) for n, v in inputs.items()}
    w_in = a["w_in"][0]
    wa, wq, wk, wv, wp = np.split(w_in, [512, 1024, 1536, 2048], axis=1)
    w_cm = np.concatenate([wa, wq, wk, wp], axis=1).reshape(KD, P, 14, P)
    conv = np.concatenate([a["conv_w"][0], a["conv_b"]], axis=0)
    width = np.repeat(np.array(POOL_WINDOWS, np.float32), HD).reshape(2, P).T[:, :, None]
    inv_first = (1.0 / np.minimum(np.arange(1, P + 1, dtype=np.float32), width)).astype(np.float32)
    inv_rest = np.broadcast_to(1.0 / width, (P, 2, P)).astype(np.float32)
    return {
        "x": a["x"][0],
        "norm1_g": a["norm1_g"],
        "w_chunks": w_cm.transpose(2, 1, 0, 3)[CHUNK_ORDER],
        "w_v": wv.reshape(KD, P, 512),
        "sgu_g": a["sgu_norm_g"],
        "sgu_w": a["sgu_w"][0].transpose(2, 0, 1),
        "sgu_b": a["sgu_b"][0].transpose(1, 0),
        "pool_w": a["pool_w"][0],
        "pool_scale": a["pool_scale"],
        "inv_first": inv_first,
        "inv_rest": inv_rest,
        "mix_g": a["mix_norm_g"],
        "w_o": a["w_o"][0].reshape(KD, P, D),
        "norm2_g": a["norm2_g"],
        "w_up": a["w_up"][0].reshape(KD, P, 2, NF, P).transpose(3, 2, 1, 0, 4),
        "conv": conv.reshape(4, 2, NF, P).transpose(3, 2, 1, 0),
        "w_down": a["w_down"][0].reshape(NF, P, D),
        "final_g": a["final_g"][None, :],
    }


def kernel(**inputs):
    import numpy as np
    import concourse.bacc as bacc
    from concourse.bass_utils import run_bass_kernel_spmd

    nc = bacc.Bacc("TRN2", target_bir_lowering=False, num_devices=1)
    arrays = {n: np.ascontiguousarray(v) for n, v in laid_out(inputs).items()}
    io = {n: nc.dram_tensor(f"in_{n}", v.shape, F32, kind="ExternalInput").ap() for n, v in arrays.items()}
    io["out"] = nc.dram_tensor("out", (S, D), F32, kind="ExternalOutput").ap()
    build(nc, io)
    r = run_bass_kernel_spmd(nc, [{f"in_{n}": v for n, v in arrays.items()}], core_ids=[0])
    return r.results[0]["out"].reshape(1, S, D)
```
